# Optimizing a Trainium2 kernel written in Bass

```python
import math
import jax, jax.numpy as jnp
from jax import lax
import numpy as np

D_MODEL = 1024
BATCH = 1
SEQ = 256
DEPTH = 1

HEAD_DIM = 64
BRANCH_W = D_MODEL // 4
N_BRANCH = 4
N_HEADS = BRANCH_W // HEAD_DIM
SC_K = 3
SB_BLOCK = 128
SSM_GROUPS = 2
SSM_STATE = 64
SSM_CONV_K = 4
SSM_CHUNK = 256
SSM_CONV_DIM = BRANCH_W + 2 * SSM_GROUPS * SSM_STATE
MOBA_BLOCK = 256
MOBA_TOPK = 3
MOBA_QCHUNK = 128
SEQ_MULTIPLE = 256
FFN_HIDDEN = ((8 * D_MODEL + 3 * 256 - 1) // (3 * 256)) * 256
RMS_EPS = 1e-6

W_A_IN = 3 * BRANCH_W
W_B_IN = 3 * BRANCH_W
W_C_IN = BRANCH_W + SSM_CONV_DIM + N_HEADS
W_D_IN = 3 * BRANCH_W
W_G_IN = N_BRANCH * D_MODEL
IN_SPLITS = [W_A_IN, W_A_IN + W_B_IN, W_A_IN + W_B_IN + W_C_IN,
             W_A_IN + W_B_IN + W_C_IN + W_D_IN]
N_IN = W_A_IN + W_B_IN + W_C_IN + W_D_IN + W_G_IN


def rmsnorm(x, g):
    xf = x.astype(jnp.float32)
    y = xf * lax.rsqrt(jnp.mean(xf * xf, axis=-1, keepdims=True) + RMS_EPS)
    return (y * g.astype(jnp.float32)).astype(x.dtype)

def causal_depthwise_conv(x, w):
    k = w.shape[0]
    return lax.conv_general_dilated(
        x, w[:, None, :].astype(x.dtype), window_strides=(1,), padding=[(k - 1, 0)],
        dimension_numbers=("NWC", "WIO", "NWC"), feature_group_count=x.shape[-1])

def short_conv_mixer(u, conv_w):
    xa, b_gate, c_gate = jnp.split(u, 3, axis=-1)
    return b_gate * causal_depthwise_conv(c_gate * xa, conv_w)

def stick_breaking_attention(q, k, v):
    bsz, seq, nh, dh = q.shape
    nqb = seq // SB_BLOCK
    f32 = jnp.float32
    qs = q * (dh ** -0.5)
    within_mat = jnp.tril(jnp.ones((SB_BLOCK, SB_BLOCK), f32), -1)
    outs = []
    for c in range(nqb):
        nkb = c + 1
        kc = nkb * SB_BLOCK
        qi = qs[:, c * SB_BLOCK:(c + 1) * SB_BLOCK]
        z = jnp.einsum("bqhd,bkhd->bhqk", qi, k[:, :kc], preferred_element_type=f32)
        q_pos = c * SB_BLOCK + jnp.arange(SB_BLOCK)
        past = jnp.arange(kc)[None, :] < q_pos[:, None]
        z = jnp.where(past, z, -jnp.inf)
        sp = jax.nn.softplus(z)
        lk = sp.reshape(bsz, nh, SB_BLOCK, nkb, SB_BLOCK)
        within = jnp.einsum("bhqnj,js->bhqns", lk, within_mat)
        after_mat = jnp.tril(jnp.ones((nkb, nkb), f32), -1)
        after = jnp.einsum("bhqm,mn->bhqn", jnp.sum(lk, axis=-1), after_mat)
        between = (within + after[..., None]).reshape(bsz, nh, SB_BLOCK, kc)
        w = jnp.exp(z - sp - between)
        outs.append(jnp.einsum("bhqk,bkhd->bqhd", w.astype(v.dtype), v[:, :kc]))
    return jnp.concatenate(outs, axis=1).reshape(bsz, seq, nh * dh)

def ssd_chunked(x, a, b_in, c_in):
    bsz, seq, nh, hp = x.shape
    ng, ns = b_in.shape[2], b_in.shape[3]
    ne = nh // ng
    t = SSM_CHUNK
    nc = seq // t
    f32 = jnp.float32
    x = x.astype(f32).reshape(bsz, nc, t, ng, ne, hp)
    a = a.astype(f32).reshape(bsz, nc, t, ng, ne)
    bc = b_in.astype(f32).reshape(bsz, nc, t, ng, ns)
    cc = c_in.astype(f32).reshape(bsz, nc, t, ng, ns)
    a_cs = jnp.cumsum(a, axis=2)
    causal = jnp.tril(jnp.ones((t, t), dtype=bool))[:, :, None, None]
    seg = a_cs[:, :, :, None] - a_cs[:, :, None, :]
    decay = jnp.exp(jnp.where(causal, seg, -jnp.inf))
    cb = jnp.einsum("bclgn,bcsgn->bclsg", cc, bc)
    y_diag = jnp.einsum("bclsge,bcsgep->bclgep", cb[..., None] * decay, x)
    decay_to_end = jnp.exp(a_cs[:, :, -1:] - a_cs)
    chunk_states = jnp.einsum("bclgn,bclge,bclgep->bcgepn", bc, decay_to_end, x)
    chunk_decay = jnp.exp(a_cs[:, :, -1])

    def step(h, inp):
        s_c, d_c = inp
        return h * d_c[..., None, None] + s_c, h

    h0 = jnp.zeros((bsz, ng, ne, hp, ns), f32)
    _, h_enter = lax.scan(step, h0, (jnp.moveaxis(chunk_states, 1, 0),
                                     jnp.moveaxis(chunk_decay, 1, 0)))
    h_enter = jnp.moveaxis(h_enter, 0, 1)
    y_off = jnp.einsum("bclgn,bcgepn,bclge->bclgep", cc, h_enter, jnp.exp(a_cs))
    return (y_diag + y_off).reshape(bsz, seq, nh, hp)

def mamba2_mixer(u, conv_w, conv_b, dt_bias, a_log, d_skip, norm_g):
    bsz, seq, _ = u.shape
    z, xbc, dt = jnp.split(u, [BRANCH_W, BRANCH_W + SSM_CONV_DIM], axis=-1)
    xbc = jax.nn.silu(causal_depthwise_conv(xbc, conv_w) + conv_b)
    xs, b_in, c_in = jnp.split(xbc, [BRANCH_W, BRANCH_W + SSM_GROUPS * SSM_STATE], axis=-1)
    dt = jax.nn.softplus(dt.astype(jnp.float32) + dt_bias.astype(jnp.float32))
    a = -jnp.exp(a_log.astype(jnp.float32))
    xh = xs.reshape(bsz, seq, N_HEADS, HEAD_DIM)
    y = ssd_chunked(xh.astype(jnp.float32) * dt[..., None], dt * a,
                    b_in.reshape(bsz, seq, SSM_GROUPS, SSM_STATE),
                    c_in.reshape(bsz, seq, SSM_GROUPS, SSM_STATE))
    y = y.astype(u.dtype) + xh * d_skip[:, None]
    gsz = BRANCH_W // SSM_GROUPS
    gated = y.reshape(bsz, seq, SSM_GROUPS, gsz) * jax.nn.silu(z.reshape(bsz, seq, SSM_GROUPS, gsz))
    return rmsnorm(gated, norm_g.reshape(SSM_GROUPS, gsz)).reshape(bsz, seq, BRANCH_W)

def moba_head(q, k, v):
    seq, dh = q.shape
    nb = seq // MOBA_BLOCK
    ke = max(1, min(MOBA_TOPK, nb - 1))
    cq = MOBA_QCHUNK
    n_pairs = seq * ke
    n_chunks = -(-(n_pairs + (nb + 1) * (cq - 1)) // cq)
    scale = dh ** -0.5
    f32 = jnp.float32
    kblk = k.reshape(nb, MOBA_BLOCK, dh)
    vblk = v.reshape(nb, MOBA_BLOCK, dh)
    k_mean = jnp.mean(kblk.astype(f32), axis=1)
    gate = q.astype(f32) @ k_mean.T
    own = jnp.arange(seq) // MOBA_BLOCK
    gate = jnp.where(jnp.arange(nb)[None, :] < own[:, None], gate, -jnp.inf)
    _, sel = lax.top_k(gate, ke)
    valid = jnp.arange(ke)[None, :] < own[:, None]
    grp = jnp.where(valid, sel, nb).reshape(n_pairs)
    cnt = jnp.zeros((nb + 1,), jnp.int32).at[grp].add(1)
    padded = (cnt + cq - 1) // cq * cq
    pad_end = jnp.cumsum(padded)
    pad_start = pad_end - padded
    order = jnp.argsort(grp, stable=True)
    g_sorted = grp[order]
    rank = jnp.arange(n_pairs, dtype=jnp.int32) - (jnp.cumsum(cnt) - cnt)[g_sorted]
    dest = jnp.zeros((n_pairs,), jnp.int32).at[order].set(pad_start[g_sorted] + rank)
    slot_pair = jnp.full((n_chunks * cq,), -1, jnp.int32).at[dest].set(
        jnp.arange(n_pairs, dtype=jnp.int32)).reshape(n_chunks, cq)
    chunk_grp = jnp.searchsorted(pad_end, jnp.arange(n_chunks, dtype=jnp.int32) * cq, side="right")
    slot_ok = (slot_pair >= 0) & (chunk_grp < nb)[:, None]
    blk = jnp.minimum(chunk_grp, nb - 1)
    q_c = q[jnp.maximum(slot_pair, 0) // ke]
    k_c = kblk[blk]
    v_c = vblk[blk]
    s = jnp.einsum("cqd,ckd->cqk", q_c, k_c, preferred_element_type=f32) * scale
    s = jnp.where(slot_ok[..., None], s, -jnp.inf)
    m = jnp.where(slot_ok, jnp.max(s, axis=-1), 0.0)
    p = jnp.exp(s - m[..., None])
    l = jnp.sum(p, axis=-1)
    o = jnp.einsum("cqk,ckd->cqd", p.astype(v.dtype), v_c, preferred_element_type=f32)
    m_p = m.reshape(-1)[dest].reshape(seq, ke)
    l_p = l.reshape(-1)[dest].reshape(seq, ke)
    o_p = o.reshape(-1, dh)[dest].reshape(seq, ke, dh)
    s_own = jnp.einsum("nqd,nkd->nqk", q.reshape(nb, MOBA_BLOCK, dh), kblk,
                       preferred_element_type=f32) * scale
    s_own = jnp.where(jnp.tril(jnp.ones((MOBA_BLOCK, MOBA_BLOCK), dtype=bool)), s_own, -jnp.inf)
    m_own = jnp.max(s_own, axis=-1)
    p_own = jnp.exp(s_own - m_own[..., None])
    l_own = jnp.sum(p_own, axis=-1).reshape(seq)
    o_own = jnp.einsum("nqk,nkd->nqd", p_own.astype(v.dtype), vblk,
                       preferred_element_type=f32).reshape(seq, dh)
    m_own = m_own.reshape(seq)
    m_all = jnp.maximum(m_own, jnp.max(jnp.where(valid, m_p, -jnp.inf), axis=-1))
    w_p = jnp.where(valid, jnp.exp(m_p - m_all[:, None]), 0.0)
    w_own = jnp.exp(m_own - m_all)
    num = w_own[:, None] * o_own + jnp.einsum("sr,srd->sd", w_p, o_p)
    den = w_own * l_own + jnp.sum(w_p * l_p, axis=-1)
    return (num / den[:, None]).astype(q.dtype)

def moba_attention(q, k, v):
    bsz, seq, nh, dh = q.shape
    qt, kt, vt = [jnp.moveaxis(t, 2, 1) for t in (q, k, v)]
    out = lax.map(lambda a: jax.vmap(moba_head)(*a), (qt, kt, vt))
    return jnp.moveaxis(out, 1, 2).reshape(bsz, seq, nh * dh)

def hybrid_layer(x, norm1_g, w_in, conv_a_w, ssm_conv_w, ssm_conv_b, ssm_dt_bias,
                 ssm_a_log, ssm_d, ssm_norm_g, w_branch, w_o, norm2_g, w_gate_up, w_down):
    bsz, seq, _ = x.shape
    h = rmsnorm(x, norm1_g)
    u = h @ w_in
    u_a, u_b, u_c, u_d, u_g = jnp.split(u, IN_SPLITS, axis=-1)
    y_a = short_conv_mixer(u_a, conv_a_w)
    q_b, k_b, v_b = [t.reshape(bsz, seq, N_HEADS, HEAD_DIM) for t in jnp.split(u_b, 3, axis=-1)]
    y_b = stick_breaking_attention(q_b, k_b, v_b)
    y_c = mamba2_mixer(u_c, ssm_conv_w, ssm_conv_b, ssm_dt_bias, ssm_a_log, ssm_d, ssm_norm_g)
    q_d, k_d, v_d = [t.reshape(bsz, seq, N_HEADS, HEAD_DIM) for t in jnp.split(u_d, 3, axis=-1)]
    y_d = moba_attention(q_d, k_d, v_d)
    gates = jax.nn.sigmoid(u_g.reshape(bsz, seq, N_BRANCH, D_MODEL))
    branches = [y_a, y_b, y_c, y_d]
    merged = gates[:, :, 0] * (branches[0] @ w_branch[0])
    for i in range(1, N_BRANCH):
        merged = merged + gates[:, :, i] * (branches[i] @ w_branch[i])
    x = x + merged @ w_o
    h2 = rmsnorm(x, norm2_g)
    g_ff, up_ff = jnp.split(h2 @ w_gate_up, 2, axis=-1)
    return x + (jax.nn.silu(g_ff) * up_ff) @ w_down

def first_inputs(seed: int = 0) -> dict:
    key = jax.random.key(seed)
    ks = jax.random.split(key, 17)
    f32 = jnp.float32

    def nrm(k, shape, scale):
        return jax.random.normal(k, shape, f32) * scale

    dt0 = jnp.exp(jax.random.uniform(ks[6], (DEPTH, N_HEADS), f32, math.log(1e-3), math.log(1e-1)))
    return {
        "x": nrm(ks[0], (BATCH, SEQ, D_MODEL), 1.0),
        "norm1_g": 1.0 + nrm(ks[1], (DEPTH, D_MODEL), 0.02),
        "w_in": nrm(ks[2], (DEPTH, D_MODEL, N_IN), D_MODEL ** -0.5),
        "conv_a_w": nrm(ks[3], (DEPTH, SC_K, BRANCH_W), SC_K ** -0.5),
        "ssm_conv_w": nrm(ks[4], (DEPTH, SSM_CONV_K, SSM_CONV_DIM), SSM_CONV_K ** -0.5),
        "ssm_conv_b": nrm(ks[5], (DEPTH, SSM_CONV_DIM), 0.02),
        "ssm_dt_bias": dt0 + jnp.log(-jnp.expm1(-dt0)),
        "ssm_a_log": jnp.log(jax.random.uniform(ks[7], (DEPTH, N_HEADS), f32, 1.0, 16.0)),
        "ssm_d": 1.0 + nrm(ks[8], (DEPTH, N_HEADS), 0.1),
        "ssm_norm_g": 1.0 + nrm(ks[9], (DEPTH, BRANCH_W), 0.02),
        "w_branch": nrm(ks[10], (DEPTH, N_BRANCH, BRANCH_W, D_MODEL), BRANCH_W ** -0.5),
        "w_o": nrm(ks[11], (DEPTH, D_MODEL, D_MODEL), D_MODEL ** -0.5),
        "norm2_g": 1.0 + nrm(ks[12], (DEPTH, D_MODEL), 0.02),
        "w_gate_up": nrm(ks[13], (DEPTH, D_MODEL, 2 * FFN_HIDDEN), D_MODEL ** -0.5),
        "w_down": nrm(ks[14], (DEPTH, FFN_HIDDEN, D_MODEL), FFN_HIDDEN ** -0.5),
        "final_g": 1.0 + nrm(ks[15], (D_MODEL,), 0.02),
    }

def first_block(x, norm1_g, w_in, conv_a_w, ssm_conv_w, ssm_conv_b, ssm_dt_bias, ssm_a_log,
              ssm_d, ssm_norm_g, w_branch, w_o, norm2_g, w_gate_up, w_down, final_g):
    seq = x.shape[1]
    seq_pad = -(-seq // SEQ_MULTIPLE) * SEQ_MULTIPLE
    h = jnp.pad(x, ((0, 0), (0, seq_pad - seq), (0, 0)))
    for l in range(DEPTH):
        h = hybrid_layer(h, norm1_g[l], w_in[l], conv_a_w[l], ssm_conv_w[l], ssm_conv_b[l],
                         ssm_dt_bias[l], ssm_a_log[l], ssm_d[l], ssm_norm_g[l], w_branch[l],
                         w_o[l], norm2_g[l], w_gate_up[l], w_down[l])
    return rmsnorm(h, final_g)[:, :seq]


DEPTH_2 = 2

N_MIXERS = 2
RET_HEADS = 4
RET_QK_DIM = D_MODEL // RET_HEADS
RET_V_DIM = 2 * RET_QK_DIM
RET_QK_WIDTH = RET_HEADS * RET_QK_DIM
RET_V_WIDTH = RET_HEADS * RET_V_DIM
RET_IN_WIDTH = 2 * RET_QK_WIDTH + 2 * RET_V_WIDTH
RET_CHUNK = 128
ROPE_BASE = 10000.0
FNET_GROUPS = 4
FNET_GROUP_DIM = D_MODEL // FNET_GROUPS
D_FF_DENSE = ((8 * D_MODEL // 3 + 255) // 256) * 256
N_EXPERTS = 8
TOP_K = 2
D_FF_EXPERT = 7 * D_MODEL // 2
EPS = 1e-6


def rms_norm(x, g):
    xf = x.astype(jnp.float32)
    y = xf * lax.rsqrt(jnp.mean(xf * xf, axis=-1, keepdims=True) + EPS)
    return (y * g.astype(jnp.float32)).astype(x.dtype)

def rotary(t):
    s, dh = t.shape[1], t.shape[-1]
    half = dh // 2
    inv = ROPE_BASE ** (-jnp.arange(half, dtype=jnp.float32) / half)
    ang = jnp.arange(s, dtype=jnp.float32)[:, None] * inv[None, :]
    cos = jnp.cos(ang)[None, :, None, :]
    sin = jnp.sin(ang)[None, :, None, :]
    t1 = t[..., :half].astype(jnp.float32)
    t2 = t[..., half:].astype(jnp.float32)
    return jnp.concatenate([t1 * cos - t2 * sin, t1 * sin + t2 * cos], axis=-1).astype(t.dtype)

def chunk_retention(q, k, v, log_gamma, inclusive):
    b, h, s, dk = q.shape
    dv = v.shape[-1]
    c = RET_CHUNK
    n = s // c
    dt = q.dtype
    qc = q.reshape(b, h, n, c, dk)
    kc = k.reshape(b, h, n, c, dk)
    vc = v.reshape(b, h, n, c, dv)
    idx = jnp.arange(c, dtype=jnp.float32)
    diff = idx[:, None] - idx[None, :]
    mask = (diff >= 0) if inclusive else (diff > 0)
    lg = log_gamma[:, None, None]
    decay = jnp.where(mask[None], jnp.exp(jnp.where(mask[None], diff[None] * lg, 0.0)), 0.0)
    scores = jnp.einsum('bhnid,bhnjd->bhnij', qc, kc) * decay[None, :, None].astype(dt)
    intra = jnp.einsum('bhnij,bhnje->bhnie', scores, vc)

    xi = jnp.exp((idx[None, :] + 1.0) * log_gamma[:, None]).astype(dt)
    zeta = jnp.exp((c - 1.0 - idx[None, :]) * log_gamma[:, None]).astype(dt)
    g_chunk = jnp.exp(c * log_gamma).astype(dt)

    def step(state, inp):
        q_n, k_n, v_n = inp
        cross = jnp.einsum('bhid,bhde->bhie', q_n * xi[None, :, :, None], state)
        state = state * g_chunk[None, :, None, None] + jnp.einsum(
            'bhjd,bhje->bhde', k_n * zeta[None, :, :, None], v_n)
        return state, cross

    state0 = jnp.zeros((b, h, dk, dv), dt)
    xs = (jnp.moveaxis(qc, 2, 0), jnp.moveaxis(kc, 2, 0), jnp.moveaxis(vc, 2, 0))
    _, cross = lax.scan(step, state0, xs)
    cross = jnp.moveaxis(cross, 0, 2)
    return (intra + cross).reshape(b, h, s, dv)

def retention_mixer(h, w_in, decay_logit, gn_gain, w_out):
    b, s, _ = h.shape
    proj = h @ w_in
    q, k, v, g = jnp.split(proj, [RET_QK_WIDTH, 2 * RET_QK_WIDTH, 2 * RET_QK_WIDTH + RET_V_WIDTH], axis=-1)
    q = rotary(q.reshape(b, s, RET_HEADS, RET_QK_DIM))
    k = rotary(k.reshape(b, s, RET_HEADS, RET_QK_DIM)) * (RET_QK_DIM ** -0.5)
    v = v.reshape(b, s, RET_HEADS, RET_V_DIM)
    q, k, v = (jnp.transpose(t, (0, 2, 1, 3)) for t in (q, k, v))
    log_g = jax.nn.log_sigmoid(decay_logit.astype(jnp.float32))
    fwd = chunk_retention(q, k, v, log_g[0], True)
    bwd = jnp.flip(chunk_retention(jnp.flip(q, 2), jnp.flip(k, 2), jnp.flip(v, 2), log_g[1], False), 2)
    y = (fwd + bwd).astype(jnp.float32)
    mu = jnp.mean(y, axis=-1, keepdims=True)
    var = jnp.mean(jnp.square(y - mu), axis=-1, keepdims=True)
    yn = (y - mu) * lax.rsqrt(var + EPS)
    yn = jnp.transpose(yn, (0, 2, 1, 3)).reshape(b, s, RET_V_WIDTH) * gn_gain.astype(jnp.float32)
    return (jax.nn.silu(g) * yn.astype(h.dtype)) @ w_out

def fourier_mixer(h, w_out):
    b, s, d = h.shape
    hg = h.astype(jnp.float32).reshape(b, s, FNET_GROUPS, FNET_GROUP_DIM)
    y = jnp.fft.fft2(hg, axes=(1, 3), norm='ortho').real
    return y.reshape(b, s, d).astype(h.dtype) @ w_out

def swiglu(t, w_gate, w_up, w_down):
    return (jax.nn.silu(t @ w_gate) * (t @ w_up)) @ w_down

def moe_swiglu(h, w_router, w_gate, w_up, w_down):
    b, s, d = h.shape
    t = h.reshape(-1, d)
    logits = (t @ w_router).astype(jnp.float32)
    top_val, top_idx = lax.top_k(logits, TOP_K)
    top_w = jax.nn.softmax(top_val, axis=-1)
    gates = jnp.sum(jax.nn.one_hot(top_idx, N_EXPERTS, dtype=jnp.float32) * top_w[..., None], axis=1)
    gates = gates.astype(h.dtype)
    out = jnp.zeros_like(t)
    for e in range(N_EXPERTS):
        out = out + gates[:, e:e + 1] * swiglu(t, w_gate[e], w_up[e], w_down[e])
    return out.reshape(b, s, d)

def second_inputs(seed: int = 0) -> dict:
    key = jax.random.key(seed)
    ks = jax.random.split(key, 20)
    n_even = (DEPTH_2 + 1) // 2
    n_odd = DEPTH_2 // 2
    f32 = jnp.float32

    def nrm(k, shape, fan_in):
        return jax.random.normal(k, shape, f32) * (fan_in ** -0.5)

    x = jax.random.normal(ks[0], (BATCH, SEQ, D_MODEL), f32)
    mix_norm = 1.0 + 0.02 * jax.random.normal(ks[1], (DEPTH_2, D_MODEL), f32)
    ffn_norm = 1.0 + 0.02 * jax.random.normal(ks[2], (DEPTH_2, D_MODEL), f32)
    ret_w_in = nrm(ks[3], (n_even, D_MODEL, RET_IN_WIDTH), D_MODEL)
    gam = 1.0 - jnp.exp(jnp.linspace(math.log(1.0 / 32), math.log(1.0 / 512), RET_HEADS)).astype(f32)
    base_logit = jnp.log(gam) - jnp.log1p(-gam)
    ret_decay_logit = base_logit[None, None, :] + 0.05 * jax.random.normal(ks[4], (n_even, 2, RET_HEADS), f32)
    ret_gn_gain = 1.0 + 0.02 * jax.random.normal(ks[5], (n_even, RET_V_WIDTH), f32)
    ret_w_out = nrm(ks[6], (n_even, RET_V_WIDTH, D_MODEL), RET_V_WIDTH)
    dense_w_gate = nrm(ks[7], (n_even, D_MODEL, D_FF_DENSE), D_MODEL)
    dense_w_up = nrm(ks[8], (n_even, D_MODEL, D_FF_DENSE), D_MODEL)
    dense_w_down = nrm(ks[9], (n_even, D_FF_DENSE, D_MODEL), D_FF_DENSE)
    fnet_w_out = nrm(ks[10], (n_odd, D_MODEL, D_MODEL), D_MODEL)
    moe_router = nrm(ks[11], (n_odd, D_MODEL, N_EXPERTS), D_MODEL)
    moe_w_gate = nrm(ks[12], (n_odd, N_EXPERTS, D_MODEL, D_FF_EXPERT), D_MODEL)
    moe_w_up = nrm(ks[13], (n_odd, N_EXPERTS, D_MODEL, D_FF_EXPERT), D_MODEL)
    moe_w_down = nrm(ks[14], (n_odd, N_EXPERTS, D_FF_EXPERT, D_MODEL), D_FF_EXPERT)
    final_norm = 1.0 + 0.02 * jax.random.normal(ks[15], (D_MODEL,), f32)
    return {"x": x, "mix_norm": mix_norm, "ffn_norm": ffn_norm,
            "ret_w_in": ret_w_in, "ret_decay_logit": ret_decay_logit,
            "ret_gn_gain": ret_gn_gain, "ret_w_out": ret_w_out,
            "dense_w_gate": dense_w_gate, "dense_w_up": dense_w_up, "dense_w_down": dense_w_down,
            "fnet_w_out": fnet_w_out, "moe_router": moe_router,
            "moe_w_gate": moe_w_gate, "moe_w_up": moe_w_up, "moe_w_down": moe_w_down,
            "final_norm": final_norm}

def second_block(x, mix_norm, ffn_norm, ret_w_in, ret_decay_logit, ret_gn_gain, ret_w_out,
              dense_w_gate, dense_w_up, dense_w_down, fnet_w_out, moe_router,
              moe_w_gate, moe_w_up, moe_w_down, final_norm):
    h = x
    for i in range(DEPTH_2):
        j = i // 2
        hn = rms_norm(h, mix_norm[i])
        if i % N_MIXERS == 0:
            h = h + retention_mixer(hn, ret_w_in[j], ret_decay_logit[j], ret_gn_gain[j], ret_w_out[j])
        else:
            h = h + fourier_mixer(hn, fnet_w_out[j])
        hn = rms_norm(h, ffn_norm[i])
        if i % 2 == 0:
            h = h + swiglu(hn, dense_w_gate[j], dense_w_up[j], dense_w_down[j])
        else:
            h = h + moe_swiglu(hn, moe_router[j], moe_w_gate[j], moe_w_up[j], moe_w_down[j])
    return rms_norm(h, final_norm)


def setup_inputs(seed=0):
    out = dict(first_inputs(seed))
    for name, value in second_inputs(seed + 1).items():
        if name != "x":
            out[name + "_2"] = value
    return out


def reference(
    x, norm1_g, w_in, conv_a_w, ssm_conv_w, ssm_conv_b, ssm_dt_bias, ssm_a_log, ssm_d,
    ssm_norm_g, w_branch, w_o, norm2_g, w_gate_up, w_down, final_g, mix_norm_2, ffn_norm_2,
    ret_w_in_2, ret_decay_logit_2, ret_gn_gain_2, ret_w_out_2, dense_w_gate_2, dense_w_up_2,
    dense_w_down_2, fnet_w_out_2, moe_router_2, moe_w_gate_2, moe_w_up_2, moe_w_down_2,
    final_norm_2,
):
    x = first_block(
        x, norm1_g, w_in, conv_a_w, ssm_conv_w, ssm_conv_b, ssm_dt_bias, ssm_a_log, ssm_d,
        ssm_norm_g, w_branch, w_o, norm2_g, w_gate_up, w_down, final_g,
    )
    return second_block(
        x, mix_norm_2, ffn_norm_2, ret_w_in_2, ret_decay_logit_2, ret_gn_gain_2, ret_w_out_2,
        dense_w_gate_2, dense_w_up_2, dense_w_down_2, fnet_w_out_2, moe_router_2, moe_w_gate_2,
        moe_w_up_2, moe_w_down_2, final_norm_2,
    )


_drawn_inputs = setup_inputs


def setup_inputs(seed=0):
    import zlib

    import numpy as np

    out = dict(_drawn_inputs(seed))
    spreads = {}
    factors = {}
    for name, (base, spread) in spreads.items():
        noise = np.random.default_rng([zlib.crc32(name.encode()), seed]).standard_normal(out[name].shape)
        drawn = base * np.exp(spread * noise) if base else spread * noise
        out[name] = __import__('jax').numpy.asarray(drawn.astype(out[name].dtype))
    for name, factor in factors.items():
        out[name] = (out[name] * factor).astype(out[name].dtype)
    return out
```

```python
from contextlib import ExitStack

import numpy as np

import concourse.bass as bass
from concourse import mybir

F32 = mybir.dt.float32
F32R = mybir.dt.float32r
BF16 = mybir.dt.bfloat16
I32 = mybir.dt.int32
ACT = mybir.ActivationFunctionType
ALU = mybir.AluOpType
AX = mybir.AxisListType

P = 128
S = 256
TT = S // P
D = 1024
KD = D // P
NH = 4
HD = 64
BW = 256
FF = 2816
NE = 8
FE = 3584
EPS = 1e-6
NEG = -1e30

COL_A, COL_B, COL_Z, COL_XBC, COL_DT = 0, 768, 1536, 1792, 2304
COL_D, COL_G = 2308, 3076

SLAB = 2048
NRAW = 6
NSPLIT = 3
LEAD = 2
START = 8

PARAMS = {}
_at = 0
for _name, _n in [("norm1", KD), ("norm2", KD), ("mix0", KD), ("mix1", KD), ("ffn0", KD), ("ffn1", KD),
                  ("final1", KD), ("final2", KD), ("ssm_taps", 16), ("a_taps", 6), ("ssm_bias", 4),
                  ("dt_bias", 8), ("a_log", 8), ("skip", 2), ("ssm_norm", 2), ("gn_gain", 16),
                  ("decay", 8), ("w_dt", KD * NH), ("router", KD * NE)]:
    PARAMS[_name] = (_at, _n)
    _at += _n
NPARAM = _at

CONSTS = {}
_at = 0
for _name, _n in [("ident", P), ("suffix", P), ("prefix", P), ("ones", P), ("before", P),
                  ("slot", 2 * P), ("order", NE)]:
    CONSTS[_name] = (_at, _n)
    _at += _n
NCONST = _at
NSTAGE = 1536


def host_constants():
    f = np.float32
    p = np.arange(P)[:, None]
    q = np.arange(P)[None, :]
    s = np.arange(S)[None, :]
    lasting = [np.eye(P), p >= q, p <= q, np.ones((P, P)), p < q,
               np.broadcast_to(s, (P, S)), np.broadcast_to(NE - np.arange(NE)[None, :], (P, NE))]
    lasting = np.concatenate([a.astype(f) for a in lasting], 1)
    strict = np.concatenate([np.where(p < s, 0, NEG), np.where(p < q, 0, NEG)], 1)
    causal = np.concatenate([np.where(q <= p, 0, NEG), np.where(s <= p + P, 0, NEG)], 1)
    ssm = np.concatenate([np.where(s >= p, 0, NEG), np.where(q >= p, 0, NEG)], 1)
    one = np.concatenate([strict, causal, ssm, np.zeros((P, NSTAGE - 1152))], 1).astype(f)
    inv = np.power(f(10000.0), -np.arange(P, dtype=f) / f(P)).astype(f)
    ang = (np.arange(S, dtype=f)[None, :] * inv[:, None]).astype(f).astype(np.float64)
    dist = np.concatenate([s - p, s - p - P], 1)
    two = np.concatenate([np.cos(ang), np.sin(ang), np.maximum(dist, 0), np.maximum(-dist, 0)], 1).astype(f)
    w = 2 * np.pi * ((np.arange(S)[:, None] * np.arange(S)[None, :]) % S) / S
    cs = np.concatenate([np.cos(w), np.sin(w)], 1).reshape(2, P, 2 * S).transpose(1, 0, 2).reshape(P, -1) / 16
    ns = (-np.sin(w)).reshape(2, P, S).transpose(1, 0, 2).reshape(P, -1) / 16
    three = np.concatenate([cs, ns], 1).astype(f)
    return lasting, np.stack([one, two, three])


class Loop:

    def __init__(self, trips):
        self.trips, self.turn = trips, None


class Count:

    def __init__(self, sem, const, steps=()):
        self.sem, self.const, self.steps = sem, const, tuple(steps)

    def value(self):
        out = self.const
        for loop, step in self.steps:
            out = out + (loop.turn if loop.turn is not None else loop.trips - 1) * step
        return out


class Done:

    def __init__(self, nc, ctx, name, engine, step=1):
        self.sem, self.step, self.n, self.steps = ctx.enter_context(nc.semaphore(name)), step, START, []
        engine.sem_inc(self.sem, START)

    def __call__(self, instruction):
        instruction.then_inc(self.sem, self.step)
        self.n += self.step
        return Count(self.sem, self.n, self.steps)

    def ahead(self, k):
        return Count(self.sem, self.n + k * self.step, self.steps)


def wait(engine, *counts):
    last = {}
    for c in counts:
        known = last.get(id(c.sem))
        if known is None:
            last[id(c.sem)] = c
        elif known.steps == c.steps:
            last[id(c.sem)] = c if c.const > known.const else known
        else:
            engine.wait_ge(c.sem, c.value())
    for c in last.values():
        engine.wait_ge(c.sem, c.value())


def stationary_pair(pe, out, w_hi, w_lo, x_hi, x_lo, start, stop, **kw):
    pe.matmul(out, w_hi, x_hi, start=start, stop=False, **kw)
    pe.matmul(out, w_hi, x_lo, start=False, stop=False, **kw)
    return pe.matmul(out, w_lo, x_hi, start=False, stop=stop, **kw)


class Kernel:
    def __init__(self, nc, ctx):
        self.nc, self.ctx = nc, ctx
        self.PE, self.ACT, self.DVE, self.POOL, self.SP = nc.tensor, nc.scalar, nc.vector, nc.gpsimd, nc.sync
        self.at = 16512

    def place(self, name, shape, dtype=F32, at=None):
        size = int(np.prod(shape[1:])) * mybir.dt.size(dtype)
        if at is None:
            at = self.at
            self.at += -(-size // 32) * 32
        return self.nc.alloc_sbuf_tensor_at(name, shape, dtype, offset=at)

    def region(self, size):
        at = self.at
        self.at += size
        return at

    def fresh_counters(self, tag):
        c, nc = self.ctx, self.nc
        self.pe = Done(nc, c, f"pe_done{tag}", self.PE)
        self.act = Done(nc, c, f"act_done{tag}", self.ACT)
        self.dve = Done(nc, c, f"dve_done{tag}", self.DVE)

    def loop(self, trips, per, body, slabs=0):
        per = dict(per)
        counters = list(per)
        if slabs:
            for c in (self.split_hi, self.split_lo, self.slab_used):
                counters.append(c)
                per[c] = slabs
        loop = Loop(trips)
        starts = {c: c.n for c in counters}
        others = {c: c.n for c in self.all_counters() if c not in per}
        for c in counters:
            c.steps.append((loop, per[c] * c.step))
        slab0 = self.slab
        if slabs:
            assert slabs % NRAW == 0 and slabs % NSPLIT == 0
            self.slab_steps.append((loop, slabs))
        with self.nc.Fori(0, trips) as turn:
            loop.turn = turn
            body(turn)
        loop.turn = None
        for c in counters:
            assert c.n - starts[c] == per[c] * c.step, (c.sem, c.n - starts[c], per[c] * c.step)
            c.steps.pop()
            c.n = starts[c] + per[c] * c.step * trips
        for c, n in others.items():
            assert c.n == n, ("not declared", c.sem)
        assert self.slab - slab0 == slabs
        if slabs:
            self.slab_steps.pop()
            self.slab = slab0 + slabs * trips

    def all_counters(self):
        return [self.pe, self.act, self.dve, self.split_hi, self.split_lo, self.slab_used]

    def raw_landed(self, ahead):
        n = self.slab + ahead
        return Count(self.raw_sems[n % NRAW], 16 * (n // NRAW + 1),
                     [(l, 16 * k // NRAW) for l, k in self.slab_steps])

    def split(self, ahead):
        n = self.slab + ahead
        raw, hi, lo = self.raw[:, n % NRAW, :], self.w_hi[:, n % NSPLIT, :], self.w_lo[:, n % NSPLIT, :]
        wait(self.ACT, self.raw_landed(ahead),
             self.slab_used.ahead(ahead - NSPLIT + 1))
        hi_ready = self.split_hi(self.ACT.activation(hi, raw, ACT.Copy))
        wait(self.DVE, hi_ready)
        self.split_lo(self.DVE.tensor_tensor(lo, raw, hi.bitcast(F32), ALU.subtract))

    def slab_step(self, source, products, closing=False):
        n = self.slab
        if n >= NRAW or self.slab_steps:
            wait(self.SP, self.split_lo.ahead(1 - self.split_ahead - NRAW))
        k = source.shape[1]
        self.SP.dma_start(self.raw[:, n % NRAW, :].rearrange("p (k n) -> p k n", k=k), source)\
            .then_inc(self.raw_sems[n % NRAW], 16)
        if closing:
            self.split_ahead -= 1
        else:
            self.split(LEAD)
        wait(self.PE, self.split_lo.ahead(-self.split_ahead))
        hi = self.w_hi[:, n % NSPLIT, :].rearrange("p (k n) -> p k n", k=k)
        lo = self.w_lo[:, n % NSPLIT, :].rearrange("p (k n) -> p k n", k=k)
        self.slab_used(products(hi, lo))
        self.slab += 1

    def open_stream(self):
        for ahead in range(LEAD):
            self.split(ahead)
        self.split_ahead = LEAD

    def close_stream(self, source):
        for ahead in range(LEAD):
            wait(self.SP, self.split_lo.ahead(1 - LEAD - NRAW + ahead))
            slot = (self.slab + ahead) % NRAW
            self.SP.dma_start(self.raw[:, slot:slot + 1, 0:P], source[:, 0:1, 0:P]).then_inc(self.raw_sems[slot], 16)
        wait(self.PE, self.split_lo.ahead(0))
        self.PE.drain().then_inc(self.slab_used.sem, LEAD)
        self.slab_used.n += LEAD
        self.slab += LEAD
        self.split_ahead = 0

    def allocate(self):
        nc, ctx, place = self.nc, self.ctx, self.place
        self.raw = place("raw", [P, NRAW, SLAB])
        self.w_hi = place("w_hi", [P, NSPLIT, SLAB], F32R)
        self.w_lo = place("w_lo", [P, NSPLIT, SLAB], F32R)
        self.xt = place("xt", [P, KD, S])
        self.ht_hi = place("ht_hi", [P, KD, S], F32R)
        self.ht_lo = place("ht_lo", [P, KD, S], F32R)
        self.params = place("params", [P, NPARAM])
        self.consts = place("consts", [P, NCONST])
        self.stage = place("stage", [P, NSTAGE])
        self.small = place("small", [P, 96])
        self.zero = place("zero", [P, P], BF16)
        self.eps = place("eps", [P, 1])
        self.junk = place("junk", [P, 1])
        self.root = place("root", [P, TT])
        self.ra = self.region(24 * 2 * S * 4)
        self.rb = self.region(2 * KD * S * 4)
        self.rc = self.region(8256)
        self.rd = self.region(4160)
        self.sq = place("sq", [P, KD, S], at=self.rc)
        self.h32 = place("h32", [P, KD, S], at=self.rc)
        self.spread = place("spread", [P, TT, P], at=self.rd)
        self.ps = ctx.enter_context(nc.psum_tensor("ps", [P, 8, 512], F32))
        self.rstd = self.ps[:, 7, S:2 * S]
        self.split_hi = Done(nc, ctx, "split_hi_done", self.ACT)
        self.split_lo = Done(nc, ctx, "split_lo_done", self.DVE)
        self.slab_used = Done(nc, ctx, "slab_used", self.PE)
        self.raw_sems = [ctx.enter_context(nc.semaphore(f"raw_landed{i}")) for i in range(NRAW)]
        self.slab, self.slab_steps, self.split_ahead = 0, [], 0
        self.fresh_counters("")
        self.load_sem = ctx.enter_context(nc.semaphore("small_loads"))
        self.loads = 0

    def load(self, out, source):
        self.POOL.dma_start(out, source).then_inc(self.load_sem, 16)
        self.loads += 16
        c = Count(self.load_sem, self.loads)
        wait(self.POOL, c)
        return c

    def param(self, name, i=0, n=1):
        at, _ = PARAMS[name]
        return self.params[:, at + i:at + i + n]

    def const(self, name, n=None):
        at, width = CONSTS[name]
        return self.consts[:, at:at + (n or width)]

    def ready_table(self, func):
        self.ACT.activation(self.junk[:, :], self.eps[:, :], func)

    def norm_factor(self, x_ready):
        nc, ps = self.nc, self.ps[:, 7, :]
        squares = []
        for k in range(0, KD, 2):
            wait(self.ACT, *(x_ready[k // 2:k // 2 + 1] if len(x_ready) == KD // 2 else x_ready[k + 1:k + 2]))
            squares.append(self.act(self.ACT.activation(self.sq[:, k:k + 2, :], self.xt[:, k:k + 2, :], ACT.Square)))
        if len(x_ready) == KD:
            wait(self.PE, x_ready[-1])
        for t in range(TT):
            for k in range(KD):
                wait(self.PE, squares[k // 2])
                mm = self.PE.matmul(ps[:, t:t + 1], self.sq[:, k, t * P:(t + 1) * P], self.const("ones", 1),
                                    start=k == 0, stop=k == KD - 1)
        summed = self.pe(mm)
        wait(self.ACT, summed)
        root = self.act(self.ACT.activation(self.root[:, :], ps[:, 0:TT], ACT.Sqrt, scale=1.0 / D, bias=self.eps[:, :]))
        wait(self.DVE, root)
        inverse = self.dve(self.DVE.reciprocal(self.root[:, :], self.root[:, :]))
        wait(self.DVE, inverse)
        for t in range(TT):
            spread = self.dve(self.DVE.tensor_scalar(self.spread[:, t, :], self.const("ones"), self.root[:, t:t + 1], None, ALU.mult))
        wait(self.PE, spread)
        for t in range(TT):
            mm = self.PE.matmul(ps[:, S + t * P:S + (t + 1) * P], self.spread[:, t, :], self.const("ident"), start=True, stop=True)
        return self.pe(mm)

    def norm(self, gain, x_ready, ht_free, row_major=False):
        wait(self.DVE, self.norm_factor(x_ready))
        highs, ready = [], []

        def low_part(k):
            wait(self.DVE, highs[k // 2])
            ready.append(self.dve(self.DVE.tensor_tensor(
                self.ht_lo[:, k:k + 2, :], self.h32[:, k:k + 2, :], self.ht_hi[:, k:k + 2, :].bitcast(F32), ALU.subtract)))
        for k in range(0, KD, 2):
            for c in (k, k + 1):
                whole = self.dve(self.DVE.scalar_tensor_tensor(
                    self.h32[:, c, :], self.xt[:, c, :], self.param(gain, c), self.rstd, ALU.mult, ALU.mult))
            wait(self.ACT, whole, *ht_free)
            highs.append(self.act(self.ACT.activation(self.ht_hi[:, k:k + 2, :], self.h32[:, k:k + 2, :], ACT.Copy)))
            if k:
                low_part(k - 2)
        low_part(KD - 2)
        return ready

    def split_from(self, hi, lo, source, source_ready, free=()):
        wait(self.ACT, source_ready, *free)
        high = self.act(self.ACT.activation(hi, source, ACT.Copy))
        wait(self.DVE, high)
        return self.dve(self.DVE.tensor_tensor(lo, source, hi.bitcast(F32), ALU.subtract))

    def columns(self, weight, start, n=2 * P):
        return weight.rearrange("(k p) n -> p k n", p=P)[:, :, bass.ds(start, n)]

    def rows(self, weight, start):
        return weight.rearrange("(k p) n -> p k n", p=P)[:, bass.ds(start, 2), :]

    def feature_major(self, bank, ht_ready=()):
        def products(hi, lo):
            for c in range(2):
                for k in range(KD):
                    if c == 0 and k % 2 == 0 and ht_ready:
                        wait(self.PE, ht_ready[k // 2])
                    mm = stationary_pair(self.PE, self.ps[:, bank, c * S:(c + 1) * S],
                                         hi[:, k, c * P:(c + 1) * P], lo[:, k, c * P:(c + 1) * P],
                                         self.ht_hi[:, k, :], self.ht_lo[:, k, :], k == 0, k == KD - 1)
            return mm
        return products

    def clear_banks(self, banks):
        for b in banks:
            self.PE.matmul(self.ps[:, b, :].rearrange("p (a n) -> p a n", n=P), self.zero[:, :],
                           self.zero[:, :].unsqueeze(1).to_broadcast([P, 4, P]), start=True, stop=True)

    def into_residual(self, weight, y_hi, y_lo, chunks, banks_free, closing=False):
        wait(self.PE, *banks_free)
        self.clear_banks(range(4))
        def step(start, i, closing=False):
            def products(hi, lo):
                for k in range(2):
                    for f in range(KD):
                        mm = stationary_pair(
                            self.PE, self.ps[:, f // 2, f % 2 * S:(f % 2 + 1) * S],
                            hi[:, k, f * P:(f + 1) * P], lo[:, k, f * P:(f + 1) * P],
                            y_hi(start + k), y_lo(start + k), False, False, skip_group_check=True)
                return mm
            self.slab_step(self.rows(weight, start), products, closing)
        steps = chunks // 2
        whole = steps // NRAW if steps >= 2 * NRAW else 0
        if whole:
            def body(turn):
                for j in range(NRAW):
                    step(turn * (2 * NRAW) + 2 * j, j)
            self.loop(whole, {}, body, slabs=NRAW)
        for i in range(whole * NRAW, steps):
            step(2 * i, i)
        done = self.slab_used.ahead(0)
        ready = []
        self.ready_table(ACT.Sqrt)
        for b in range(4):
            wait(self.DVE, done)
            ready.append(self.dve(self.DVE.tensor_tensor(
                self.xt[:, 2 * b:2 * b + 2, :], self.ps[:, b, :].rearrange("p (c s) -> p c s", c=2),
                self.xt[:, 2 * b:2 * b + 2, :], ALU.add)))
        return ready

    def load_input(self, x):
        rows = self.place("x_rows", [P, TT, D], at=self.ra)
        self.SP.dma_start(rows[:, :, :], x.rearrange("a (t p) d -> p (a t) d", p=P)).then_inc(self.x_sem, 16)
        landed = Count(self.x_sem, 16)
        ready = []
        wait(self.PE, landed)
        for k in range(0, KD, 2):
            for c in (k, k + 1):
                for t in range(TT):
                    mm = self.PE.transpose(self.ps[:, k // 2, (c - k) * S + t * P:(c - k) * S + (t + 1) * P],
                                           rows[:, t, c * P:(c + 1) * P], self.const("ident"))
            turned = self.pe(mm)
            wait(self.DVE, turned)
            ready.append(self.dve(self.DVE.tensor_copy(
                self.xt[:, k:k + 2, :], self.ps[:, k // 2, :].rearrange("p (c s) -> p c s", c=2))))
        return ready

    def project_inputs(self, w_in, ht_ready):
        self.u = u = self.place("u", [P, 24, S], at=self.ra)
        def body(turn):
            for j in range(NRAW):
                start = turn * (NRAW * BW + (COL_D - COL_DT if j >= 3 else 0)) + j * BW
                engine, done = (self.ACT, self.act) if j % 2 == 0 else (self.DVE, self.dve)
                wait(self.PE, done.ahead(1 - NRAW // 2))
                self.slab_step(self.columns(w_in, start), self.feature_major(j, ht_ready if j == 0 else ()))
                out = u[:, bass.ds(turn * 12 + 2 * j, 2), :]
                whole = self.ps[:, j, :].rearrange("p (c s) -> p c s", c=2)
                wait(engine, self.slab_used.ahead(0))
                done(engine.activation(out, whole, ACT.Copy) if j % 2 == 0 else engine.tensor_copy(out, whole))
        self.loop(2, {self.act: NRAW // 2, self.dve: NRAW // 2}, body, slabs=NRAW)
        return [self.act.ahead(0), self.dve.ahead(0)]

    def token_major(self, bank, chunks, out, ready, free=()):
        wait(self.PE, *ready, *free)
        for t in range(TT):
            for c in range(2):
                mm = self.PE.transpose(self.ps[:, bank, t * S + c * P:t * S + (c + 1) * P],
                                       self.u[:, chunks + c, t * P:(t + 1) * P], self.const("ident"))
        turned = self.pe(mm)
        wait(self.DVE, turned)
        return self.dve(self.DVE.tensor_copy(out, self.ps[:, bank, :].rearrange("p (t f) -> p t f", t=TT)))

    def softplus(self, out, x, x_ready, scratch):
        wait(self.ACT, x_ready)
        a = self.act(self.ACT.activation(scratch, x, ACT.Abs))
        wait(self.ACT, a)
        b = self.act(self.ACT.activation(scratch, scratch, ACT.Exp, scale=-1.0))
        wait(self.ACT, b)
        c = self.act(self.ACT.activation(scratch, scratch, ACT.Ln, bias=1.0))
        wait(self.DVE, c)
        return self.dve(self.DVE.scalar_tensor_tensor(out, x, 0.0, scratch, ALU.max, ALU.add))

    def weighted_values(self, banks, weights, values, ready):
        wait(self.PE, *ready)
        for h in range(NH):
            low = h % 2 * HD
            out = self.ps[low:low + HD, banks + h // 2, :]
            v = lambda t: values[:, t, h * HD:(h + 1) * HD]
            self.PE.matmul(out[:, 0:S], v(0), weights[:, h, 0:S], start=True, stop=False)
            mm = self.PE.matmul(out[:, P:S], v(1), weights[:, h, S:S + P], start=False, stop=True)
        return self.pe(mm)

    def mixers(self, u_ready):
        PE, ACT_, DVE, pe, act, dve, u, ps = self.PE, self.ACT, self.DVE, self.pe, self.act, self.dve, self.u, self.ps
        W3 = S + P
        self.y_hi = y_hi = self.place("y_hi", [P, KD, S], F32R, at=self.rb)
        self.y_lo = y_lo = self.place("y_lo", [P, KD, S], F32R, at=self.rb + KD * S * 4)
        zb = self.place("sb_scores", [P, NH, W3], at=self.ra + 24576)
        sb = self.place("sb_softplus", [P, NH, W3], at=self.ra + 24576 + 6144)
        zd = self.place("moba_scores", [P, NH, W3], at=self.ra + 24576 + 12288)
        pd = self.place("moba_turned", [P, NH, W3], at=self.ra + 24576 + 18432)
        vb = self.place("sb_values", [P, TT, BW], at=self.rc)
        vd = self.place("moba_values", [P, TT, BW], at=self.rc + 2048)
        xd = self.place("ssm_values", [P, TT, BW], at=self.rc + 4096)
        ap = self.place("a_padded", [P, 2, S + 2], at=self.rc + 6144)
        cp = self.place("xbc_padded", [P, 4, S + 3], at=self.rd)
        tri = self.place("ssm_steps", [P, NH, W3], at=self.ra + 18 * 1024)
        dm = self.place("ssm_decay", [P, NH, W3], at=self.ra + 6 * 1024)
        small = self.small
        strict = self.stage[:, 0:W3]
        causal = self.stage[:, W3:2 * W3]
        ssm_mask = self.stage[:, 2 * W3:3 * W3]
        over_heads = lambda a: a.unsqueeze(1).to_broadcast([P, NH, a.shape[-1]])

        vb_ready = self.token_major(4, 10, vb[:, :, :], u_ready)
        vd_ready = self.token_major(5, 22, vd[:, :, :], u_ready)

        for h in range(NH):
            r = slice(h % 2 * HD, h % 2 * HD + HD)
            q, k = u[r, 6 + h // 2, :], u[r, 8 + h // 2, :]
            PE.matmul(ps[:, h, 0:S], k[:, 0:P], q, start=True, stop=True)
            mm = PE.matmul(ps[:, h, S:W3], k[:, P:S], q[:, P:S], start=True, stop=True)
        scores_b = pe(mm)
        wait(PE, vb_ready, vd_ready)
        for h in range(NH):
            r = slice(h % 2 * HD, h % 2 * HD + HD)
            q, k = u[r, 18 + h // 2, :], u[r, 20 + h // 2, :]
            PE.matmul(ps[:, 4 + h, 0:P], q[:, 0:P], k[:, 0:P], start=True, stop=True)
            mm = PE.matmul(ps[:, 4 + h, P:W3], q[:, P:S], k, start=True, stop=True)
        scores_d = pe(mm)
        wait(DVE, scores_b)
        zb_ready = dve(DVE.scalar_tensor_tensor(zb[:, :, :], ps[:, 0:4, 0:W3], HD ** -0.5, over_heads(strict), ALU.mult, ALU.add))
        wait(DVE, scores_d)
        zd_ready = dve(DVE.scalar_tensor_tensor(zd[:, :, :], ps[:, 4:8, 0:W3], HD ** -0.5, over_heads(causal), ALU.mult, ALU.add))

        sp_ready = self.softplus(sb[:, :, :], zb[:, :, :], zb_ready, sb[:, :, :])
        wait(PE, sp_ready)
        for h in range(NH):
            PE.matmul(ps[:, h, 0:S], self.const("suffix"), sb[:, h, 0:S], start=True, stop=False)
            PE.matmul(ps[:, h, P:S], self.const("ones"), sb[:, h, S:W3], start=False, stop=True)
            mm = PE.matmul(ps[:, h, S:W3], self.const("suffix"), sb[:, h, S:W3], start=True, stop=True)
        sums = pe(mm)

        top, total = small[:, 0:8], small[:, 8:16]
        wait(DVE, zd_ready)
        dve(DVE.tensor_reduce(top[:, 0:4], zd[:, :, 0:P], AX.X, ALU.max))
        tops = dve(DVE.tensor_reduce(top[:, 4:8], zd[:, :, P:W3], AX.X, ALU.max))
        wait(DVE, tops)
        negated = dve(DVE.tensor_scalar(top, top, -1.0, None, ALU.mult))
        wait(ACT_, negated)
        for t in range(TT):
            cols = slice(0, P) if t == 0 else slice(P, W3)
            for h in range(NH):
                e = act(ACT_.activation(zd[:, h, cols], zd[:, h, cols], ACT.Exp, bias=top[:, 4 * t + h:4 * t + h + 1],
                                        accum_out=total[:, 4 * t + h:4 * t + h + 1]))
        wait(DVE, e)
        inverse = dve(DVE.reciprocal(total, total))
        wait(DVE, inverse)
        for t in range(TT):
            cols = slice(0, P) if t == 0 else slice(P, W3)
            for h in range(NH):
                weights_d = dve(DVE.tensor_scalar(zd[:, h, cols], zd[:, h, cols], total[:, 4 * t + h:4 * t + h + 1], None, ALU.mult))
        wait(PE, weights_d)
        for h in range(NH):
            for source, target in ((0, 0), (P, P), (S, S)):
                mm = PE.transpose(ps[:, 4 + h, target:target + P], zd[:, h, source:source + P], self.const("ident"))
        turned = pe(mm)
        wait(ACT_, turned)
        pd_ready = act(ACT_.activation(pd[:, :, :], ps[:, 4:8, 0:W3], ACT.Copy))
        wait(DVE, sums)
        exponent = dve(DVE.tensor_tensor(zb[:, :, :], zb[:, :, :], ps[:, 0:4, 0:W3], ALU.subtract))
        wait(ACT_, exponent)
        wb_ready = act(ACT_.activation(zb[:, :, :], zb[:, :, :], ACT.Exp))
        out_b = self.weighted_values(0, zb, vb, [wb_ready])
        out_d = self.weighted_values(4, pd, vd, [pd_ready])
        two = lambda bank: ps[:, bank:bank + 2, 0:S]
        y_b = self.split_from(y_hi[:, 2:4, :], y_lo[:, 2:4, :], two(0), out_b)
        y_d = self.split_from(y_hi[:, 6:8, :], y_lo[:, 6:8, :], two(4), out_d)

        wait(DVE, *u_ready)
        zeroed = dve(DVE.memset(ap[:, :, 0:2], 0.0))
        filled = dve(DVE.tensor_tensor(ap[:, :, 2:S + 2], u[:, 4:6, :], u[:, 0:2, :], ALU.mult))
        wait(DVE, filled)
        tap = lambda c, j: self.param("a_taps", 3 * c + j)
        for j in range(3):
            for c in range(2):
                if j == 0:
                    last = dve(DVE.tensor_scalar(u[:, c, :], ap[:, c, 0:S], tap(c, 0), None, ALU.mult))
                else:
                    last = dve(DVE.scalar_tensor_tensor(u[:, c, :], ap[:, c, j:j + S], tap(c, j), u[:, c, :], ALU.mult, ALU.add))
            wait(DVE, last)
        ya = dve(DVE.tensor_tensor(u[:, 0:2, :], u[:, 0:2, :], u[:, 2:4, :], ALU.mult))
        y_a = self.split_from(y_hi[:, 0:2, :], y_lo[:, 0:2, :], u[:, 0:2, :], ya)

        zeroed = dve(DVE.memset(cp[:, :, 0:3], 0.0))
        wait(ACT_, *u_ready)
        copied = act(ACT_.activation(cp[:, :, 3:S + 3], u[:, 14:18, :], ACT.Copy))
        wait(DVE, zeroed, copied)
        tap = lambda c, j: self.param("ssm_taps", 4 * c + j)
        for j in range(4):
            for c in range(4):
                if j == 0:
                    last = dve(DVE.tensor_scalar(u[:, 14 + c, :], cp[:, c, 0:S], tap(c, 0), self.param("ssm_bias", c), ALU.mult, ALU.add))
                else:
                    last = dve(DVE.scalar_tensor_tensor(u[:, 14 + c, :], cp[:, c, j:j + S], tap(c, j), u[:, 14 + c, :], ALU.mult, ALU.add))
            wait(DVE, last)
        wait(ACT_, last)
        act(ACT_.activation(u[:, 12:14, :], u[:, 12:14, :], ACT.Silu))
        xbc = act(ACT_.activation(u[:, 14:18, :], u[:, 14:18, :], ACT.Silu))

        wait(PE, y_d)
        for t in range(TT):
            for k in range(KD):
                for part in (self.ht_hi, self.ht_lo):
                    mm = PE.matmul(ps[:, 6, t * NH:(t + 1) * NH], part[:, k, t * P:(t + 1) * P].bitcast(F32),
                                   self.param("w_dt", k * NH, NH), start=k == 0 and part is self.ht_hi,
                                   stop=k == KD - 1 and part is self.ht_lo)
        dts = pe(mm)
        dt, step, scratch = small[:, 16:24], small[:, 24:32], small[:, 32:40]
        rate, before = small[:, 40:48], small[:, 48:56]
        wait(DVE, dts)
        shifted = dve(DVE.tensor_tensor(dt, ps[:, 6, 0:8], self.param("dt_bias", 0, 8), ALU.add))
        dt_ready = self.softplus(dt, dt, shifted, scratch)
        exp_a = act(ACT_.activation(rate, self.param("a_log", 0, 8), ACT.Exp))
        wait(DVE, exp_a, dt_ready)
        steps = dve(DVE.scalar_tensor_tensor(step, dt, -1.0, rate, ALU.mult, ALU.mult))
        wait(PE, steps)
        PE.matmul(ps[:, 7, 0:4], self.const("prefix"), step[:, 0:4], start=True, stop=True)
        PE.matmul(ps[:, 7, 4:8], self.const("ones"), step[:, 0:4], start=True, stop=False)
        summed = pe(PE.matmul(ps[:, 7, 4:8], self.const("prefix"), step[:, 4:8], start=False, stop=True))
        wait(DVE, summed, steps)
        before_ready = dve(DVE.tensor_scalar(before, ps[:, 7, 0:8], -1.0, None, ALU.mult))
        prefix_ones = self.consts[:, CONSTS["prefix"][0]:CONSTS["prefix"][0] + S]
        for h in range(NH):
            dve(DVE.tensor_scalar(tri[:, h, 0:S], prefix_ones, step[:, h:h + 1], None, ALU.mult))
            tri_ready = dve(DVE.tensor_scalar(tri[:, h, S:W3], self.const("prefix"), step[:, 4 + h:5 + h], None, ALU.mult))
        wait(PE, tri_ready, y_b)
        for h in range(NH):
            PE.matmul(ps[:, h, 0:S], self.const("ones"), tri[:, h, 0:S], start=True, stop=False)
            mm = PE.matmul(ps[:, h, P:S], self.const("ones"), tri[:, h, S:W3], start=False, stop=True)
        running = pe(mm)
        wait(DVE, running, before_ready)
        for h in range(NH):
            dve(DVE.scalar_tensor_tensor(dm[:, h, 0:S], ps[:, h, 0:S], before[:, h:h + 1], ssm_mask[:, 0:S], ALU.add, ALU.add))
            seg = dve(DVE.scalar_tensor_tensor(dm[:, h, S:W3], ps[:, h, P:S], before[:, 4 + h:5 + h], ssm_mask[:, S:W3], ALU.add, ALU.add))
        wait(ACT_, seg)
        decay = act(ACT_.activation(dm[:, :, :], dm[:, :, :], ACT.Exp))
        wait(PE, xbc, dt_ready)
        for g in range(2):
            r = slice(g * HD, g * HD + HD)
            b, c = u[r, 16, :], u[r, 17, :]
            PE.matmul(ps[:, 4 + g, 0:S], b[:, 0:P], c, start=True, stop=True)
            mm = PE.matmul(ps[:, 4 + g, S:W3], b[:, P:S], c[:, P:S], start=True, stop=True)
        products = pe(mm)
        wait(DVE, decay, products)
        for h in range(NH):
            mixed = dve(DVE.tensor_tensor(dm[:, h, :], dm[:, h, :], ps[:, 4 + h // 2, 0:W3], ALU.mult))
        wait(PE, xbc, before_ready)
        for t in range(TT):
            for c in range(2):
                mm = PE.transpose(ps[:, 7, t * S + c * P:t * S + (c + 1) * P], u[:, 14 + c, t * P:(t + 1) * P], self.const("ident"))
        turned = pe(mm)
        wait(DVE, turned)
        for t in range(TT):
            for h in range(NH):
                xd_ready = dve(DVE.tensor_scalar(xd[:, t, h * HD:(h + 1) * HD], ps[:, 7, t * S + h * HD:t * S + (h + 1) * HD],
                                                 dt[:, 4 * t + h:4 * t + h + 1], None, ALU.mult))
        out_c = self.weighted_values(0, dm, xd, [mixed, xd_ready])
        wait(DVE, out_c)
        for c in range(2):
            skipped = dve(DVE.scalar_tensor_tensor(u[:, 14 + c, :], u[:, 14 + c, :], self.param("skip", c), ps[:, c, 0:S], ALU.mult, ALU.add))
        wait(DVE, skipped)
        gated = dve(DVE.tensor_tensor(u[:, 14:16, :], u[:, 14:16, :], u[:, 12:14, :], ALU.mult))
        wait(ACT_, gated)
        squares = act(ACT_.activation(u[:, 12:14, :], u[:, 14:16, :], ACT.Square))
        wait(PE, squares, mixed)
        for c in range(2):
            mm = PE.matmul(ps[:, 4, c * S:(c + 1) * S], self.const("ones"), u[:, 12 + c, :], start=True, stop=True)
        summed = pe(mm)
        factor = u[:, 16:18, :]
        wait(ACT_, summed)
        m = act(ACT_.activation(factor, ps[:, 4, :].rearrange("p (c s) -> p c s", c=2), ACT.Sqrt, scale=1.0 / P, bias=self.eps[:, :]))
        wait(DVE, m)
        m = dve(DVE.reciprocal(factor, factor))
        wait(DVE, m)
        for c in range(2):
            normed = dve(DVE.scalar_tensor_tensor(u[:, 14 + c, :], u[:, 14 + c, :], self.param("ssm_norm", c), u[:, 16 + c, :], ALU.mult, ALU.mult))
        y_c = self.split_from(y_hi[:, 4:6, :], y_lo[:, 4:6, :], u[:, 14:16, :], normed)
        return [y_a, y_b, y_c, y_d]

    def merge(self, w_branch, w_in, y_ready):
        ps, PE, ACT_, DVE = self.ps, self.PE, self.ACT, self.DVE
        merged = self.place("merged", [P, KD, S], at=self.ra)
        sig = self.place("gates", [P, 2, 2, S], at=self.ra + 8192)
        term = self.place("gated", [P, 2, S], at=self.ra + 12288)
        m_hi = self.place("m_hi", [P, KD, S], F32R, at=self.ra + 16384)
        m_lo = self.place("m_lo", [P, KD, S], F32R, at=self.ra + 24576)
        branch_rows = w_branch.rearrange("a b (k p) n -> p (a b k) n", p=P)
        wait(PE, *y_ready)
        used = []
        for i in range(4):
            def products(hi, lo):
                for f in range(KD):
                    for k in range(2):
                        mm = stationary_pair(PE, ps[:, f // 2, f % 2 * S:(f % 2 + 1) * S],
                                             hi[:, k, f * P:(f + 1) * P], lo[:, k, f * P:(f + 1) * P],
                                             self.y_hi[:, 2 * i + k, :], self.y_lo[:, 2 * i + k, :], k == 0, k == 1)
                return mm
            wait(PE, *used[-1:])
            self.slab_step(branch_rows[:, 2 * i:2 * i + 2, :], products)
            for q in range(4):
                n = 4 * i + q
                bank = 4 + n % 2
                if n >= 2:
                    wait(PE, used[n - 2])
                self.slab_step(self.columns(w_in, COL_G + i * D + q * 2 * P), self.feature_major(bank))
                wait(ACT_, self.slab_used.ahead(0), *used[n - 2:n - 1] if n >= 2 else ())
                gate = self.act(ACT_.activation(sig[:, n % 2, :, :], ps[:, bank, :].rearrange("p (c s) -> p c s", c=2), ACT.Sigmoid))
                wait(DVE, gate, *used[-1:])
                part = ps[:, q, :].rearrange("p (c s) -> p c s", c=2)
                if i == 0:
                    used.append(self.dve(DVE.tensor_tensor(merged[:, 2 * q:2 * q + 2, :], sig[:, n % 2, :, :], part, ALU.mult)))
                    continue
                used.append(self.dve(DVE.tensor_tensor(term[:, :, :], sig[:, n % 2, :, :], part, ALU.mult)))
                wait(DVE, used[-1])
                used[-1] = self.dve(DVE.tensor_tensor(merged[:, 2 * q:2 * q + 2, :], merged[:, 2 * q:2 * q + 2, :], term[:, :, :], ALU.add))
        ready = []
        for q in range(4):
            c = slice(2 * q, 2 * q + 2)
            ready.append(self.split_from(m_hi[:, c, :], m_lo[:, c, :], merged[:, c, :], used[12 + q]))
        return m_hi, m_lo, ready

    def feed_forward(self, tag, gate, up, down, ht_ready, banks_free):
        ps, PE, ACT_, DVE, act, dve = self.ps, self.PE, self.ACT, self.DVE, self.act, self.dve
        chunks = FF // P
        a_hi = self.place(f"ff_hi{tag}", [P, chunks, S], F32R, at=self.ra)
        a_lo = self.place(f"ff_lo{tag}", [P, chunks, S], F32R, at=self.ra + chunks * S * 4)
        silu = self.place(f"ff_silu{tag}", [P, 3, 2 * S], at=self.rb)
        whole = self.place(f"ff_act{tag}", [P, 3, 2 * S], at=self.rb + 6144)
        wait(PE, *banks_free)
        def step(turn, j, ht_ready=()):
            b = j % 3
            pair = turn * 3 + j
            earlier = dve.ahead(-5)
            wait(PE, earlier)
            self.slab_step(gate(pair), self.feature_major(2 * b, ht_ready))
            wait(ACT_, self.slab_used.ahead(0), earlier)
            s = act(ACT_.activation(silu[:, b, :], ps[:, 2 * b, :], ACT.Silu))
            self.slab_step(up(pair), self.feature_major(2 * b + 1))
            wait(DVE, self.slab_used.ahead(0), s, act.ahead(-5), dve.ahead(0))
            m = dve(DVE.tensor_tensor(whole[:, b, :], silu[:, b, :], ps[:, 2 * b + 1, :], ALU.mult))
            chunk = bass.ds(pair * 2, 2)
            flat = whole[:, b, :].rearrange("p (c s) -> p c s", c=2)
            self.split_from(a_hi[:, chunk, :], a_lo[:, chunk, :], flat, m)
        def body(turn):
            for j in range(3):
                step(turn, j, ht_ready if j == 0 else ())
        pairs = chunks // 2
        self.loop(pairs // 3, {act: 6, dve: 6}, body, slabs=NRAW)
        for j in range(pairs % 3):
            step(pairs // 3, j)
        a_ready = dve.ahead(0)
        return self.into_residual(down, lambda c: a_hi[:, bass.ds(c, 1), :].rearrange("p a s -> p (a s)"),
                                  lambda c: a_lo[:, bass.ds(c, 1), :].rearrange("p a s -> p (a s)"), chunks, [a_ready, act.ahead(0)])

    def norm_in_place(self, gain, x_ready):
        wait(self.DVE, self.norm_factor(x_ready))
        return [self.dve(self.DVE.scalar_tensor_tensor(
            self.xt[:, c, :], self.xt[:, c, :], self.param(gain, c), self.rstd, ALU.mult, ALU.mult))
            for c in range(KD)]

    def retention(self, w_in, w_out, ht_ready, banks_free, stage_ready):
        ps, PE, ACT_, DVE, pe, act, dve = self.ps, self.PE, self.ACT, self.DVE, self.pe, self.act, self.dve
        small = self.small
        q_t = self.place("ret_q", [P, KD, S], at=self.ra)
        k_t = self.place("ret_k", [P, KD, S], at=self.ra + 8192)
        v = self.place("ret_v", [P, TT, 2 * D], at=self.ra + 16384)
        g_t = self.place("ret_g", [P, 2 * KD, S], at=self.ra + 32768)
        cos_part = self.place("ret_cos", [P, 2, S], at=self.rd)
        sin_part = self.place("ret_sin", [P, 2, S], at=self.rd + 2048)
        table = lambda i: self.stage[:, i * S:(i + 1) * S].unsqueeze(1).to_broadcast([P, 2, S])
        wait(PE, *banks_free)
        wait(DVE, stage_ready)

        def head(turn):
            for b, out in ((0, q_t), (1, k_t)):
                wait(PE, dve.ahead(2 - 8))
                self.slab_step(self.columns(w_in, turn * BW + b * D), self.feature_major(b, ht_ready if b == 0 else ()))
                pair = ps[:, b, :].rearrange("p (c s) -> p c s", c=2)
                wait(DVE, self.slab_used.ahead(0), dve.ahead(0))
                dve(DVE.tensor_tensor(cos_part[:, :, :], pair, table(0), ALU.mult))
                parts = dve(DVE.tensor_tensor(sin_part[:, :, :], pair, table(1), ALU.mult))
                wait(DVE, parts)
                first, second = out[:, bass.ds(turn * 2, 1), :], out[:, bass.ds(turn * 2 + 1, 1), :]
                dve(DVE.tensor_tensor(first, cos_part[:, 0:1, :], sin_part[:, 1:2, :], ALU.subtract))
                dve(DVE.tensor_tensor(second, sin_part[:, 0:1, :], cos_part[:, 1:2, :], ALU.add))
            for c in range(2):
                wait(PE, act.ahead(1 - 4))
                def products(hi, lo, bank=2 + c):
                    for t in range(TT):
                        tok = slice(t * P, (t + 1) * P)
                        for k in range(KD):
                            out = ps[:, bank, t * S:(t + 1) * S]
                            PE.matmul(out, self.ht_hi[:, k, tok], hi[:, k, :], start=k == 0, stop=False)
                            PE.matmul(out, self.ht_hi[:, k, tok], lo[:, k, :], start=False, stop=False)
                            mm = PE.matmul(out, self.ht_lo[:, k, tok], hi[:, k, :], start=False, stop=k == KD - 1)
                    return mm
                self.slab_step(self.columns(w_in, turn * (2 * BW) + 2 * D + c * BW), products)
                wait(ACT_, self.slab_used.ahead(0))
                act(ACT_.activation(v[:, :, bass.ds(turn * (2 * BW) + c * BW, BW)],
                                    ps[:, 2 + c, :].rearrange("p (t f) -> p t f", t=TT), ACT.Copy))
            for c in range(2):
                wait(PE, act.ahead(1 - 4))
                self.slab_step(self.columns(w_in, turn * (2 * BW) + 4 * D + c * BW), self.feature_major(4 + c))
                wait(ACT_, self.slab_used.ahead(0))
                act(ACT_.activation(g_t[:, bass.ds(turn * 4 + 2 * c, 2), :],
                                    ps[:, 4 + c, :].rearrange("p (c s) -> p c s", c=2), ACT.Silu))
        decay = self.place("ret_decay", [P, NH, 2, S], at=self.rc)
        rate, tiny = small[:, 64:72], small[:, 72:80]
        logit = self.param("decay", 0, 8)
        a = act(ACT_.activation(tiny, logit, ACT.Abs))
        wait(ACT_, a)
        b = act(ACT_.activation(tiny, tiny, ACT.Exp, scale=-1.0))
        wait(ACT_, b)
        b = act(ACT_.activation(tiny, tiny, ACT.Ln, bias=1.0))
        wait(DVE, b)
        r = dve(DVE.scalar_tensor_tensor(rate, logit, 0.0, tiny, ALU.min, ALU.subtract))
        wait(DVE, r, *ht_ready)
        for h in range(NH):
            for m in range(TT):
                ahead = self.stage[:, (2 + m) * S:(3 + m) * S]
                behind = self.stage[:, (4 + m) * S:(5 + m) * S]
                a = dve(DVE.tensor_scalar(decay[:, h, m, :], ahead, rate[:, h:h + 1], None, ALU.mult))
                wait(DVE, a)
                a = dve(DVE.scalar_tensor_tensor(decay[:, h, m, :], behind, rate[:, 4 + h:5 + h], decay[:, h, m, :], ALU.mult, ALU.add))
        wait(ACT_, a, *ht_ready)
        decay_ready = act(ACT_.activation(decay[:, :, :, :], decay[:, :, :, :], ACT.Exp))
        self.loop(NH, {act: 4, dve: 8}, head, slabs=NRAW)
        loop_act, loop_dve = act.ahead(0), dve.ahead(0)

        wait(PE, loop_dve, loop_act)
        for h in range(NH):
            for m in range(TT):
                for c in range(2):
                    mm = PE.matmul(ps[:, h, m * S:(m + 1) * S], k_t[:, 2 * h + c, m * P:(m + 1) * P], q_t[:, 2 * h + c, :],
                                   start=c == 0, stop=c == 1)
            scored = pe(mm)
            wait(DVE, scored, decay_ready)
            pair = ps[:, h, :].rearrange("p (m s) -> p m s", m=2)
            weights = dve(DVE.scalar_tensor_tensor(decay[:, h, :, :], pair, 1.0 / 16, decay[:, h, :, :], ALU.mult, ALU.mult))
        y_hi = self.place("ret_y_hi", [P, 2 * KD, S], F32R, at=self.ra)
        y_lo = self.place("ret_y_lo", [P, 2 * KD, S], F32R, at=self.rb)
        yn = self.place("ret_normed", [P, TT, 2 * BW], at=self.rd)
        stats, moments = small[:, 80:92], small[:, 92:96]
        summed, normed, turned, ready = [], [], [], []
        wait(PE, weights)

        def values(h):
            for t in range(TT):
                bank = 4 - h % 2 * 4 + t
                wait(PE, *normed[h - 2][t:t + 1] if h >= 2 else ())
                for m in range(TT):
                    mm = PE.matmul(ps[:, bank, :], decay[:, h, m, t * P:(t + 1) * P],
                                   v[:, m, h * 2 * BW:(h + 1) * 2 * BW], start=m == 0, stop=m == TT - 1)
                summed.append(pe(mm))

        def norm_values(h):
            normed.append([])
            for t in range(TT):
                bank = 4 - h % 2 * 4 + t
                wait(DVE, summed[2 * h + t], loop_dve)
                a = dve(DVE.bn_stats(stats[:, 6 * t:6 * t + 6], ps[:, bank, :]))
                wait(DVE, a)
                a = dve(DVE.bn_aggr(moments[:, 2 * t:2 * t + 2], stats[:, 6 * t:6 * t + 6]))
                wait(ACT_, a)
                a = act(ACT_.activation(stats[:, 6 * t:6 * t + 1], moments[:, 2 * t + 1:2 * t + 2], ACT.Sqrt, bias=self.eps[:, :]))
                wait(DVE, a)
                a = dve(DVE.reciprocal(stats[:, 6 * t:6 * t + 1], stats[:, 6 * t:6 * t + 1]))
                wait(DVE, a, *turned[-1:])
                normed[h].append(dve(DVE.tensor_scalar(yn[:, t, :], ps[:, bank, :], moments[:, 2 * t:2 * t + 1],
                                                       stats[:, 6 * t:6 * t + 1], ALU.subtract, ALU.mult)))

        def turn_values(h):
            wait(PE, *normed[h], *ready[-1:])
            for c in range(4):
                for t in range(TT):
                    mm = PE.transpose(ps[:, 6 + c // 2, c % 2 * S + t * P:c % 2 * S + (t + 1) * P],
                                      yn[:, t, c * P:(c + 1) * P], self.const("ident"))
            turned.append(pe(mm))
            wait(DVE, turned[-1])
            for c in range(4):
                z = dve(DVE.scalar_tensor_tensor(g_t[:, 4 * h + c, :], ps[:, 6 + c // 2, c % 2 * S:(c % 2 + 1) * S],
                                                 self.param("gn_gain", 4 * h + c), g_t[:, 4 * h + c, :], ALU.mult, ALU.mult))
            c = slice(4 * h, 4 * h + 4)
            ready.append(self.split_from(y_hi[:, c, :], y_lo[:, c, :], g_t[:, c, :], z))
        values(0)
        for h in range(NH):
            norm_values(h)
            if h + 1 < NH:
                values(h + 1)
            turn_values(h)
        one = lambda a: (lambda c: a[:, bass.ds(c, 1), :].rearrange("p a s -> p (a s)"))
        return self.into_residual(w_out, one(y_hi), one(y_lo), 2 * KD, ready)

    def fourier(self, w_out, ht_ready, stage_ready):
        ps, PE, ACT_, DVE, pe, act, dve = self.ps, self.PE, self.ACT, self.DVE, self.pe, self.act, self.dve
        mixed = self.place("fft_features", [P, KD, 2 * S], at=self.ra)
        y_hi = self.place("fft_hi", [P, KD, S], F32R, at=self.rb)
        y_lo = self.place("fft_lo", [P, KD, S], F32R, at=self.rb + KD * S * 4)
        cos_sin = self.stage[:, 0:4 * S].rearrange("p (c n) -> p c n", c=2)
        minus_sin = self.stage[:, 4 * S:6 * S].rearrange("p (c n) -> p c n", c=2)
        wait(PE, *ht_ready, stage_ready)
        copied = []
        for g in range(4):
            for t in range(TT):
                b = 2 * g + t
                for c in range(2):
                    mm = PE.matmul(ps[:, b, :], self.h32[:, 2 * g + c, t * P:(t + 1) * P], cos_sin[:, c, :],
                                   start=c == 0, stop=c == 1)
                done = pe(mm)
                engine, count = (ACT_, act) if b % 2 else (DVE, dve)
                wait(engine, done)
                copied.append(count(engine.activation(mixed[:, b, :], ps[:, b, :], ACT.Copy) if b % 2
                                    else engine.tensor_copy(mixed[:, b, :], ps[:, b, :])))
        ready = []
        for g in range(4):
            wait(PE, copied[2 * g], copied[2 * g + 1])
            for c in range(2):
                for t in range(TT):
                    out = ps[:, g, c * S:(c + 1) * S]
                    PE.matmul(out, mixed[:, 2 * g + t, c * P:(c + 1) * P], cos_sin[:, t, 0:S], start=t == 0, stop=False)
                    mm = PE.matmul(out, mixed[:, 2 * g + t, S + c * P:S + (c + 1) * P], minus_sin[:, t, :],
                                   start=False, stop=t == TT - 1)
            done = pe(mm)
            ready.append(self.split_from(y_hi[:, 2 * g:2 * g + 2, :], y_lo[:, 2 * g:2 * g + 2, :],
                                         ps[:, g, :].rearrange("p (c s) -> p c s", c=2), done))
        one = lambda a: (lambda c: a[:, bass.ds(c, 1), :].rearrange("p a s -> p (a s)"))
        return self.into_residual(w_out, one(y_hi), one(y_lo), KD, ready)

    def route(self, ht_ready):
        ps, PE, ACT_, DVE, pe, act, dve = self.ps, self.PE, self.ACT, self.DVE, self.pe, self.act, self.dve
        self.rows_hi = rows_hi = self.place("rows_hi", [P, TT, D], F32R, at=self.rb)
        self.rows_lo = rows_lo = self.place("rows_lo", [P, TT, D], F32R, at=self.rb + TT * D * 4)
        names = ["logit", "score", "first", "rest", "second", "gate", "chosen"]
        at = self.ra + 32768
        tiles = {}
        for n in names:
            tiles[n] = self.place("route_" + n, [P, TT, NE], at=at)
            at += TT * NE * 4
        self.gates = self.place("gates_of", [P, TT, NE + 1], at=at)
        self.places = self.place("place_of", [P, TT, NE + 1], at=at + 96)
        self.total = self.place("chosen_total", [P, NE + 1], at=at + 192)
        self.most = self.place("most_chosen", [P, 1], I32, at=at + 256)
        col = self.place("route_columns", [P, 16], at=at + 288)
        logit, score, first, rest, second, gate, chosen = (tiles[n] for n in names)
        order = self.const("order")

        wait(PE, *ht_ready)
        for t in range(TT):
            for k in range(KD):
                mm = PE.matmul(ps[:, 7, t * NE:(t + 1) * NE], self.h32[:, k, t * P:(t + 1) * P],
                               self.param("router", k * NE, NE), start=k == 0, stop=k == KD - 1)
        routed = pe(mm)
        turned = []
        for t in range(TT):
            for half in range(2):
                b = 2 * t + half
                for c in range(4):
                    mm = PE.transpose(ps[:, b, c * P:(c + 1) * P], self.h32[:, 4 * half + c, t * P:(t + 1) * P], self.const("ident"))
                turned.append(pe(mm))
        wait(DVE, routed)
        last = dve(DVE.tensor_copy(logit[:, :, :], ps[:, 7, 0:TT * NE].rearrange("p (t e) -> p t e", t=TT)))

        def pick(values, out, top, mark):
            nonlocal last
            for t in range(TT):
                wait(DVE, last)
                last = dve(DVE.tensor_reduce(top(t), values[:, t, :], AX.X, ALU.max))
                wait(DVE, last)
                last = dve(DVE.scalar_tensor_tensor(score[:, t, :], values[:, t, :], top(t), order, ALU.is_equal, ALU.mult))
                wait(DVE, last)
                last = dve(DVE.tensor_reduce(mark(t), score[:, t, :], AX.X, ALU.max))
                wait(DVE, last)
                last = dve(DVE.tensor_scalar(out[:, t, :], score[:, t, :], mark(t), None, ALU.is_equal))
        c1 = lambda base: (lambda t: col[:, base + t:base + t + 1])
        pick(logit, first, c1(0), c1(4))
        wait(DVE, last)
        last = dve(DVE.scalar_tensor_tensor(rest[:, :, :], first[:, :, :], NEG, logit[:, :, :], ALU.mult, ALU.add))
        pick(rest, second, c1(2), c1(4))
        wait(DVE, last)
        last = dve(DVE.tensor_tensor(col[:, 6:8], col[:, 2:4], col[:, 0:2], ALU.subtract))
        wait(ACT_, last)
        e = act(ACT_.activation(col[:, 8:10], col[:, 6:8], ACT.Exp))
        wait(DVE, e)
        last = dve(DVE.tensor_scalar(col[:, 10:12], col[:, 8:10], 1.0, None, ALU.add))
        wait(DVE, last)
        last = dve(DVE.reciprocal(col[:, 12:14], col[:, 10:12]))
        wait(DVE, last)
        last = dve(DVE.tensor_tensor(col[:, 14:16], col[:, 8:10], col[:, 12:14], ALU.mult))
        picked = dve(DVE.tensor_tensor(chosen[:, :, :], first[:, :, :], second[:, :, :], ALU.add))
        wait(DVE, last)
        for t in range(TT):
            last = dve(DVE.tensor_scalar(gate[:, t, :], first[:, t, :], col[:, 12 + t:13 + t], None, ALU.mult))
        dve(DVE.memset(self.gates[:, :, NE:NE + 1], 0.0))
        cleared = dve(DVE.memset(self.places[:, :, NE:NE + 1], -1.0))
        wait(DVE, last)
        for t in range(TT):
            last = dve(DVE.scalar_tensor_tensor(self.gates[:, t, 0:NE], second[:, t, :], col[:, 14 + t:15 + t], gate[:, t, :], ALU.mult, ALU.add))
        wait(PE, picked)
        PE.matmul(ps[:, 6, 0:NE], self.const("before"), chosen[:, 0, :], start=True, stop=True)
        PE.matmul(ps[:, 6, NE:2 * NE], self.const("ones"), chosen[:, 0, :], start=True, stop=False)
        PE.matmul(ps[:, 6, NE:2 * NE], self.const("before"), chosen[:, 1, :], start=False, stop=True)
        PE.matmul(ps[:, 6, 2 * NE:3 * NE], self.const("ones"), chosen[:, 0, :], start=True, stop=False)
        counted = pe(PE.matmul(ps[:, 6, 2 * NE:3 * NE], self.const("ones"), chosen[:, 1, :], start=False, stop=True))
        wait(DVE, counted)
        a = dve(DVE.scalar_tensor_tensor(self.places[:, :, 0:NE], ps[:, 6, 0:2 * NE].rearrange("p (t e) -> p t e", t=TT),
                                         1.0, chosen[:, :, :], ALU.add, ALU.mult))
        wait(DVE, a)
        placed = dve(DVE.tensor_scalar(self.places[:, :, 0:NE], self.places[:, :, 0:NE], -1.0, None, ALU.add))
        a = dve(DVE.tensor_reduce(self.total[:, 0:1], ps[:, 6, 2 * NE:3 * NE], AX.X, ALU.max))
        wait(DVE, a)
        most = dve(DVE.tensor_copy(self.most[:, :], self.total[:, 0:1]))
        for t in range(TT):
            for half in range(2):
                b = 2 * t + half
                c = slice(4 * P * half, 4 * P * half + 4 * P)
                rows = self.split_from(rows_hi[:, t, c], rows_lo[:, t, c], ps[:, b, :], turned[b])
        return [placed, last, rows, most, cleared]

    def experts(self, w_gate, w_up, w_down, slot0, routed, tag):
        ps, PE, ACT_, DVE, pe, act, dve = self.ps, self.PE, self.ACT, self.DVE, self.pe, self.act, self.dve
        at = self.ra
        def buf(name, shape, dtype=F32):
            nonlocal at
            t = self.place(name + tag, shape, dtype, at=at)
            at += -(-int(np.prod(shape[1:])) * 4 // 32) * 32
            return t
        xg_hi, xg_lo = buf("xg_hi", [P, KD, P], F32R), buf("xg_lo", [P, KD, P], F32R)
        pick = buf("pick", [P, TT, P], F32R)
        pick_t = buf("pick_t", [P, S], F32R)
        y_hi, y_lo = buf("y_hi_", [P, D], F32R), buf("y_lo_", [P, D], F32R)
        silu, whole = buf("silu_", [P, 4 * P]), buf("act_", [P, 4 * P])
        a_parts = [(buf(f"a_hi{i}_", [P, 4, P], F32R), buf(f"a_lo{i}_", [P, 4, P], F32R))
                   for i in range(2)]
        columns = buf("expert_columns", [P, 8])
        slot_gate = buf("slot_gate", [P, 1])
        gate_w = w_gate.rearrange("a e (k p) n -> p (a e k) n", p=P)
        up_w = w_up.rearrange("a e (k p) n -> p (a e k) n", p=P)
        down_w = w_down.rearrange("a e (k p) n -> p (a e k) n", p=P)
        slots = self.consts[:, CONSTS["slot"][0] + slot0:CONSTS["slot"][0] + slot0 + P]
        tiles = FE // (4 * P)
        HC = FE // P

        def build_pick(e, free):
            wait(DVE, *free, dve.ahead(0))
            a = dve(DVE.tensor_copy(columns[:, 0:TT], self.places[:, :, bass.ds(e, 1)].rearrange("p t e -> p (t e)")))
            wait(DVE, a)
            for t in range(TT):
                p = dve(DVE.tensor_scalar(pick[:, t, :], slots, columns[:, t:t + 1], None, ALU.is_equal))
            return p

        def gather(pick_ready, banks_free):
            wait(PE, pick_ready, *banks_free)
            for f in range(KD):
                out = ps[:, 6 + f // 4, f % 4 * P:(f % 4 + 1) * P]
                n = 0
                for t in range(TT):
                    for part in (self.rows_hi, self.rows_lo):
                        mm = PE.matmul(out, part[:, t, f * P:(f + 1) * P], pick[:, t, :], start=n == 0, stop=n == 3)
                        n += 1
            return pe(mm)

        def split_gathered(done):
            flat = lambda a: a[:, :, :].rearrange("p k s -> p (k s)")
            return self.split_from(flat(xg_hi), flat(xg_lo), ps[:, 6:8, :].rearrange("p b n -> p (b n)"), done,
                                   free=[self.slab_used.ahead(0)])

        def hidden(weight, e, f, half, bank):
            def products(hi, lo):
                for k in range(4):
                    kk = 4 * half + k
                    PE.matmul(ps[:, bank, :], xg_hi[:, kk, :], hi[:, k, :], start=kk == 0, stop=False)
                    PE.matmul(ps[:, bank, :], xg_hi[:, kk, :], lo[:, k, :], start=False, stop=False)
                    mm = PE.matmul(ps[:, bank, :], xg_lo[:, kk, :], hi[:, k, :], start=False, stop=kk == KD - 1)
                return mm
            return weight[:, bass.ds(e * KD + 4 * half, 4), bass.ds(f * (4 * P), 4 * P)], products

        def gate_tile(e, f):
            wait(PE, act.ahead(0))
            for half in range(2):
                self.slab_step(*hidden(gate_w, e, f, half, 0))

        def silu_tile():
            wait(ACT_, self.slab_used.ahead(0), dve.ahead(0))
            return act(ACT_.activation(silu[:, :], ps[:, 0, :], ACT.Silu))

        def up_tile(e, f):
            for half in range(2):
                self.slab_step(*hidden(up_w, e, f, half, 1))

        def act_tile(s):
            wait(DVE, self.slab_used.ahead(0), s, pe.ahead(0))
            return dve(DVE.tensor_tensor(whole[:, :], silu[:, :], ps[:, 1, :], ALU.mult))

        def turn_tile(whole_ready, bank_free):
            wait(PE, whole_ready, *bank_free)
            for c in range(4):
                mm = PE.transpose(ps[:, 2, c * P:(c + 1) * P], whole[:, c * P:(c + 1) * P], self.const("ident"))
            return pe(mm)

        def split_tile(turned, which=0):
            flat = lambda a: a[:, :, :].rearrange("p k s -> p (k s)")
            return self.split_from(flat(a_parts[which][0]), flat(a_parts[which][1]), ps[:, 2, :], turned)

        def down_tile(e, f, a_ready, which=0, halves=range(2)):
            a_hi, a_lo = a_parts[which]
            wait(PE, a_ready)
            for j in halves:
                def products(hi, lo):
                    for k in range(2):
                        for n in range(2):
                            out = ps[:, 4 + n, :]
                            w = slice(n * 512, (n + 1) * 512)
                            PE.matmul(out, a_hi[:, 2 * j + k, :], hi[:, k, w], start=False, stop=False, skip_group_check=True)
                            PE.matmul(out, a_hi[:, 2 * j + k, :], lo[:, k, w], start=False, stop=False, skip_group_check=True)
                            mm = PE.matmul(out, a_lo[:, 2 * j + k, :], hi[:, k, w], start=False, stop=False, skip_group_check=True)
                    return mm
                self.slab_step(down_w[:, bass.ds(e * HC + f * 4 + 2 * j, 2), :], products)

        def give_back(free):
            wait(PE, *free)
            banks = (2, 3, 6, 7)
            adds = []
            for f in range(KD):
                out = ps[:, banks[f // 2], f % 2 * S:(f % 2 + 1) * S]
                PE.matmul(out, y_hi[:, f * P:(f + 1) * P], pick_t[:, :], start=True, stop=False)
                mm = PE.matmul(out, y_lo[:, f * P:(f + 1) * P], pick_t[:, :], start=False, stop=True)
                if f % 2:
                    done = pe(mm)
                    wait(DVE, done)
                    c = slice(f - 1, f + 1)
                    adds.append(dve(DVE.tensor_tensor(self.xt[:, c, :], ps[:, banks[f // 2], :].rearrange("p (c s) -> p c s", c=2),
                                                      self.xt[:, c, :], ALU.add)))
            return adds

        wait(DVE, *routed)
        dve(DVE.memset(y_hi[:, :].bitcast(F32), 0.0))
        dve(DVE.memset(y_lo[:, :].bitcast(F32), 0.0))
        y_ready = dve(DVE.memset(pick_t[:, :].bitcast(F32), 0.0))
        xg_ready = split_gathered(gather(build_pick(0, []), routed))
        wait(PE, xg_ready, y_ready)

        def expert(e):
            last_split = [dve.ahead(0), act.ahead(0)]
            gate_tile(e, 0)
            s = silu_tile()
            adds = give_back(last_split)
            up_tile(e, 0)
            g = dve(DVE.tensor_copy(columns[:, 4:4 + TT], self.gates[:, :, bass.ds(e, 1)].rearrange("p t e -> p (t e)")))
            wait(PE, g, adds[1])
            for t in range(TT):
                PE.transpose(ps[:, 3, t * P:(t + 1) * P], pick[:, t, :].bitcast(F32), self.const("ident"))
            for t in range(TT):
                mm = PE.matmul(ps[:, 3, S:S + 1], pick[:, t, :].bitcast(F32), columns[:, 4 + t:5 + t], start=t == 0, stop=t == TT - 1)
            picked = pe(mm)
            wait(ACT_, picked)
            act(ACT_.activation(pick_t[:, :], ps[:, 3, 0:S], ACT.Copy))
            slot_ready = act(ACT_.activation(slot_gate[:, :], ps[:, 3, S:S + 1], ACT.Copy))
            act_tile(s)
            next_pick = build_pick(e + 1, [picked])
            wait(PE, adds[0])
            self.clear_banks((4, 5))

            def tile(turn):
                f = turn + 1
                gate_tile(e, f)
                s = silu_tile()
                turned = turn_tile(dve.ahead(0), [])
                a_ready = split_tile(turned)
                up_tile(e, f)
                act_tile(s)
                down_tile(e, f - 1, a_ready)
            self.loop(tiles - 2, {act: 2, dve: 2, pe: 1}, tile, slabs=NRAW)

            gate_tile(e, tiles - 1)
            s = silu_tile()
            a_ready = split_tile(turn_tile(dve.ahead(0), []))
            gathered = gather(next_pick, adds)
            up_tile(e, tiles - 1)
            whole_ready = act_tile(s)
            xg_ready = split_gathered(gathered)
            down_tile(e, tiles - 2, a_ready, halves=[0])
            last_ready = split_tile(turn_tile(whole_ready, [a_ready]), 1)
            down_tile(e, tiles - 2, a_ready, halves=[1])
            down_tile(e, tiles - 1, last_ready, 1)
            wait(ACT_, self.slab_used.ahead(0), slot_ready)
            both = ps[:, 4:6, :].rearrange("p b n -> p (b n)")
            high = act(ACT_.activation(y_hi[:, :], both, ACT.Copy, scale=slot_gate[:, :]))
            wait(DVE, high)
            y_ready = dve(DVE.scalar_tensor_tensor(y_lo[:, :], both, slot_gate[:, :], y_hi[:, :].bitcast(F32), ALU.mult, ALU.subtract))
            wait(PE, xg_ready)
        self.loop(NE, {act: 18, dve: 24, pe: 13}, expert, slabs=6 * tiles)
        last_split = [dve.ahead(0), act.ahead(0)]
        self.close_stream(gate_w)
        return give_back(last_split)


def build(nc, x, packed, lasting, staged, w_in, w_branch, w_o, w_gate_up, w_down, ret_w_in, ret_w_out,
          dense_gate, dense_up, dense_down, fnet_w, moe_gate, moe_up, moe_down, out, until=None, force=False):
    with ExitStack() as ctx:
        k = Kernel(nc, ctx)
        k.allocate()
        k.x_sem = ctx.enter_context(nc.semaphore("x_landed"))
        stored = ctx.enter_context(nc.semaphore("stored"))
        first_loads = []

        for tile, source in ((k.consts, lasting), (k.params, packed), (k.stage, staged[0, :, :])):
            landed = Count(ctx.enter_context(nc.semaphore(f"landed_{tile.name}")), 16)
            k.ACT.dma_start(tile[:, :], source).then_inc(landed.sem, 16)
            first_loads.append(landed)
        consts_ready, params_ready, stage_ready = first_loads
        zeroed = k.dve(k.DVE.memset(k.zero[:, :], 0.0))
        wait(k.PE, zeroed)
        wait(k.ACT, k.dve(k.DVE.memset(k.eps[:, :], EPS)))

        wait(k.PE, consts_ready)
        wait(k.DVE, consts_ready)
        x_ready = k.load_input(x)
        k.open_stream()
        for engine in (k.ACT, k.DVE, k.PE):
            wait(engine, params_ready)
        ht = k.norm("norm1", x_ready, [])
        u_ready = k.project_inputs(w_in, ht)
        for engine in (k.ACT, k.DVE):
            wait(engine, stage_ready)
        y_ready = k.mixers(u_ready)
        wait(k.POOL, *y_ready)
        stage_ready = k.load(k.stage[:, :], staged[1, :, :])
        m_hi, m_lo, merged = k.merge(w_branch, w_in, y_ready)
        x_ready = k.into_residual(w_o, lambda c: m_hi[:, c, :], lambda c: m_lo[:, c, :], KD, merged)
        if until == "mix":
            k.close_stream(k.rows(w_o, 0))
            return finish(k, x_ready, None, out, stored)
        ht = k.norm("norm2", x_ready, [])
        x_ready = k.feed_forward(
            "1", lambda j: k.columns(w_gate_up, j * (2 * P)), lambda j: k.columns(w_gate_up, j * (2 * P) + FF),
            w_down, ht, x_ready)
        x_ready = k.norm_in_place("final1", x_ready)
        if until == "first":
            k.close_stream(k.rows(w_o, 0))
            return finish(k, x_ready, None, out, stored)

        ht = k.norm("mix0", x_ready, [])
        x_ready = k.retention(ret_w_in, ret_w_out, ht, x_ready, stage_ready)
        wait(k.POOL, *x_ready)
        stage_ready = k.load(k.stage[:, :], staged[2, :, :])
        if until == "ret":
            k.close_stream(k.rows(w_o, 0))
            return finish(k, x_ready, None, out, stored)
        ht = k.norm("ffn0", x_ready, [])
        x_ready = k.feed_forward(
            "2", lambda j: k.columns(dense_gate, j * (2 * P)), lambda j: k.columns(dense_up, j * (2 * P)),
            dense_down, ht, x_ready)

        ht = k.norm("mix1", x_ready, [])
        x_ready = k.fourier(fnet_w, ht, stage_ready)
        if until == "four":
            k.close_stream(k.rows(w_o, 0))
            return finish(k, x_ready, None, out, stored)
        ht = k.norm("ffn1", x_ready, [])
        routed = k.route(ht)
        x_ready = k.experts(moe_gate, moe_up, moe_down, 0, routed, "")
        for engine in (k.SP, k.POOL, k.ACT, k.DVE, k.PE):
            wait(engine, *x_ready)
        most = nc.values_load(k.most[0:1, 0:1], min_val=0, max_val=S)
        with nc.If(most > (P if not force else 1)):
            k.open_stream()
            extra = k.experts(moe_gate, moe_up, moe_down, P, routed, "_more")
            for engine in (k.SP, k.POOL, k.ACT, k.DVE, k.PE):
                wait(engine, *extra)
        k.fresh_counters("_final")
        finish(k, [], "final2", out, stored)


def finish(k, x_ready, gain, out, stored):
    if gain:
        x_ready = k.norm_in_place(gain, x_ready)
    rows = k.place("out_rows", [P, TT, D], at=k.ra)
    wait(k.PE, *x_ready)
    wait(k.ACT, *x_ready)
    for t in range(TT):
        copied = []
        for half in range(2):
            b = 2 * t + half
            for c in range(4):
                mm = k.PE.transpose(k.ps[:, b, c * P:(c + 1) * P], k.xt[:, 4 * half + c, t * P:(t + 1) * P], k.const("ident"))
            turned = k.pe(mm)
            wait(k.ACT, turned)
            copied.append(k.act(k.ACT.activation(rows[:, t, 4 * P * half:4 * P * (half + 1)], k.ps[:, b, :], ACT.Copy)))
        wait(k.SP, *copied)
        k.SP.dma_start(out[0, t * P:(t + 1) * P, :], rows[:, t, :]).then_inc(stored, 16)
    k.SP.wait_ge(stored, 16 * TT)


_WEIGHTS = ["w_in", "w_branch", "w_o", "w_gate_up", "w_down", "ret_w_in_2", "ret_w_out_2", "dense_w_gate_2",
            "dense_w_up_2", "dense_w_down_2", "fnet_w_out_2", "moe_w_gate_2", "moe_w_up_2", "moe_w_down_2"]


def pack_parameters(v):
    def chunks(a):
        return np.ascontiguousarray(a).reshape(-1, P).T

    def everywhere(a):
        return np.broadcast_to(np.ascontiguousarray(a).reshape(1, -1), (P, a.size))

    def per_head(a):
        return np.repeat(a, HD).reshape(2, P).T

    taps = lambda w: w.reshape(w.shape[-2], -1, P).transpose(2, 1, 0).reshape(P, -1)
    rows = lambda w: w.reshape(KD, P, -1).transpose(1, 0, 2).reshape(P, -1)
    twice = lambda a: np.concatenate([a.reshape(-1), a.reshape(-1)])
    parts = dict(
        norm1=chunks(v["norm1_g"]), norm2=chunks(v["norm2_g"]), mix0=chunks(v["mix_norm_2"][0]),
        mix1=chunks(v["mix_norm_2"][1]), ffn0=chunks(v["ffn_norm_2"][0]), ffn1=chunks(v["ffn_norm_2"][1]),
        final1=chunks(v["final_g"]), final2=chunks(v["final_norm_2"]),
        ssm_taps=taps(v["ssm_conv_w"]), a_taps=taps(v["conv_a_w"]), ssm_bias=chunks(v["ssm_conv_b"]),
        dt_bias=everywhere(twice(v["ssm_dt_bias"])), a_log=everywhere(twice(v["ssm_a_log"])),
        skip=per_head(v["ssm_d"].reshape(-1)), ssm_norm=chunks(v["ssm_norm_g"]), gn_gain=chunks(v["ret_gn_gain_2"]),
        decay=everywhere(v["ret_decay_logit_2"]), w_dt=rows(v["w_in"][0, :, COL_DT:COL_DT + NH]),
        router=rows(v["moe_router_2"][0]))
    return np.ascontiguousarray(np.concatenate([parts[name] for name in PARAMS], 1))


def kernel(**inputs):
    import concourse.bacc as _bacc
    from concourse.bass_utils import run_bass_kernel_spmd as _run

    v = {name: np.asarray(a) for name, a in inputs.items()}
    nc = _bacc.Bacc("TRN2", target_bir_lowering=False, num_devices=1)
    lasting, staged = host_constants()
    arrays = {"x": v["x"], "params": pack_parameters(v), "lasting": lasting, "staged": staged}
    arrays.update({name: v[name] for name in _WEIGHTS})
    arrays = {f"in_{name}": np.ascontiguousarray(a) for name, a in arrays.items()}
    args = []
    for name, a in arrays.items():
        t = nc.dram_tensor(name, a.shape, mybir.dt.from_np(a.dtype), kind="ExternalInput").ap()
        short = name[3:]
        if short in ("w_in", "w_o", "w_gate_up", "w_down", "ret_w_in_2", "ret_w_out_2", "dense_w_gate_2",
                     "dense_w_up_2", "dense_w_down_2", "fnet_w_out_2"):
            t = t.rearrange("a k n -> (a k) n")
        args.append(t)
    args.append(nc.dram_tensor("out", (1, S, D), F32, kind="ExternalOutput").ap())
    build(nc, *args)
    r = _run(nc, [arrays], core_ids=[0])
    return r.results[0]["out"]
```

```python
from contextlib import ExitStack

import numpy as np

import concourse.bass as bass
from concourse import mybir

F32 = mybir.dt.float32
F32R = mybir.dt.float32r
BF16 = mybir.dt.bfloat16
I32 = mybir.dt.int32
ACT = mybir.ActivationFunctionType
ALU = mybir.AluOpType
AX = mybir.AxisListType

P = 128
S = 256
TT = S // P
D = 1024
KD = D // P
NH = 4
HD = 64
BW = 256
FF = 2816
NE = 8
FE = 3584
EPS = 1e-6
NEG = -1e30

COL_A, COL_B, COL_Z, COL_XBC, COL_DT = 0, 768, 1536, 1792, 2304
COL_D, COL_G = 2308, 3076

SLAB = 2048
NRAW = 6
NSPLIT = 3
LEAD = 2
START = 8

PARAMS = {}
_at = 0
for _name, _n in [("norm1", KD), ("norm2", KD), ("mix0", KD), ("mix1", KD), ("ffn0", KD), ("ffn1", KD),
                  ("final1", KD), ("final2", KD), ("ssm_taps", 16), ("a_taps", 6), ("ssm_bias", 4),
                  ("dt_bias", 8), ("a_log", 8), ("skip", 2), ("ssm_norm", 2), ("gn_gain", 16),
                  ("decay", 8), ("w_dt", KD * NH), ("router", KD * NE)]:
    PARAMS[_name] = (_at, _n)
    _at += _n
NPARAM = _at

CONSTS = {}
_at = 0
for _name, _n in [("ident", P), ("suffix", P), ("prefix", P), ("ones", P), ("before", P),
                  ("slot", 2 * P), ("order", NE)]:
    CONSTS[_name] = (_at, _n)
    _at += _n
NCONST = _at
NSTAGE = 1536


def host_constants():
    f = np.float32
    p = np.arange(P)[:, None]
    q = np.arange(P)[None, :]
    s = np.arange(S)[None, :]
    lasting = [np.eye(P), p >= q, p <= q, np.ones((P, P)), p < q,
               np.broadcast_to(s, (P, S)), np.broadcast_to(NE - np.arange(NE)[None, :], (P, NE))]
    lasting = np.concatenate([a.astype(f) for a in lasting], 1)
    strict = np.concatenate([np.where(p < s, 0, NEG), np.where(p < q, 0, NEG)], 1)
    causal = np.concatenate([np.where(q <= p, 0, NEG), np.where(s <= p + P, 0, NEG)], 1)
    ssm = np.concatenate([np.where(s >= p, 0, NEG), np.where(q >= p, 0, NEG)], 1)
    one = np.concatenate([strict, causal, ssm, np.zeros((P, NSTAGE - 1152))], 1).astype(f)
    inv = np.power(f(10000.0), -np.arange(P, dtype=f) / f(P)).astype(f)
    ang = (np.arange(S, dtype=f)[None, :] * inv[:, None]).astype(f).astype(np.float64)
    dist = np.concatenate([s - p, s - p - P], 1)
    two = np.concatenate([np.cos(ang), np.sin(ang), np.maximum(dist, 0), np.maximum(-dist, 0)], 1).astype(f)
    w = 2 * np.pi * ((np.arange(S)[:, None] * np.arange(S)[None, :]) % S) / S
    cs = np.concatenate([np.cos(w), np.sin(w)], 1).reshape(2, P, 2 * S).transpose(1, 0, 2).reshape(P, -1) / 16
    ns = (-np.sin(w)).reshape(2, P, S).transpose(1, 0, 2).reshape(P, -1) / 16
    three = np.concatenate([cs, ns], 1).astype(f)
    return lasting, np.stack([one, two, three])


class Loop:

    def __init__(self, trips):
        self.trips, self.turn = trips, None


class Count:

    def __init__(self, sem, const, steps=()):
        self.sem, self.const, self.steps = sem, const, tuple(steps)

    def value(self):
        out = self.const
        for loop, step in self.steps:
            out = out + (loop.turn if loop.turn is not None else loop.trips - 1) * step
        return out


class Done:

    def __init__(self, nc, ctx, name, engine, step=1):
        self.sem, self.step, self.n, self.steps = ctx.enter_context(nc.semaphore(name)), step, START, []
        engine.sem_inc(self.sem, START)

    def __call__(self, instruction):
        instruction.then_inc(self.sem, self.step)
        self.n += self.step
        return Count(self.sem, self.n, self.steps)

    def ahead(self, k):
        return Count(self.sem, self.n + k * self.step, self.steps)


def wait(engine, *counts):
    last = {}
    for c in counts:
        known = last.get(id(c.sem))
        if known is None:
            last[id(c.sem)] = c
        elif known.steps == c.steps:
            last[id(c.sem)] = c if c.const > known.const else known
        else:
            engine.wait_ge(c.sem, c.value())
    for c in last.values():
        engine.wait_ge(c.sem, c.value())


def stationary_pair(pe, out, w_hi, w_lo, x_hi, x_lo, start, stop, **kw):
    pe.matmul(out, w_hi, x_hi, start=start, stop=False, **kw)
    pe.matmul(out, w_hi, x_lo, start=False, stop=False, **kw)
    return pe.matmul(out, w_lo, x_hi, start=False, stop=stop, **kw)


class Kernel:
    def __init__(self, nc, ctx):
        self.nc, self.ctx = nc, ctx
        self.PE, self.ACT, self.DVE, self.POOL, self.SP = nc.tensor, nc.scalar, nc.vector, nc.gpsimd, nc.sync
        self.at = 16512

    def place(self, name, shape, dtype=F32, at=None):
        size = int(np.prod(shape[1:])) * mybir.dt.size(dtype)
        if at is None:
            at = self.at
            self.at += -(-size // 32) * 32
        return self.nc.alloc_sbuf_tensor_at(name, shape, dtype, offset=at)

    def region(self, size):
        at = self.at
        self.at += size
        return at

    def fresh_counters(self, tag):
        c, nc = self.ctx, self.nc
        self.pe = Done(nc, c, f"pe_done{tag}", self.PE)
        self.act = Done(nc, c, f"act_done{tag}", self.ACT)
        self.dve = Done(nc, c, f"dve_done{tag}", self.DVE)

    def loop(self, trips, per, body, slabs=0):
        per = dict(per)
        counters = list(per)
        if slabs:
            for c in (self.split_hi, self.split_lo, self.slab_used):
                counters.append(c)
                per[c] = slabs
        loop = Loop(trips)
        starts = {c: c.n for c in counters}
        others = {c: c.n for c in self.all_counters() if c not in per}
        for c in counters:
            c.steps.append((loop, per[c] * c.step))
        slab0 = self.slab
        if slabs:
            assert slabs % NRAW == 0 and slabs % NSPLIT == 0
            self.slab_steps.append((loop, slabs))
        with self.nc.Fori(0, trips) as turn:
            loop.turn = turn
            body(turn)
        loop.turn = None
        for c in counters:
            assert c.n - starts[c] == per[c] * c.step, (c.sem, c.n - starts[c], per[c] * c.step)
            c.steps.pop()
            c.n = starts[c] + per[c] * c.step * trips
        for c, n in others.items():
            assert c.n == n, ("not declared", c.sem)
        assert self.slab - slab0 == slabs
        if slabs:
            self.slab_steps.pop()
            self.slab = slab0 + slabs * trips

    def all_counters(self):
        return [self.pe, self.act, self.dve, self.split_hi, self.split_lo, self.slab_used]

    def raw_landed(self, ahead):
        n = self.slab + ahead
        return Count(self.raw_sems[n % NRAW], 16 * (n // NRAW + 1),
                     [(l, 16 * k // NRAW) for l, k in self.slab_steps])

    def split(self, ahead):
        n = self.slab + ahead
        raw, hi, lo = self.raw[:, n % NRAW, :], self.w_hi[:, n % NSPLIT, :], self.w_lo[:, n % NSPLIT, :]
        wait(self.ACT, self.raw_landed(ahead),
             self.slab_used.ahead(ahead - NSPLIT + 1))
        hi_ready = self.split_hi(self.ACT.activation(hi, raw, ACT.Copy))
        wait(self.DVE, hi_ready)
        self.split_lo(self.DVE.tensor_tensor(lo, raw, hi.bitcast(F32), ALU.subtract))

    def slab_step(self, source, products):
        n = self.slab
        if n >= NRAW or self.slab_steps:
            wait(self.SP, self.split_lo.ahead(1 - self.split_ahead - NRAW))
        k = source.shape[1]
        self.SP.dma_start(self.raw[:, n % NRAW, :].rearrange("p (k n) -> p k n", k=k), source)\
            .then_inc(self.raw_sems[n % NRAW], 16)
        self.split(LEAD)
        wait(self.PE, self.split_lo.ahead(-self.split_ahead))
        hi = self.w_hi[:, n % NSPLIT, :].rearrange("p (k n) -> p k n", k=k)
        lo = self.w_lo[:, n % NSPLIT, :].rearrange("p (k n) -> p k n", k=k)
        self.slab_used(products(hi, lo))
        self.slab += 1

    def open_stream(self):
        for ahead in range(LEAD):
            self.split(ahead)
        self.split_ahead = LEAD

    def close_stream(self, source):
        for ahead in range(LEAD):
            wait(self.SP, self.split_lo.ahead(1 - LEAD - NRAW + ahead))
            slot = (self.slab + ahead) % NRAW
            self.SP.dma_start(self.raw[:, slot:slot + 1, 0:P], source[:, 0:1, 0:P]).then_inc(self.raw_sems[slot], 16)
        wait(self.PE, self.split_lo.ahead(0))
        self.PE.drain().then_inc(self.slab_used.sem, LEAD)
        self.slab_used.n += LEAD
        self.slab += LEAD
        self.split_ahead = 0

    def allocate(self):
        nc, ctx, place = self.nc, self.ctx, self.place
        self.raw = place("raw", [P, NRAW, SLAB])
        self.w_hi = place("w_hi", [P, NSPLIT, SLAB], F32R)
        self.w_lo = place("w_lo", [P, NSPLIT, SLAB], F32R)
        self.xt = place("xt", [P, KD, S])
        self.ht_hi = place("ht_hi", [P, KD, S], F32R)
        self.ht_lo = place("ht_lo", [P, KD, S], F32R)
        self.params = place("params", [P, NPARAM])
        self.consts = place("consts", [P, NCONST])
        self.stage = place("stage", [P, NSTAGE])
        self.small = place("small", [P, 96])
        self.zero = place("zero", [P, P], BF16)
        self.eps = place("eps", [P, 1])
        self.junk = place("junk", [P, 1])
        self.root = place("root", [P, TT])
        self.ra = self.region(24 * 2 * S * 4)
        self.rb = self.region(2 * KD * S * 4)
        self.rc = self.region(8256)
        self.rd = self.region(4160)
        self.sq = place("sq", [P, KD, S], at=self.rc)
        self.h32 = place("h32", [P, KD, S], at=self.rc)
        self.spread = place("spread", [P, TT, P], at=self.rd)
        self.ps = ctx.enter_context(nc.psum_tensor("ps", [P, 8, 512], F32))
        self.rstd = self.ps[:, 7, S:2 * S]
        self.split_hi = Done(nc, ctx, "split_hi_done", self.ACT)
        self.split_lo = Done(nc, ctx, "split_lo_done", self.DVE)
        self.slab_used = Done(nc, ctx, "slab_used", self.PE)
        self.raw_sems = [ctx.enter_context(nc.semaphore(f"raw_landed{i}")) for i in range(NRAW)]
        self.slab, self.slab_steps, self.split_ahead = 0, [], 0
        self.fresh_counters("")
        self.load_sem = ctx.enter_context(nc.semaphore("small_loads"))
        self.loads = 0

    def load(self, out, source):
        self.POOL.dma_start(out, source).then_inc(self.load_sem, 16)
        self.loads += 16
        c = Count(self.load_sem, self.loads)
        wait(self.POOL, c)
        return c

    def param(self, name, i=0, n=1):
        at, _ = PARAMS[name]
        return self.params[:, at + i:at + i + n]

    def const(self, name, n=None):
        at, width = CONSTS[name]
        return self.consts[:, at:at + (n or width)]

    def ready_table(self, func):
        self.ACT.activation(self.junk[:, :], self.eps[:, :], func)

    def norm_factor(self, x_ready):
        nc, ps = self.nc, self.ps[:, 7, :]
        squares = []
        for k in range(0, KD, 2):
            wait(self.ACT, *(x_ready[k // 2:k // 2 + 1] if len(x_ready) == KD // 2 else x_ready[k + 1:k + 2]))
            squares.append(self.act(self.ACT.activation(self.sq[:, k:k + 2, :], self.xt[:, k:k + 2, :], ACT.Square)))
        if len(x_ready) == KD:
            wait(self.PE, x_ready[-1])
        for t in range(TT):
            for k in range(KD):
                wait(self.PE, squares[k // 2])
                mm = self.PE.matmul(ps[:, t:t + 1], self.sq[:, k, t * P:(t + 1) * P], self.const("ones", 1),
                                    start=k == 0, stop=k == KD - 1)
        summed = self.pe(mm)
        wait(self.ACT, summed)
        root = self.act(self.ACT.activation(self.root[:, :], ps[:, 0:TT], ACT.Sqrt, scale=1.0 / D, bias=self.eps[:, :]))
        wait(self.DVE, root)
        inverse = self.dve(self.DVE.reciprocal(self.root[:, :], self.root[:, :]))
        wait(self.DVE, inverse)
        for t in range(TT):
            spread = self.dve(self.DVE.tensor_scalar(self.spread[:, t, :], self.const("ones"), self.root[:, t:t + 1], None, ALU.mult))
        wait(self.PE, spread)
        for t in range(TT):
            mm = self.PE.matmul(ps[:, S + t * P:S + (t + 1) * P], self.spread[:, t, :], self.const("ident"), start=True, stop=True)
        return self.pe(mm)

    def norm(self, gain, x_ready, ht_free, row_major=False):
        wait(self.DVE, self.norm_factor(x_ready))
        highs, ready, self.h32_ready = [], [], []

        def low_part(k):
            wait(self.DVE, highs[k // 2])
            ready.append(self.dve(self.DVE.tensor_tensor(
                self.ht_lo[:, k:k + 2, :], self.h32[:, k:k + 2, :], self.ht_hi[:, k:k + 2, :].bitcast(F32), ALU.subtract)))
        for k in range(0, KD, 2):
            for c in (k, k + 1):
                whole = self.dve(self.DVE.scalar_tensor_tensor(
                    self.h32[:, c, :], self.xt[:, c, :], self.param(gain, c), self.rstd, ALU.mult, ALU.mult))
                self.h32_ready.append(whole)
            wait(self.ACT, whole, *ht_free)
            highs.append(self.act(self.ACT.activation(self.ht_hi[:, k:k + 2, :], self.h32[:, k:k + 2, :], ACT.Copy)))
            if k:
                low_part(k - 2)
        low_part(KD - 2)
        return ready

    def split_from(self, hi, lo, source, source_ready, free=()):
        wait(self.ACT, source_ready, *free)
        high = self.act(self.ACT.activation(hi, source, ACT.Copy))
        wait(self.DVE, high)
        return self.dve(self.DVE.tensor_tensor(lo, source, hi.bitcast(F32), ALU.subtract))

    def columns(self, weight, start, n=2 * P):
        return weight.rearrange("(k p) n -> p k n", p=P)[:, :, bass.ds(start, n)]

    def rows(self, weight, start):
        return weight.rearrange("(k p) n -> p k n", p=P)[:, bass.ds(start, 2), :]

    def feature_major(self, bank, ht_ready=()):
        def products(hi, lo):
            for c in range(2):
                for k in range(KD):
                    if c == 0 and k % 2 == 0 and ht_ready:
                        wait(self.PE, ht_ready[k // 2])
                    mm = stationary_pair(self.PE, self.ps[:, bank, c * S:(c + 1) * S],
                                         hi[:, k, c * P:(c + 1) * P], lo[:, k, c * P:(c + 1) * P],
                                         self.ht_hi[:, k, :], self.ht_lo[:, k, :], k == 0, k == KD - 1)
            return mm
        return products

    def clear_banks(self, banks):
        for b in banks:
            self.PE.matmul(self.ps[:, b, :].rearrange("p (a n) -> p a n", n=P), self.zero[:, :],
                           self.zero[:, :].unsqueeze(1).to_broadcast([P, 4, P]), start=True, stop=True)

    def into_residual(self, weight, y_hi, y_lo, chunks, banks_free, y_ready=()):
        wait(self.PE, *banks_free)
        self.clear_banks(range(4))
        def step(start, i):
            wait(self.PE, *y_ready[i:i + 1])
            def products(hi, lo):
                for k in range(2):
                    for f in range(KD):
                        mm = stationary_pair(
                            self.PE, self.ps[:, f // 2, f % 2 * S:(f % 2 + 1) * S],
                            hi[:, k, f * P:(f + 1) * P], lo[:, k, f * P:(f + 1) * P],
                            y_hi(start + k), y_lo(start + k), False, False, skip_group_check=True)
                return mm
            self.slab_step(self.rows(weight, start), products)
        steps = chunks // 2
        whole = steps // NRAW if steps >= 2 * NRAW else 0
        if whole:
            def body(turn):
                for j in range(NRAW):
                    step(turn * (2 * NRAW) + 2 * j, j)
            self.loop(whole, {}, body, slabs=NRAW)
        for i in range(whole * NRAW, steps):
            step(2 * i, i)
        done = self.slab_used.ahead(0)
        ready = []
        self.ready_table(ACT.Sqrt)
        for b in range(4):
            wait(self.DVE, done)
            ready.append(self.dve(self.DVE.tensor_tensor(
                self.xt[:, 2 * b:2 * b + 2, :], self.ps[:, b, :].rearrange("p (c s) -> p c s", c=2),
                self.xt[:, 2 * b:2 * b + 2, :], ALU.add)))
        return ready

    def load_input(self, x):
        rows = self.place("x_rows", [P, TT, D], at=self.ra)
        self.SP.dma_start(rows[:, :, :], x.rearrange("a (t p) d -> p (a t) d", p=P)).then_inc(self.x_sem, 16)
        landed = Count(self.x_sem, 16)
        ready = []
        wait(self.PE, landed)
        for k in range(0, KD, 2):
            for c in (k, k + 1):
                for t in range(TT):
                    mm = self.PE.transpose(self.ps[:, k // 2, (c - k) * S + t * P:(c - k) * S + (t + 1) * P],
                                           rows[:, t, c * P:(c + 1) * P], self.const("ident"))
            turned = self.pe(mm)
            wait(self.DVE, turned)
            ready.append(self.dve(self.DVE.tensor_copy(
                self.xt[:, k:k + 2, :], self.ps[:, k // 2, :].rearrange("p (c s) -> p c s", c=2))))
        return ready

    def project_inputs(self, w_in, ht_ready):
        self.u = u = self.place("u", [P, 24, S], at=self.ra)
        def body(turn):
            for j in range(NRAW):
                start = turn * (NRAW * BW + (COL_D - COL_DT if j >= 3 else 0)) + j * BW
                engine, done = (self.ACT, self.act) if j % 2 == 0 else (self.DVE, self.dve)
                wait(self.PE, done.ahead(1 - NRAW // 2))
                self.slab_step(self.columns(w_in, start), self.feature_major(j, ht_ready if j == 0 else ()))
                out = u[:, bass.ds(turn * 12 + 2 * j, 2), :]
                whole = self.ps[:, j, :].rearrange("p (c s) -> p c s", c=2)
                wait(engine, self.slab_used.ahead(0))
                done(engine.activation(out, whole, ACT.Copy) if j % 2 == 0 else engine.tensor_copy(out, whole))
        self.loop(2, {self.act: NRAW // 2, self.dve: NRAW // 2}, body, slabs=NRAW)
        return [self.act.ahead(0), self.dve.ahead(0)]

    def token_major(self, bank, chunks, out, ready, free=()):
        wait(self.PE, *ready, *free)
        for t in range(TT):
            for c in range(2):
                mm = self.PE.transpose(self.ps[:, bank, t * S + c * P:t * S + (c + 1) * P],
                                       self.u[:, chunks + c, t * P:(t + 1) * P], self.const("ident"))
        turned = self.pe(mm)
        wait(self.ACT, turned)
        return self.act(self.ACT.activation(out, self.ps[:, bank, :].rearrange("p (t f) -> p t f", t=TT), ACT.Copy))

    def softplus(self, out, x, x_ready, scratch):
        wait(self.ACT, x_ready)
        a = self.act(self.ACT.activation(scratch, x, ACT.Abs))
        wait(self.ACT, a)
        b = self.act(self.ACT.activation(scratch, scratch, ACT.Exp, scale=-1.0))
        wait(self.ACT, b)
        c = self.act(self.ACT.activation(scratch, scratch, ACT.Ln, bias=1.0))
        wait(self.DVE, c)
        return self.dve(self.DVE.scalar_tensor_tensor(out, x, 0.0, scratch, ALU.max, ALU.add))

    def wide(self, a, h, n=1):
        out = a[:, h * S:(h + n) * S]
        return out.rearrange("p (h s) -> p h s", h=n) if n > 1 else out

    def tail(self, a, h, n=1):
        out = a[:, NH * S + h * P:NH * S + (h + n) * P]
        return out.rearrange("p (h s) -> p h s", h=n) if n > 1 else out

    def banks(self, first, n=3):
        return self.ps[:, first:first + n, :].rearrange("p b n -> p (b n)")

    def time_steps(self, h32_ready):
        PE, ACT_, DVE, small = self.PE, self.ACT, self.DVE, self.small
        for t in range(TT):
            for k in range(KD):
                wait(PE, h32_ready[k])
                mm = PE.matmul(self.ps[:, 6, t * NH:(t + 1) * NH], self.h32[:, k, t * P:(t + 1) * P],
                               self.param("w_dt", k * NH, NH), start=k == 0, stop=k == KD - 1)
        dts = self.pe(mm)
        dt, step, scratch, rate = small[:, 16:24], small[:, 24:32], small[:, 32:40], small[:, 40:48]
        wait(DVE, dts)
        shifted = self.dve(DVE.tensor_tensor(dt, self.ps[:, 6, 0:8], self.param("dt_bias", 0, 8), ALU.add))
        dt_ready = self.softplus(dt, dt, shifted, scratch)
        exp_a = self.act(ACT_.activation(rate, self.param("a_log", 0, 8), ACT.Exp))
        wait(DVE, exp_a, dt_ready)
        return self.dve(DVE.scalar_tensor_tensor(step, dt, -1.0, rate, ALU.mult, ALU.mult))

    def retention_rates(self):
        ACT_, DVE, rate, tiny = self.ACT, self.DVE, self.small[:, 64:72], self.small[:, 72:80]
        logit = self.param("decay", 0, 8)
        a = self.act(ACT_.activation(tiny, logit, ACT.Abs))
        wait(ACT_, a)
        a = self.act(ACT_.activation(tiny, tiny, ACT.Exp, scale=-1.0))
        wait(ACT_, a)
        a = self.act(ACT_.activation(tiny, tiny, ACT.Ln, bias=1.0))
        wait(DVE, a)
        return self.dve(DVE.scalar_tensor_tensor(rate, logit, 0.0, tiny, ALU.min, ALU.subtract))

    def weighted_values(self, bank, weights, values, ready):
        wait(self.PE, *ready)
        for h in range(NH):
            low = h % 2 * HD
            out = self.ps[low:low + HD, bank + h // 2, :]
            v = lambda t: values[:, t, h * HD:(h + 1) * HD]
            self.PE.matmul(out[:, 0:S], v(0), self.wide(weights, h), start=True, stop=False)
            mm = self.PE.matmul(out[:, P:S], v(1), self.tail(weights, h), start=False, stop=True)
        return self.pe(mm)

    def mixers_and_merge(self, w_in, w_branch, u_ready, steps_ready, masks_ready):
        PE, ACT_, DVE, pe, act, dve, u, ps = self.PE, self.ACT, self.DVE, self.pe, self.act, self.dve, self.u, self.ps
        wide, tail, banks = self.wide, self.tail, self.banks
        y_hi = self.place("y_hi", [P, KD, S], F32R, at=self.rb)
        y_lo = self.place("y_lo", [P, KD, S], F32R, at=self.rb + KD * S * 4)
        zb = self.place("sb_scores", [P, NSTAGE], at=self.ra + 24576)
        sb = self.place("sb_softplus", [P, NSTAGE], at=self.ra + 24576 + 6144)
        zd = self.place("moba_scores", [P, NSTAGE], at=self.ra + 24576 + 12288)
        pd = self.place("moba_turned", [P, NSTAGE], at=self.ra + 24576 + 18432)
        vb = self.place("sb_values", [P, TT, BW], at=self.rc)
        vd = self.place("moba_values", [P, TT, BW], at=self.rc + 2048)
        xd = self.place("ssm_values", [P, TT, BW], at=self.rc)
        ap = self.place("a_padded", [P, 2, S + 2], at=self.rc + 6144)
        cp = self.place("xbc_padded", [P, 4, S + 3], at=self.rd)
        tri = self.place("ssm_steps", [P, NSTAGE], at=self.ra + 18 * 1024)
        dm = self.place("ssm_decay", [P, NSTAGE], at=self.ra + 6 * 1024)
        small, dt, step, before = self.small, self.small[:, 16:24], self.small[:, 24:32], self.small[:, 48:56]
        top, total = small[:, 0:8], small[:, 8:16]
        W3 = S + P
        strict_wide, strict_tail = self.stage[:, 0:S], self.stage[:, S:W3]
        causal_tail, causal_wide = self.stage[:, W3:W3 + P], self.stage[:, W3 + P:2 * W3]
        ssm_wide, ssm_tail = self.stage[:, 2 * W3:2 * W3 + S], self.stage[:, 2 * W3 + S:3 * W3]
        over_heads = lambda a: a.unsqueeze(1).to_broadcast([P, NH, a.shape[-1]])
        pair = lambda a: a.rearrange("p (c s) -> p c s", c=2)

        first_gate = self.place("gate_0", [P, 2, S], at=self.rc + 4096)
        later = self.place("gate_store", [P, 12, 2, S], at=self.ra + 24576)
        order = (3, 0, 1, 2)
        slots = [first_gate[:, :, :]] + [u[:, 2 * j:2 * j + 2, :] for j in range(3)] + \
            [later[:, j, :, :] for j in range(12)]
        bank_read, gates = {6: None, 7: None}, []
        slabs_done = []

        def gate_slab():
            n = len(slabs_done)
            bank = 6 + n % 2
            wait(PE, bank_read[bank])
            self.slab_step(self.columns(w_in, COL_G + order[n // 4] * D + n % 4 * 2 * P), self.feature_major(bank))
            slabs_done.append(self.slab_used.ahead(0))

        def gate_out(slot_free, raw=True):
            n = len(gates)
            wait(ACT_, slabs_done[n], *slot_free)
            bank_read[6 + n % 2] = act(ACT_.activation(slots[n], pair(ps[:, 6 + n % 2, :]), ACT.Copy if raw else ACT.Sigmoid))
            gates.append(bank_read[6 + n % 2])

        y_parts = {}
        branch_rows = w_branch.rearrange("a b (k p) n -> p (a b k) n", p=P)

        term_bank = lambda n: (n + 2) % 6
        used = []

        def branch_slab(place, banks_read=()):
            i = order[place]
            def products(hi, lo):
                for f in range(KD):
                    n = 4 * place + f // 2
                    if f % 2 == 0 and n >= 6:
                        wait(PE, used[n - 6])
                    for k in range(2):
                        mm = stationary_pair(PE, ps[:, term_bank(n), f % 2 * S:(f % 2 + 1) * S],
                                             hi[:, k, f * P:(f + 1) * P], lo[:, k, f * P:(f + 1) * P],
                                             y_hi[:, 2 * i + k, :], y_lo[:, 2 * i + k, :], k == 0, k == 1)
                return mm
            wait(PE, y_parts[i], *banks_read)
            self.slab_step(branch_rows[:, 2 * i:2 * i + 2, :], products)
            return self.slab_used.ahead(0)

        wait(PE, steps_ready, *u_ready)
        PE.matmul(ps[:, 5, 0:4], self.const("prefix"), step[:, 0:4], start=True, stop=True)
        PE.matmul(ps[:, 5, 4:8], self.const("ones"), step[:, 0:4], start=True, stop=False)
        summed = pe(PE.matmul(ps[:, 5, 4:8], self.const("prefix"), step[:, 4:8], start=False, stop=True))
        wait(DVE, summed)
        before_ready = dve(DVE.tensor_scalar(before, ps[:, 5, 0:8], -1.0, None, ALU.mult))

        for h in (0, 2, 1, 3):
            if h == 1:
                wait(PE, pe(mm))
            r = slice(h % 2 * HD, h % 2 * HD + HD)
            q, k = u[r, 6 + h // 2, :], u[r, 8 + h // 2, :]
            PE.matmul(wide(banks(0), h), k[:, 0:P], q, start=True, stop=True)
            mm = PE.matmul(tail(banks(0), h), k[:, P:S], q[:, P:S], start=True, stop=True)
        scores_b = pe(mm)
        bank_read[6] = vb_ready = self.token_major(6, 10, vb[:, :, :], [])
        bank_read[7] = vd_ready = self.token_major(7, 22, vd[:, :, :], [])
        wait(PE, before_ready)
        for h in (0, 2, 1, 3):
            if h == 1:
                wait(PE, pe(mm))
            r = slice(h % 2 * HD, h % 2 * HD + HD)
            q, k = u[r, 18 + h // 2, :], u[r, 20 + h // 2, :]
            PE.matmul(tail(banks(3), h), q[:, 0:P], k[:, 0:P], start=True, stop=True)
            mm = PE.matmul(wide(banks(3), h), q[:, P:S], k, start=True, stop=True)
        scores_d = pe(mm)
        wait(DVE, scores_b, masks_ready)
        dve(DVE.scalar_tensor_tensor(wide(zb, 0, NH), wide(banks(0), 0, NH), HD ** -0.5, over_heads(strict_wide), ALU.mult, ALU.add))
        zb_ready = dve(DVE.scalar_tensor_tensor(tail(zb, 0, NH), tail(banks(0), 0, NH), HD ** -0.5, over_heads(strict_tail), ALU.mult, ALU.add))
        wait(DVE, scores_d)
        dve(DVE.scalar_tensor_tensor(tail(zd, 0, NH), tail(banks(3), 0, NH), HD ** -0.5, over_heads(causal_tail), ALU.mult, ALU.add))
        zd_ready = dve(DVE.scalar_tensor_tensor(wide(zd, 0, NH), wide(banks(3), 0, NH), HD ** -0.5, over_heads(causal_wide), ALU.mult, ALU.add))
        gate_slab()
        self.ready_table(ACT.Exp)

        wait(DVE, zd_ready)
        dve(DVE.tensor_reduce(top[:, 0:4], tail(zd, 0, NH), AX.X, ALU.max))
        tops = dve(DVE.tensor_reduce(top[:, 4:8], wide(zd, 0, NH), AX.X, ALU.max))
        wait(DVE, tops)
        negated = dve(DVE.tensor_scalar(top, top, -1.0, None, ALU.mult))

        wait(DVE, *u_ready)
        dve(DVE.memset(ap[:, :, 0:2], 0.0))
        last = dve(DVE.tensor_tensor(ap[:, :, 2:S + 2], u[:, 4:6, :], u[:, 0:2, :], ALU.mult))
        wait(DVE, last)
        tap = lambda c, j: self.param("a_taps", 3 * c + j)
        for j in range(3):
            for c in range(2):
                if j == 0:
                    last = dve(DVE.tensor_scalar(u[:, c, :], ap[:, c, 0:S], tap(c, 0), None, ALU.mult))
                else:
                    last = dve(DVE.scalar_tensor_tensor(u[:, c, :], ap[:, c, j:j + S], tap(c, j), u[:, c, :], ALU.mult, ALU.add))
            wait(DVE, last)
        ya = dve(DVE.tensor_tensor(u[:, 0:2, :], u[:, 0:2, :], u[:, 2:4, :], ALU.mult))

        sp_ready = self.softplus(sb[:, :], zb[:, :], zb_ready, sb[:, :])
        gate_slab()
        gate_out([])
        y_parts[0] = y_a = self.split_from(y_hi[:, 0:2, :], y_lo[:, 0:2, :], u[:, 0:2, :], ya)
        gate_out([y_a])
        wait(PE, sp_ready)
        for h in range(NH):
            PE.matmul(wide(banks(0), h), self.const("suffix"), wide(sb, h), start=True, stop=False)
            PE.matmul(wide(banks(0), h)[:, P:S], self.const("ones"), tail(sb, h), start=False, stop=True)
            mm = PE.matmul(tail(banks(0), h), self.const("suffix"), tail(sb, h), start=True, stop=True)
        sums = pe(mm)

        wait(DVE, steps_ready, scores_d)
        prefix_ones = self.consts[:, CONSTS["prefix"][0]:CONSTS["prefix"][0] + S]
        for h in range(NH):
            dve(DVE.tensor_scalar(wide(tri, h), prefix_ones, step[:, h:h + 1], None, ALU.mult))
            tri_ready = dve(DVE.tensor_scalar(tail(tri, h), self.const("prefix"), step[:, 4 + h:5 + h], None, ALU.mult))
        zeroed = dve(DVE.memset(cp[:, :, 0:3], 0.0))

        wait(ACT_, negated)
        for t, part in ((0, tail), (1, wide)):
            for h in range(NH):
                e = act(ACT_.activation(part(zd, h), part(zd, h), ACT.Exp, bias=top[:, 4 * t + h:4 * t + h + 1],
                                        accum_out=total[:, 4 * t + h:4 * t + h + 1]))
        wait(DVE, sums)
        exponent = dve(DVE.tensor_tensor(zb[:, :], zb[:, :], banks(0), ALU.subtract))
        wait(ACT_, exponent)
        wb_ready = act(ACT_.activation(zb[:, :], zb[:, :], ACT.Exp))
        wait(DVE, e)
        inverse = dve(DVE.reciprocal(total, total))
        wait(DVE, inverse)
        for t, part in ((0, tail), (1, wide)):
            for h in range(NH):
                weights_d = dve(DVE.tensor_scalar(part(zd, h), part(zd, h), total[:, 4 * t + h:4 * t + h + 1], None, ALU.mult))
        gate_slab()
        copied = act(ACT_.activation(cp[:, :, 3:S + 3], u[:, 14:18, :], ACT.Copy))
        gate_slab()
        gate_out([y_a])
        wait(PE, weights_d)
        for h in range(NH):
            for source, target in ((tail(zd, h), wide(banks(3), h)[:, 0:P]), (wide(zd, h)[:, 0:P], wide(banks(3), h)[:, P:S]),
                                   (wide(zd, h)[:, P:S], tail(banks(3), h))):
                mm = PE.transpose(target, source, self.const("ident"))
        turned = pe(mm)
        out_b = self.weighted_values(0, zb, vb, [wb_ready, vb_ready])
        wait(ACT_, turned)
        pd_ready = act(ACT_.activation(pd[:, :], banks(3), ACT.Copy))

        wait(DVE, zeroed, copied)
        tap = lambda c, j: self.param("ssm_taps", 4 * c + j)
        for j in range(4):
            for c in range(4):
                if j == 0:
                    last = dve(DVE.tensor_scalar(u[:, 14 + c, :], cp[:, c, 0:S], tap(c, 0), self.param("ssm_bias", c), ALU.mult, ALU.add))
                else:
                    last = dve(DVE.scalar_tensor_tensor(u[:, 14 + c, :], cp[:, c, j:j + S], tap(c, j), u[:, 14 + c, :], ALU.mult, ALU.add))
            wait(DVE, last)
        gate_slab()
        gate_out([y_a])
        out_d = self.weighted_values(3, pd, vd, [pd_ready, vd_ready])
        wait(ACT_, last)
        act(ACT_.activation(u[:, 12:14, :], u[:, 12:14, :], ACT.Silu))
        xbc = act(ACT_.activation(u[:, 14:18, :], u[:, 14:18, :], ACT.Silu))
        two = lambda bank: ps[:, bank:bank + 2, 0:S]
        y_parts[1] = y_b = self.split_from(y_hi[:, 2:4, :], y_lo[:, 2:4, :], two(0), out_b)
        y_parts[3] = y_d = self.split_from(y_hi[:, 6:8, :], y_lo[:, 6:8, :], two(3), out_d)
        gate_out([out_b])

        wait(PE, tri_ready, y_b)
        for h in range(NH):
            PE.matmul(wide(banks(0), h), self.const("ones"), wide(tri, h), start=True, stop=False)
            mm = PE.matmul(wide(banks(0), h)[:, P:S], self.const("ones"), tail(tri, h), start=False, stop=True)
        running = pe(mm)
        wait(PE, xbc, y_d)
        for g in range(2):
            r = slice(g * HD, g * HD + HD)
            b, c = u[r, 16, :], u[r, 17, :]
            PE.matmul(ps[:, 3 + g, 0:S], b[:, 0:P], c, start=True, stop=True)
            mm = PE.matmul(ps[:, 3 + g, S:W3], b[:, P:S], c[:, P:S], start=True, stop=True)
        products = pe(mm)
        for t in range(TT):
            for c in range(2):
                mm = PE.transpose(ps[:, 5, t * S + c * P:t * S + (c + 1) * P], u[:, 14 + c, t * P:(t + 1) * P], self.const("ident"))
        turned = pe(mm)
        gate_slab()
        gate_out([out_b])
        wait(DVE, running, before_ready)
        for h in range(NH):
            dve(DVE.scalar_tensor_tensor(wide(dm, h), wide(banks(0), h), before[:, h:h + 1], ssm_wide, ALU.add, ALU.add))
            seg = dve(DVE.scalar_tensor_tensor(tail(dm, h), wide(banks(0), h)[:, P:S], before[:, 4 + h:5 + h], ssm_tail, ALU.add, ALU.add))
        wait(ACT_, seg)
        decay = act(ACT_.activation(dm[:, :], dm[:, :], ACT.Exp))
        wait(DVE, turned, out_b)
        for t in range(TT):
            for h in range(NH):
                xd_ready = dve(DVE.tensor_scalar(xd[:, t, h * HD:(h + 1) * HD], ps[:, 5, t * S + h * HD:t * S + (h + 1) * HD],
                                                 dt[:, 4 * t + h:4 * t + h + 1], None, ALU.mult))
        wait(DVE, decay, products)
        for g in range(2):
            group = lambda n: ps[:, 3 + g, n].unsqueeze(1).to_broadcast([P, 2, n.stop - n.start])
            dve(DVE.tensor_tensor(wide(dm, 2 * g, 2), wide(dm, 2 * g, 2), group(slice(0, S)), ALU.mult))
            mixed = dve(DVE.tensor_tensor(tail(dm, 2 * g, 2), tail(dm, 2 * g, 2), group(slice(S, W3)), ALU.mult))
        gate_slab()
        gate_out([out_b])
        out_c = self.weighted_values(0, dm, xd, [mixed, xd_ready])
        gate_slab()
        gate_out([out_d])
        wait(DVE, out_c)
        for c in range(2):
            skipped = dve(DVE.scalar_tensor_tensor(u[:, 14 + c, :], u[:, 14 + c, :], self.param("skip", c), ps[:, c, 0:S], ALU.mult, ALU.add))
        wait(DVE, skipped)
        gated = dve(DVE.tensor_tensor(u[:, 14:16, :], u[:, 14:16, :], u[:, 12:14, :], ALU.mult))
        wait(ACT_, gated)
        squares = act(ACT_.activation(u[:, 12:14, :], u[:, 14:16, :], ACT.Square))
        wait(PE, squares)
        for c in range(2):
            mm = PE.matmul(ps[:, 0, c * S:(c + 1) * S], self.const("ones"), u[:, 12 + c, :], start=True, stop=True)
        summed = pe(mm)
        branch_done = [branch_slab(0, [mixed, xd_ready])]
        gate_slab()
        gate_out([out_d])
        factor = u[:, 16:18, :]
        wait(ACT_, summed)
        m = root = act(ACT_.activation(factor, pair(ps[:, 0, :]), ACT.Sqrt, scale=1.0 / P, bias=self.eps[:, :]))
        wait(DVE, m)
        m = dve(DVE.reciprocal(factor, factor))
        wait(DVE, m)
        for c in range(2):
            normed = dve(DVE.scalar_tensor_tensor(u[:, 14 + c, :], u[:, 14 + c, :], self.param("ssm_norm", c), u[:, 16 + c, :], ALU.mult, ALU.mult))
        y_parts[2] = y_c = self.split_from(y_hi[:, 4:6, :], y_lo[:, 4:6, :], u[:, 14:16, :], normed)

        gate_slab()
        gate_out([out_d])

        held = len(gates)
        merged = self.place("merged", [P, KD, S], at=self.ra + 6144)
        m_hi = self.place("m_hi", [P, KD, S], F32R, at=self.ra + 24576)
        m_lo = self.place("m_lo", [P, KD, S], F32R, at=self.ra + 24576 + 8192)
        ready = []

        def add_term(n, branch_done):
            q = n % 4
            if n < held:
                wait(ACT_, gates[n])
                gates[n] = act(ACT_.activation(slots[n], slots[n], ACT.Sigmoid))
            chunk = merged[:, 2 * q:2 * q + 2, :]
            wait(DVE, gates[n], branch_done, *(used[-1:] or [y_c]))
            if n < 4:
                used.append(dve(DVE.tensor_tensor(chunk, slots[n], pair(ps[:, term_bank(n), :]), ALU.mult)))
                return
            term = dve(DVE.tensor_tensor(slots[n], slots[n], pair(ps[:, term_bank(n), :]), ALU.mult))
            wait(DVE, term)
            used.append(dve(DVE.tensor_tensor(chunk, chunk, slots[n], ALU.add)))

        def split_merged(q):
            c = slice(2 * q, 2 * q + 2)
            ready.append(self.split_from(m_hi[:, c, :], m_lo[:, c, :], merged[:, c, :], used[-1]))

        self.ready_table(ACT.Sigmoid)
        for place in range(4):
            if place:
                branch_done.append(branch_slab(place, [root, skipped]))
            for q in range(4):
                if place and q >= 2:
                    gate_slab()
                    gate_out([out_b, out_d], raw=False)
                add_term(4 * place + q, branch_done[place])
                if place == 3:
                    split_merged(q)
        self.y_banks_free = used[12:14]
        return m_hi, m_lo, ready

    def feed_forward(self, tag, gate, up, down, ht_ready, banks_free):
        ps, PE, ACT_, DVE, act, dve = self.ps, self.PE, self.ACT, self.DVE, self.act, self.dve
        chunks = FF // P
        a_hi = self.place(f"ff_hi{tag}", [P, chunks, S], F32R, at=self.ra)
        a_lo = self.place(f"ff_lo{tag}", [P, chunks, S], F32R, at=self.ra + chunks * S * 4)
        silu = self.place(f"ff_silu{tag}", [P, 3, 2 * S], at=self.rb)
        whole = self.place(f"ff_act{tag}", [P, 3, 2 * S], at=self.rb + 6144)
        wait(PE, *banks_free)
        def step(turn, j, ht_ready=()):
            b = j % 3
            pair = turn * 3 + j
            earlier = dve.ahead(-5)
            wait(PE, earlier)
            self.slab_step(gate(pair), self.feature_major(2 * b, ht_ready))
            wait(ACT_, self.slab_used.ahead(0), earlier)
            s = act(ACT_.activation(silu[:, b, :], ps[:, 2 * b, :], ACT.Silu))
            self.slab_step(up(pair), self.feature_major(2 * b + 1))
            wait(DVE, self.slab_used.ahead(0), s, act.ahead(-5), dve.ahead(0))
            m = dve(DVE.tensor_tensor(whole[:, b, :], silu[:, b, :], ps[:, 2 * b + 1, :], ALU.mult))
            chunk = bass.ds(pair * 2, 2)
            flat = whole[:, b, :].rearrange("p (c s) -> p c s", c=2)
            self.split_from(a_hi[:, chunk, :], a_lo[:, chunk, :], flat, m)
        def body(turn):
            for j in range(3):
                step(turn, j, ht_ready if j == 0 else ())
        pairs = chunks // 2
        self.loop(pairs // 3, {act: 6, dve: 6}, body, slabs=NRAW)
        for j in range(pairs % 3):
            step(pairs // 3, j)
        a_ready = dve.ahead(0)
        return self.into_residual(down, lambda c: a_hi[:, bass.ds(c, 1), :].rearrange("p a s -> p (a s)"),
                                  lambda c: a_lo[:, bass.ds(c, 1), :].rearrange("p a s -> p (a s)"), chunks, [a_ready, act.ahead(0)])

    def norm_in_place(self, gain, x_ready):
        wait(self.DVE, self.norm_factor(x_ready))
        return [self.dve(self.DVE.scalar_tensor_tensor(
            self.xt[:, c, :], self.xt[:, c, :], self.param(gain, c), self.rstd, ALU.mult, ALU.mult))
            for c in range(KD)]

    def retention(self, w_in, w_out, ht_ready, banks_free, stage_ready, rates_ready):
        ps, PE, ACT_, DVE, pe, act, dve = self.ps, self.PE, self.ACT, self.DVE, self.pe, self.act, self.dve
        small = self.small
        q_t = self.place("ret_q", [P, KD, S], at=self.ra)
        k_t = self.place("ret_k", [P, KD, S], at=self.ra + 8192)
        v = self.place("ret_v", [P, TT, 2 * D], at=self.ra + 16384)
        g_t = self.place("ret_g", [P, 2 * KD, S], at=self.ra + 32768)
        cos_part = self.place("ret_cos", [P, 2, S], at=self.rd)
        sin_part = self.place("ret_sin", [P, 2, S], at=self.rd + 2048)
        table = lambda i: self.stage[:, i * S:(i + 1) * S].unsqueeze(1).to_broadcast([P, 2, S])
        wait(PE, *banks_free)
        wait(DVE, stage_ready)

        def head(turn):
            for b, out in ((0, q_t), (1, k_t)):
                wait(PE, dve.ahead(2 - 8))
                self.slab_step(self.columns(w_in, turn * BW + b * D), self.feature_major(b, ht_ready if b == 0 else ()))
                pair = ps[:, b, :].rearrange("p (c s) -> p c s", c=2)
                wait(DVE, self.slab_used.ahead(0), dve.ahead(0))
                dve(DVE.tensor_tensor(cos_part[:, :, :], pair, table(0), ALU.mult))
                parts = dve(DVE.tensor_tensor(sin_part[:, :, :], pair, table(1), ALU.mult))
                wait(DVE, parts)
                first, second = out[:, bass.ds(turn * 2, 1), :], out[:, bass.ds(turn * 2 + 1, 1), :]
                dve(DVE.tensor_tensor(first, cos_part[:, 0:1, :], sin_part[:, 1:2, :], ALU.subtract))
                dve(DVE.tensor_tensor(second, sin_part[:, 0:1, :], cos_part[:, 1:2, :], ALU.add))
            for c in range(2):
                wait(PE, act.ahead(1 - 4))
                def products(hi, lo, bank=2 + c):
                    for t in range(TT):
                        tok = slice(t * P, (t + 1) * P)
                        for k in range(KD):
                            out = ps[:, bank, t * S:(t + 1) * S]
                            PE.matmul(out, self.ht_hi[:, k, tok], hi[:, k, :], start=k == 0, stop=False)
                            PE.matmul(out, self.ht_hi[:, k, tok], lo[:, k, :], start=False, stop=False)
                            mm = PE.matmul(out, self.ht_lo[:, k, tok], hi[:, k, :], start=False, stop=k == KD - 1)
                    return mm
                self.slab_step(self.columns(w_in, turn * (2 * BW) + 2 * D + c * BW), products)
                wait(ACT_, self.slab_used.ahead(0))
                act(ACT_.activation(v[:, :, bass.ds(turn * (2 * BW) + c * BW, BW)],
                                    ps[:, 2 + c, :].rearrange("p (t f) -> p t f", t=TT), ACT.Copy))
            for c in range(2):
                wait(PE, act.ahead(1 - 4))
                self.slab_step(self.columns(w_in, turn * (2 * BW) + 4 * D + c * BW), self.feature_major(4 + c))
                wait(ACT_, self.slab_used.ahead(0))
                act(ACT_.activation(g_t[:, bass.ds(turn * 4 + 2 * c, 2), :],
                                    ps[:, 4 + c, :].rearrange("p (c s) -> p c s", c=2), ACT.Silu))
        self.loop(NH, {act: 4, dve: 8}, head, slabs=NRAW)
        loop_act, loop_dve = act.ahead(0), dve.ahead(0)

        decay = self.place("ret_decay", [P, NH, 2, S], at=self.rc)
        rate, decay_ready = small[:, 64:72], []
        distances = lambda i: self.stage[:, 2 * i * S:2 * (i + 1) * S].rearrange("p (m s) -> p m s", m=TT)
        wait(DVE, rates_ready, *ht_ready)
        for h in range(NH):
            a = dve(DVE.tensor_scalar(decay[:, h, :, :], distances(1), rate[:, h:h + 1], None, ALU.mult))
            wait(DVE, a)
            a = dve(DVE.scalar_tensor_tensor(decay[:, h, :, :], distances(2), rate[:, 4 + h:5 + h], decay[:, h, :, :], ALU.mult, ALU.add))
            wait(ACT_, a)
            decay_ready.append(act(ACT_.activation(decay[:, h, :, :], decay[:, h, :, :], ACT.Exp)))

        wait(PE, loop_dve, loop_act)
        for h in range(NH):
            for m in range(TT):
                for c in range(2):
                    mm = PE.matmul(ps[:, h, m * S:(m + 1) * S], k_t[:, 2 * h + c, m * P:(m + 1) * P], q_t[:, 2 * h + c, :],
                                   start=c == 0, stop=c == 1)
            scored = pe(mm)
            wait(DVE, scored, decay_ready[h])
            pair = ps[:, h, :].rearrange("p (m s) -> p m s", m=2)
            weights = dve(DVE.scalar_tensor_tensor(decay[:, h, :, :], pair, 1.0 / 16, decay[:, h, :, :], ALU.mult, ALU.mult))
        y_hi = self.place("ret_y_hi", [P, 2 * KD, S], F32R, at=self.ra)
        y_lo = self.place("ret_y_lo", [P, 2 * KD, S], F32R, at=self.rb)
        yn = self.place("ret_normed", [P, TT, 2 * BW], at=self.rd)
        stats, moments = small[:, 80:92], small[:, 92:96]
        summed, normed, turned, ready = [], [], [], []
        wait(PE, weights)

        def values(h):
            for t in range(TT):
                bank = 4 - h % 2 * 4 + t
                wait(PE, *normed[h - 2][t:t + 1] if h >= 2 else ())
                for m in range(TT):
                    mm = PE.matmul(ps[:, bank, :], decay[:, h, m, t * P:(t + 1) * P],
                                   v[:, m, h * 2 * BW:(h + 1) * 2 * BW], start=m == 0, stop=m == TT - 1)
                summed.append(pe(mm))

        def norm_values(h):
            normed.append([])
            for t in range(TT):
                bank = 4 - h % 2 * 4 + t
                wait(DVE, summed[2 * h + t], loop_dve)
                a = dve(DVE.bn_stats(stats[:, 6 * t:6 * t + 6], ps[:, bank, :]))
                wait(DVE, a)
                a = dve(DVE.bn_aggr(moments[:, 2 * t:2 * t + 2], stats[:, 6 * t:6 * t + 6]))
                wait(ACT_, a)
                a = act(ACT_.activation(stats[:, 6 * t:6 * t + 1], moments[:, 2 * t + 1:2 * t + 2], ACT.Sqrt, bias=self.eps[:, :]))
                wait(DVE, a)
                a = dve(DVE.reciprocal(stats[:, 6 * t:6 * t + 1], stats[:, 6 * t:6 * t + 1]))
                wait(DVE, a, *turned[-1:])
                normed[h].append(dve(DVE.tensor_scalar(yn[:, t, :], ps[:, bank, :], moments[:, 2 * t:2 * t + 1],
                                                       stats[:, 6 * t:6 * t + 1], ALU.subtract, ALU.mult)))

        def turn_values(h):
            wait(PE, *normed[h], *ready[-1:])
            for c in range(4):
                for t in range(TT):
                    mm = PE.transpose(ps[:, 6 + c // 2, c % 2 * S + t * P:c % 2 * S + (t + 1) * P],
                                      yn[:, t, c * P:(c + 1) * P], self.const("ident"))
            turned.append(pe(mm))
            wait(DVE, turned[-1])
            for c in range(4):
                z = dve(DVE.scalar_tensor_tensor(g_t[:, 4 * h + c, :], ps[:, 6 + c // 2, c % 2 * S:(c % 2 + 1) * S],
                                                 self.param("gn_gain", 4 * h + c), g_t[:, 4 * h + c, :], ALU.mult, ALU.mult))
            c = slice(4 * h, 4 * h + 4)
            ready.append(self.split_from(y_hi[:, c, :], y_lo[:, c, :], g_t[:, c, :], z))
        values(0)
        for h in range(NH):
            norm_values(h)
            if h + 1 < NH:
                values(h + 1)
            turn_values(h)
        one = lambda a: (lambda c: a[:, bass.ds(c, 1), :].rearrange("p a s -> p (a s)"))
        return self.into_residual(w_out, one(y_hi), one(y_lo), 2 * KD, ready)

    def fourier(self, w_out, ht_ready, stage_ready):
        ps, PE, ACT_, DVE, pe, act, dve = self.ps, self.PE, self.ACT, self.DVE, self.pe, self.act, self.dve
        mixed = self.place("fft_features", [P, KD, 2 * S], at=self.ra)
        y_hi = self.place("fft_hi", [P, KD, S], F32R, at=self.rb)
        y_lo = self.place("fft_lo", [P, KD, S], F32R, at=self.rb + KD * S * 4)
        cos_sin = self.stage[:, 0:4 * S].rearrange("p (c n) -> p c n", c=2)
        minus_sin = self.stage[:, 4 * S:6 * S].rearrange("p (c n) -> p c n", c=2)
        wait(PE, *ht_ready, stage_ready)
        copied = []
        for g in range(4):
            for t in range(TT):
                b = 2 * g + t
                for c in range(2):
                    mm = PE.matmul(ps[:, b, :], self.h32[:, 2 * g + c, t * P:(t + 1) * P], cos_sin[:, c, :],
                                   start=c == 0, stop=c == 1)
                done = pe(mm)
                engine, count = (ACT_, act) if b % 2 else (DVE, dve)
                wait(engine, done)
                copied.append(count(engine.activation(mixed[:, b, :], ps[:, b, :], ACT.Copy) if b % 2
                                    else engine.tensor_copy(mixed[:, b, :], ps[:, b, :])))
        ready = []
        for g in range(4):
            wait(PE, copied[2 * g], copied[2 * g + 1])
            for c in range(2):
                for t in range(TT):
                    out = ps[:, g, c * S:(c + 1) * S]
                    PE.matmul(out, mixed[:, 2 * g + t, c * P:(c + 1) * P], cos_sin[:, t, 0:S], start=t == 0, stop=False)
                    mm = PE.matmul(out, mixed[:, 2 * g + t, S + c * P:S + (c + 1) * P], minus_sin[:, t, :],
                                   start=False, stop=t == TT - 1)
            done = pe(mm)
            ready.append(self.split_from(y_hi[:, 2 * g:2 * g + 2, :], y_lo[:, 2 * g:2 * g + 2, :],
                                         ps[:, g, :].rearrange("p (c s) -> p c s", c=2), done))
        one = lambda a: (lambda c: a[:, bass.ds(c, 1), :].rearrange("p a s -> p (a s)"))
        return self.into_residual(w_out, one(y_hi), one(y_lo), KD, ready)

    def route(self, ht_ready):
        ps, PE, ACT_, DVE, pe, act, dve = self.ps, self.PE, self.ACT, self.DVE, self.pe, self.act, self.dve
        self.rows_hi = rows_hi = self.place("rows_hi", [P, TT, D], F32R, at=self.rb)
        self.rows_lo = rows_lo = self.place("rows_lo", [P, TT, D], F32R, at=self.rb + TT * D * 4)
        names = ["logit", "score", "first", "rest", "second", "gate", "chosen"]
        at = self.ra + 32768
        tiles = {}
        for n in names:
            tiles[n] = self.place("route_" + n, [P, TT, NE], at=at)
            at += TT * NE * 4
        self.gates = self.place("gates_of", [P, TT, NE + 1], at=at)
        self.places = self.place("place_of", [P, TT, NE + 1], at=at + 96)
        self.total = self.place("chosen_total", [P, NE + 1], at=at + 192)
        self.most = self.place("most_chosen", [P, 1], I32, at=at + 256)
        col = self.place("route_columns", [P, 16], at=at + 288)
        logit, score, first, rest, second, gate, chosen = (tiles[n] for n in names)
        order = self.const("order")

        wait(PE, *ht_ready)
        for t in range(TT):
            for k in range(KD):
                mm = PE.matmul(ps[:, 7, t * NE:(t + 1) * NE], self.h32[:, k, t * P:(t + 1) * P],
                               self.param("router", k * NE, NE), start=k == 0, stop=k == KD - 1)
        routed = pe(mm)
        turned = []
        for t in range(TT):
            for half in range(2):
                b = 2 * t + half
                for c in range(4):
                    mm = PE.transpose(ps[:, b, c * P:(c + 1) * P], self.h32[:, 4 * half + c, t * P:(t + 1) * P], self.const("ident"))
                turned.append(pe(mm))
        wait(DVE, routed)
        last = dve(DVE.tensor_copy(logit[:, :, :], ps[:, 7, 0:TT * NE].rearrange("p (t e) -> p t e", t=TT)))

        def pick(values, out, top, mark):
            nonlocal last
            for t in range(TT):
                wait(DVE, last)
                last = dve(DVE.tensor_reduce(top(t), values[:, t, :], AX.X, ALU.max))
                wait(DVE, last)
                last = dve(DVE.scalar_tensor_tensor(score[:, t, :], values[:, t, :], top(t), order, ALU.is_equal, ALU.mult))
                wait(DVE, last)
                last = dve(DVE.tensor_reduce(mark(t), score[:, t, :], AX.X, ALU.max))
                wait(DVE, last)
                last = dve(DVE.tensor_scalar(out[:, t, :], score[:, t, :], mark(t), None, ALU.is_equal))
        c1 = lambda base: (lambda t: col[:, base + t:base + t + 1])
        pick(logit, first, c1(0), c1(4))
        wait(DVE, last)
        last = dve(DVE.scalar_tensor_tensor(rest[:, :, :], first[:, :, :], NEG, logit[:, :, :], ALU.mult, ALU.add))
        pick(rest, second, c1(2), c1(4))
        wait(DVE, last)
        last = dve(DVE.tensor_tensor(col[:, 6:8], col[:, 2:4], col[:, 0:2], ALU.subtract))
        wait(ACT_, last)
        e = act(ACT_.activation(col[:, 8:10], col[:, 6:8], ACT.Exp))
        wait(DVE, e)
        last = dve(DVE.tensor_scalar(col[:, 10:12], col[:, 8:10], 1.0, None, ALU.add))
        wait(DVE, last)
        last = dve(DVE.reciprocal(col[:, 12:14], col[:, 10:12]))
        wait(DVE, last)
        last = dve(DVE.tensor_tensor(col[:, 14:16], col[:, 8:10], col[:, 12:14], ALU.mult))
        picked = dve(DVE.tensor_tensor(chosen[:, :, :], first[:, :, :], second[:, :, :], ALU.add))
        wait(DVE, last)
        for t in range(TT):
            last = dve(DVE.tensor_scalar(gate[:, t, :], first[:, t, :], col[:, 12 + t:13 + t], None, ALU.mult))
        dve(DVE.memset(self.gates[:, :, NE:NE + 1], 0.0))
        cleared = dve(DVE.memset(self.places[:, :, NE:NE + 1], -1.0))
        wait(DVE, last)
        for t in range(TT):
            last = dve(DVE.scalar_tensor_tensor(self.gates[:, t, 0:NE], second[:, t, :], col[:, 14 + t:15 + t], gate[:, t, :], ALU.mult, ALU.add))
        wait(PE, picked)
        PE.matmul(ps[:, 6, 0:NE], self.const("before"), chosen[:, 0, :], start=True, stop=True)
        PE.matmul(ps[:, 6, NE:2 * NE], self.const("ones"), chosen[:, 0, :], start=True, stop=False)
        PE.matmul(ps[:, 6, NE:2 * NE], self.const("before"), chosen[:, 1, :], start=False, stop=True)
        PE.matmul(ps[:, 6, 2 * NE:3 * NE], self.const("ones"), chosen[:, 0, :], start=True, stop=False)
        counted = pe(PE.matmul(ps[:, 6, 2 * NE:3 * NE], self.const("ones"), chosen[:, 1, :], start=False, stop=True))
        wait(DVE, counted)
        a = dve(DVE.scalar_tensor_tensor(self.places[:, :, 0:NE], ps[:, 6, 0:2 * NE].rearrange("p (t e) -> p t e", t=TT),
                                         1.0, chosen[:, :, :], ALU.add, ALU.mult))
        wait(DVE, a)
        placed = dve(DVE.tensor_scalar(self.places[:, :, 0:NE], self.places[:, :, 0:NE], -1.0, None, ALU.add))
        a = dve(DVE.tensor_reduce(self.total[:, 0:1], ps[:, 6, 2 * NE:3 * NE], AX.X, ALU.max))
        wait(DVE, a)
        most = dve(DVE.tensor_copy(self.most[:, :], self.total[:, 0:1]))
        for t in range(TT):
            for half in range(2):
                b = 2 * t + half
                c = slice(4 * P * half, 4 * P * half + 4 * P)
                rows = self.split_from(rows_hi[:, t, c], rows_lo[:, t, c], ps[:, b, :], turned[b])
        return [placed, last, rows, most, cleared]

    def experts(self, w_gate, w_up, w_down, slot0, routed, tag):
        ps, PE, ACT_, DVE, pe, act, dve = self.ps, self.PE, self.ACT, self.DVE, self.pe, self.act, self.dve
        at = self.ra
        def buf(name, shape, dtype=F32):
            nonlocal at
            t = self.place(name + tag, shape, dtype, at=at)
            at += -(-int(np.prod(shape[1:])) * 4 // 32) * 32
            return t
        xg_hi, xg_lo = buf("xg_hi", [P, KD, P], F32R), buf("xg_lo", [P, KD, P], F32R)
        pick = buf("pick", [P, TT, P], F32R)
        pick_t = buf("pick_t", [P, S], F32R)
        y_hi, y_lo = buf("y_hi_", [P, D], F32R), buf("y_lo_", [P, D], F32R)
        silu, whole = buf("silu_", [P, 4 * P]), buf("act_", [P, 4 * P])
        a_parts = [(buf(f"a_hi{i}_", [P, 4, P], F32R), buf(f"a_lo{i}_", [P, 4, P], F32R))
                   for i in range(2)]
        columns = buf("expert_columns", [P, 8])
        slot_gate = buf("slot_gate", [P, 1])
        gate_w = w_gate.rearrange("a e (k p) n -> p (a e k) n", p=P)
        up_w = w_up.rearrange("a e (k p) n -> p (a e k) n", p=P)
        down_w = w_down.rearrange("a e (k p) n -> p (a e k) n", p=P)
        slots = self.consts[:, CONSTS["slot"][0] + slot0:CONSTS["slot"][0] + slot0 + P]
        tiles = FE // (4 * P)
        HC = FE // P

        def build_pick(e, free):
            wait(DVE, *free, dve.ahead(0))
            a = dve(DVE.tensor_copy(columns[:, 0:TT], self.places[:, :, bass.ds(e, 1)].rearrange("p t e -> p (t e)")))
            wait(DVE, a)
            for t in range(TT):
                p = dve(DVE.tensor_scalar(pick[:, t, :], slots, columns[:, t:t + 1], None, ALU.is_equal))
            return p

        def gather(pick_ready, banks_free):
            wait(PE, pick_ready, *banks_free)
            for f in range(KD):
                out = ps[:, 6 + f // 4, f % 4 * P:(f % 4 + 1) * P]
                n = 0
                for t in range(TT):
                    for part in (self.rows_hi, self.rows_lo):
                        mm = PE.matmul(out, part[:, t, f * P:(f + 1) * P], pick[:, t, :], start=n == 0, stop=n == 3)
                        n += 1
            return pe(mm)

        def split_gathered(done):
            flat = lambda a: a[:, :, :].rearrange("p k s -> p (k s)")
            return self.split_from(flat(xg_hi), flat(xg_lo), ps[:, 6:8, :].rearrange("p b n -> p (b n)"), done,
                                   free=[self.slab_used.ahead(0)])

        def hidden(weight, e, f, half, bank):
            def products(hi, lo):
                for k in range(4):
                    kk = 4 * half + k
                    PE.matmul(ps[:, bank, :], xg_hi[:, kk, :], hi[:, k, :], start=kk == 0, stop=False)
                    PE.matmul(ps[:, bank, :], xg_hi[:, kk, :], lo[:, k, :], start=False, stop=False)
                    mm = PE.matmul(ps[:, bank, :], xg_lo[:, kk, :], hi[:, k, :], start=False, stop=kk == KD - 1)
                return mm
            return weight[:, bass.ds(e * KD + 4 * half, 4), bass.ds(f * (4 * P), 4 * P)], products

        def gate_tile(e, f):
            wait(PE, act.ahead(0))
            for half in range(2):
                self.slab_step(*hidden(gate_w, e, f, half, 0))

        def silu_tile():
            wait(ACT_, self.slab_used.ahead(0), dve.ahead(0))
            return act(ACT_.activation(silu[:, :], ps[:, 0, :], ACT.Silu))

        def up_tile(e, f):
            for half in range(2):
                self.slab_step(*hidden(up_w, e, f, half, 1))

        def act_tile(s):
            wait(DVE, self.slab_used.ahead(0), s, pe.ahead(0))
            return dve(DVE.tensor_tensor(whole[:, :], silu[:, :], ps[:, 1, :], ALU.mult))

        def turn_tile(whole_ready, bank_free):
            wait(PE, whole_ready, *bank_free)
            for c in range(4):
                mm = PE.transpose(ps[:, 2, c * P:(c + 1) * P], whole[:, c * P:(c + 1) * P], self.const("ident"))
            return pe(mm)

        def split_tile(turned, which=0):
            flat = lambda a: a[:, :, :].rearrange("p k s -> p (k s)")
            return self.split_from(flat(a_parts[which][0]), flat(a_parts[which][1]), ps[:, 2, :], turned)

        def down_tile(e, f, a_ready, which=0, halves=range(2)):
            a_hi, a_lo = a_parts[which]
            wait(PE, a_ready)
            for j in halves:
                def products(hi, lo):
                    for k in range(2):
                        for n in range(2):
                            out = ps[:, 4 + n, :]
                            w = slice(n * 512, (n + 1) * 512)
                            PE.matmul(out, a_hi[:, 2 * j + k, :], hi[:, k, w], start=False, stop=False, skip_group_check=True)
                            PE.matmul(out, a_hi[:, 2 * j + k, :], lo[:, k, w], start=False, stop=False, skip_group_check=True)
                            mm = PE.matmul(out, a_lo[:, 2 * j + k, :], hi[:, k, w], start=False, stop=False, skip_group_check=True)
                    return mm
                self.slab_step(down_w[:, bass.ds(e * HC + f * 4 + 2 * j, 2), :], products)

        def give_back(free):
            wait(PE, *free)
            banks = (2, 3, 6, 7)
            adds = []
            for f in range(KD):
                out = ps[:, banks[f // 2], f % 2 * S:(f % 2 + 1) * S]
                PE.matmul(out, y_hi[:, f * P:(f + 1) * P], pick_t[:, :], start=True, stop=False)
                mm = PE.matmul(out, y_lo[:, f * P:(f + 1) * P], pick_t[:, :], start=False, stop=True)
                if f % 2:
                    done = pe(mm)
                    wait(DVE, done)
                    c = slice(f - 1, f + 1)
                    adds.append(dve(DVE.tensor_tensor(self.xt[:, c, :], ps[:, banks[f // 2], :].rearrange("p (c s) -> p c s", c=2),
                                                      self.xt[:, c, :], ALU.add)))
            return adds

        wait(DVE, *routed)
        dve(DVE.memset(y_hi[:, :].bitcast(F32), 0.0))
        dve(DVE.memset(y_lo[:, :].bitcast(F32), 0.0))
        y_ready = dve(DVE.memset(pick_t[:, :].bitcast(F32), 0.0))
        xg_ready = split_gathered(gather(build_pick(0, []), routed))
        wait(PE, xg_ready, y_ready)

        def expert(e):
            last_split = [dve.ahead(0), act.ahead(0)]
            gate_tile(e, 0)
            s = silu_tile()
            adds = give_back(last_split)
            up_tile(e, 0)
            g = dve(DVE.tensor_copy(columns[:, 4:4 + TT], self.gates[:, :, bass.ds(e, 1)].rearrange("p t e -> p (t e)")))
            wait(PE, g, adds[1])
            for t in range(TT):
                PE.transpose(ps[:, 3, t * P:(t + 1) * P], pick[:, t, :].bitcast(F32), self.const("ident"))
            for t in range(TT):
                mm = PE.matmul(ps[:, 3, S:S + 1], pick[:, t, :].bitcast(F32), columns[:, 4 + t:5 + t], start=t == 0, stop=t == TT - 1)
            picked = pe(mm)
            wait(ACT_, picked)
            act(ACT_.activation(pick_t[:, :], ps[:, 3, 0:S], ACT.Copy))
            slot_ready = act(ACT_.activation(slot_gate[:, :], ps[:, 3, S:S + 1], ACT.Copy))
            act_tile(s)
            next_pick = build_pick(e + 1, [picked])
            wait(PE, adds[0])
            self.clear_banks((4, 5))

            def tile(turn):
                f = turn + 1
                gate_tile(e, f)
                s = silu_tile()
                turned = turn_tile(dve.ahead(0), [])
                a_ready = split_tile(turned)
                up_tile(e, f)
                act_tile(s)
                down_tile(e, f - 1, a_ready)
            self.loop(tiles - 2, {act: 2, dve: 2, pe: 1}, tile, slabs=NRAW)

            gate_tile(e, tiles - 1)
            s = silu_tile()
            a_ready = split_tile(turn_tile(dve.ahead(0), []))
            gathered = gather(next_pick, adds)
            up_tile(e, tiles - 1)
            whole_ready = act_tile(s)
            xg_ready = split_gathered(gathered)
            down_tile(e, tiles - 2, a_ready, halves=[0])
            last_ready = split_tile(turn_tile(whole_ready, [a_ready]), 1)
            down_tile(e, tiles - 2, a_ready, halves=[1])
            down_tile(e, tiles - 1, last_ready, 1)
            wait(ACT_, self.slab_used.ahead(0), slot_ready)
            both = ps[:, 4:6, :].rearrange("p b n -> p (b n)")
            high = act(ACT_.activation(y_hi[:, :], both, ACT.Copy, scale=slot_gate[:, :]))
            wait(DVE, high)
            y_ready = dve(DVE.scalar_tensor_tensor(y_lo[:, :], both, slot_gate[:, :], y_hi[:, :].bitcast(F32), ALU.mult, ALU.subtract))
            wait(PE, xg_ready)
        self.loop(NE, {act: 18, dve: 24, pe: 13}, expert, slabs=6 * tiles)
        last_split = [dve.ahead(0), act.ahead(0)]
        self.close_stream(gate_w)
        return give_back(last_split)


def build(nc, x, packed, lasting, staged, w_in, w_branch, w_o, w_gate_up, w_down, ret_w_in, ret_w_out,
          dense_gate, dense_up, dense_down, fnet_w, moe_gate, moe_up, moe_down, out, until=None, force=False):
    with ExitStack() as ctx:
        k = Kernel(nc, ctx)
        k.allocate()
        k.x_sem = ctx.enter_context(nc.semaphore("x_landed"))
        stored = ctx.enter_context(nc.semaphore("stored"))
        first_loads = []

        for tile, source in ((k.consts, lasting), (k.params, packed), (k.stage, staged[0, :, :])):
            landed = Count(ctx.enter_context(nc.semaphore(f"landed_{tile.name}")), 16)
            k.ACT.dma_start(tile[:, :], source).then_inc(landed.sem, 16)
            first_loads.append(landed)
        consts_ready, params_ready, stage_ready = first_loads
        zeroed = k.dve(k.DVE.memset(k.zero[:, :], 0.0))
        wait(k.PE, zeroed)
        wait(k.ACT, k.dve(k.DVE.memset(k.eps[:, :], EPS)))

        wait(k.PE, consts_ready)
        wait(k.DVE, consts_ready)
        x_ready = k.load_input(x)
        k.open_stream()
        for engine in (k.ACT, k.DVE, k.PE):
            wait(engine, params_ready)
        ht = k.norm("norm1", x_ready, [])
        steps_ready = k.time_steps(k.h32_ready)
        rates_ready = k.retention_rates()
        u_ready = k.project_inputs(w_in, ht)
        m_hi, m_lo, merged = k.mixers_and_merge(w_in, w_branch, u_ready, steps_ready, stage_ready)
        wait(k.POOL, *merged)
        stage_ready = k.load(k.stage[:, :], staged[1, :, :])
        x_ready = k.into_residual(w_o, lambda c: m_hi[:, c, :], lambda c: m_lo[:, c, :], KD, k.y_banks_free, merged)
        if until == "mix":
            k.close_stream(k.rows(w_o, 0))
            return finish(k, x_ready, None, out, stored)
        ht = k.norm("norm2", x_ready, [])
        x_ready = k.feed_forward(
            "1", lambda j: k.columns(w_gate_up, j * (2 * P)), lambda j: k.columns(w_gate_up, j * (2 * P) + FF),
            w_down, ht, x_ready)
        x_ready = k.norm_in_place("final1", x_ready)
        if until == "first":
            k.close_stream(k.rows(w_o, 0))
            return finish(k, x_ready, None, out, stored)

        ht = k.norm("mix0", x_ready, [])
        x_ready = k.retention(ret_w_in, ret_w_out, ht, x_ready, stage_ready, rates_ready)
        wait(k.POOL, *x_ready)
        stage_ready = k.load(k.stage[:, :], staged[2, :, :])
        if until == "ret":
            k.close_stream(k.rows(w_o, 0))
            return finish(k, x_ready, None, out, stored)
        ht = k.norm("ffn0", x_ready, [])
        x_ready = k.feed_forward(
            "2", lambda j: k.columns(dense_gate, j * (2 * P)), lambda j: k.columns(dense_up, j * (2 * P)),
            dense_down, ht, x_ready)

        ht = k.norm("mix1", x_ready, [])
        x_ready = k.fourier(fnet_w, ht, stage_ready)
        if until == "four":
            k.close_stream(k.rows(w_o, 0))
            return finish(k, x_ready, None, out, stored)
        ht = k.norm("ffn1", x_ready, [])
        routed = k.route(ht)
        x_ready = k.experts(moe_gate, moe_up, moe_down, 0, routed, "")
        for engine in (k.SP, k.POOL, k.ACT, k.DVE, k.PE):
            wait(engine, *x_ready)
        most = nc.values_load(k.most[0:1, 0:1], min_val=0, max_val=S)
        with nc.If(most > (P if not force else 1)):
            k.open_stream()
            extra = k.experts(moe_gate, moe_up, moe_down, P, routed, "_more")
            for engine in (k.SP, k.POOL, k.ACT, k.DVE, k.PE):
                wait(engine, *extra)
        k.fresh_counters("_final")
        finish(k, [], "final2", out, stored)


def finish(k, x_ready, gain, out, stored):
    if gain:
        x_ready = k.norm_in_place(gain, x_ready)
    rows = k.place("out_rows", [P, TT, D], at=k.ra)
    wait(k.PE, *x_ready)
    wait(k.ACT, *x_ready)
    for t in range(TT):
        copied = []
        for half in range(2):
            b = 2 * t + half
            for c in range(4):
                mm = k.PE.transpose(k.ps[:, b, c * P:(c + 1) * P], k.xt[:, 4 * half + c, t * P:(t + 1) * P], k.const("ident"))
            turned = k.pe(mm)
            wait(k.ACT, turned)
            copied.append(k.act(k.ACT.activation(rows[:, t, 4 * P * half:4 * P * (half + 1)], k.ps[:, b, :], ACT.Copy)))
        wait(k.SP, *copied)
        k.SP.dma_start(out[0, t * P:(t + 1) * P, :], rows[:, t, :]).then_inc(stored, 16)
    k.SP.wait_ge(stored, 16 * TT)


_WEIGHTS = ["w_in", "w_branch", "w_o", "w_gate_up", "w_down", "ret_w_in_2", "ret_w_out_2", "dense_w_gate_2",
            "dense_w_up_2", "dense_w_down_2", "fnet_w_out_2", "moe_w_gate_2", "moe_w_up_2", "moe_w_down_2"]


def pack_parameters(v):
    def chunks(a):
        return np.ascontiguousarray(a).reshape(-1, P).T

    def everywhere(a):
        return np.broadcast_to(np.ascontiguousarray(a).reshape(1, -1), (P, a.size))

    def per_head(a):
        return np.repeat(a, HD).reshape(2, P).T

    taps = lambda w: w.reshape(w.shape[-2], -1, P).transpose(2, 1, 0).reshape(P, -1)
    rows = lambda w: w.reshape(KD, P, -1).transpose(1, 0, 2).reshape(P, -1)
    twice = lambda a: np.concatenate([a.reshape(-1), a.reshape(-1)])
    parts = dict(
        norm1=chunks(v["norm1_g"]), norm2=chunks(v["norm2_g"]), mix0=chunks(v["mix_norm_2"][0]),
        mix1=chunks(v["mix_norm_2"][1]), ffn0=chunks(v["ffn_norm_2"][0]), ffn1=chunks(v["ffn_norm_2"][1]),
        final1=chunks(v["final_g"]), final2=chunks(v["final_norm_2"]),
        ssm_taps=taps(v["ssm_conv_w"]), a_taps=taps(v["conv_a_w"]), ssm_bias=chunks(v["ssm_conv_b"]),
        dt_bias=everywhere(twice(v["ssm_dt_bias"])), a_log=everywhere(twice(v["ssm_a_log"])),
        skip=per_head(v["ssm_d"].reshape(-1)), ssm_norm=chunks(v["ssm_norm_g"]), gn_gain=chunks(v["ret_gn_gain_2"]),
        decay=everywhere(v["ret_decay_logit_2"]), w_dt=rows(v["w_in"][0, :, COL_DT:COL_DT + NH]),
        router=rows(v["moe_router_2"][0]))
    return np.ascontiguousarray(np.concatenate([parts[name] for name in PARAMS], 1))


def kernel(**inputs):
    import concourse.bacc as _bacc
    from concourse.bass_utils import run_bass_kernel_spmd as _run

    v = {name: np.asarray(a) for name, a in inputs.items()}
    nc = _bacc.Bacc("TRN2", target_bir_lowering=False, num_devices=1)
    lasting, staged = host_constants()
    arrays = {"x": v["x"], "params": pack_parameters(v), "lasting": lasting, "staged": staged}
    arrays.update({name: v[name] for name in _WEIGHTS})
    arrays = {f"in_{name}": np.ascontiguousarray(a) for name, a in arrays.items()}
    args = []
    for name, a in arrays.items():
        t = nc.dram_tensor(name, a.shape, mybir.dt.from_np(a.dtype), kind="ExternalInput").ap()
        short = name[3:]
        if short in ("w_in", "w_o", "w_gate_up", "w_down", "ret_w_in_2", "ret_w_out_2", "dense_w_gate_2",
                     "dense_w_up_2", "dense_w_down_2", "fnet_w_out_2"):
            t = t.rearrange("a k n -> (a k) n")
        args.append(t)
    args.append(nc.dram_tensor("out", (1, S, D), F32, kind="ExternalOutput").ap())
    build(nc, *args)
    r = _run(nc, [arrays], core_ids=[0])
    return r.results[0]["out"]
```

```python
from contextlib import ExitStack

import numpy as np

import concourse.bass as bass
from concourse import mybir

F32 = mybir.dt.float32
F32R = mybir.dt.float32r
BF16 = mybir.dt.bfloat16
I32 = mybir.dt.int32
ACT = mybir.ActivationFunctionType
ALU = mybir.AluOpType
AX = mybir.AxisListType

P = 128
S = 256
TT = S // P
D = 1024
KD = D // P
NH = 4
HD = 64
BW = 256
FF = 2816
NE = 8
FE = 3584
EPS = 1e-6
NEG = -1e30

COL_A, COL_B, COL_Z, COL_XBC, COL_DT = 0, 768, 1536, 1792, 2304
COL_D, COL_G = 2308, 3076

SLAB = 2048
NRAW = 6
NSPLIT = 3
LEAD = 2
START = 8

PARAMS = {}
_at = 0
for _name, _n in [("norm1", KD), ("norm2", KD), ("mix0", KD), ("mix1", KD), ("ffn0", KD), ("ffn1", KD),
                  ("final1", KD), ("final2", KD), ("ssm_taps", 16), ("a_taps", 6), ("ssm_bias", 4),
                  ("dt_bias", 8), ("a_log", 8), ("skip", 2), ("ssm_norm", 2), ("gn_gain", 16),
                  ("decay", 8), ("w_dt", KD * NH), ("router", KD * NE)]:
    PARAMS[_name] = (_at, _n)
    _at += _n
NPARAM = _at

CONSTS = {}
_at = 0
for _name, _n in [("ident", P), ("suffix", P), ("prefix", P), ("ones", P), ("before", P),
                  ("slot", 2 * P), ("order", NE)]:
    CONSTS[_name] = (_at, _n)
    _at += _n
NCONST = _at
NSTAGE = 1536


def host_constants():
    f = np.float32
    p = np.arange(P)[:, None]
    q = np.arange(P)[None, :]
    s = np.arange(S)[None, :]
    lasting = [np.eye(P), p >= q, p <= q, np.ones((P, P)), p < q,
               np.broadcast_to(s, (P, S)), np.broadcast_to(NE - np.arange(NE)[None, :], (P, NE))]
    lasting = np.concatenate([a.astype(f) for a in lasting], 1)
    strict = np.concatenate([np.where(p < s, 0, NEG), np.where(p < q, 0, NEG)], 1)
    causal = np.concatenate([np.where(q <= p, 0, NEG), np.where(s <= p + P, 0, NEG)], 1)
    ssm = np.concatenate([np.where(s >= p, 0, NEG), np.where(q >= p, 0, NEG)], 1)
    one = np.concatenate([strict, causal, ssm, np.zeros((P, NSTAGE - 1152))], 1).astype(f)
    inv = np.power(f(10000.0), -np.arange(P, dtype=f) / f(P)).astype(f)
    ang = (np.arange(S, dtype=f)[None, :] * inv[:, None]).astype(f).astype(np.float64)
    dist = np.concatenate([s - p, s - p - P], 1)
    two = np.concatenate([np.cos(ang), np.sin(ang), np.maximum(dist, 0), np.maximum(-dist, 0)], 1).astype(f)
    w = 2 * np.pi * ((np.arange(S)[:, None] * np.arange(S)[None, :]) % S) / S
    cs = np.concatenate([np.cos(w), np.sin(w)], 1).reshape(2, P, 2 * S).transpose(1, 0, 2).reshape(P, -1) / 16
    ns = (-np.sin(w)).reshape(2, P, S).transpose(1, 0, 2).reshape(P, -1) / 16
    three = np.concatenate([cs, ns], 1).astype(f)
    return lasting, np.stack([one, two, three])


class Loop:

    def __init__(self, trips):
        self.trips, self.turn = trips, None


class Count:

    def __init__(self, sem, const, steps=()):
        self.sem, self.const, self.steps = sem, const, tuple(steps)

    def value(self):
        out = self.const
        for loop, step in self.steps:
            out = out + (loop.turn if loop.turn is not None else loop.trips - 1) * step
        return out


class Done:

    def __init__(self, nc, ctx, name, engine, step=1):
        self.sem, self.step, self.n, self.steps = ctx.enter_context(nc.semaphore(name)), step, START, []
        engine.sem_inc(self.sem, START)

    def __call__(self, instruction):
        instruction.then_inc(self.sem, self.step)
        self.n += self.step
        return Count(self.sem, self.n, self.steps)

    def ahead(self, k):
        return Count(self.sem, self.n + k * self.step, self.steps)


def wait(engine, *counts):
    last = {}
    for c in counts:
        known = last.get(id(c.sem))
        if known is None:
            last[id(c.sem)] = c
        elif known.steps == c.steps:
            last[id(c.sem)] = c if c.const > known.const else known
        else:
            engine.wait_ge(c.sem, c.value())
    for c in last.values():
        engine.wait_ge(c.sem, c.value())


def stationary_pair(pe, out, w_hi, w_lo, x_hi, x_lo, start, stop, **kw):
    pe.matmul(out, w_hi, x_hi, start=start, stop=False, **kw)
    pe.matmul(out, w_hi, x_lo, start=False, stop=False, **kw)
    return pe.matmul(out, w_lo, x_hi, start=False, stop=stop, **kw)


class Kernel:
    def __init__(self, nc, ctx):
        self.nc, self.ctx = nc, ctx
        self.PE, self.ACT, self.DVE, self.POOL, self.SP = nc.tensor, nc.scalar, nc.vector, nc.gpsimd, nc.sync
        self.at = 16512

    def place(self, name, shape, dtype=F32, at=None):
        size = int(np.prod(shape[1:])) * mybir.dt.size(dtype)
        if at is None:
            at = self.at
            self.at += -(-size // 32) * 32
        return self.nc.alloc_sbuf_tensor_at(name, shape, dtype, offset=at)

    def region(self, size):
        at = self.at
        self.at += size
        return at

    def fresh_counters(self, tag):
        c, nc = self.ctx, self.nc
        self.pe = Done(nc, c, f"pe_done{tag}", self.PE)
        self.act = Done(nc, c, f"act_done{tag}", self.ACT)
        self.dve = Done(nc, c, f"dve_done{tag}", self.DVE)
        self.dve_turns = Done(nc, c, f"dve_turns_done{tag}", self.DVE)

    def loop(self, trips, per, body, slabs=0):
        per = dict(per)
        counters = list(per)
        if slabs:
            for c in (self.split_hi, self.split_lo, self.slab_used):
                counters.append(c)
                per[c] = slabs
        loop = Loop(trips)
        starts = {c: c.n for c in counters}
        others = {c: c.n for c in self.all_counters() if c not in per}
        for c in counters:
            c.steps.append((loop, per[c] * c.step))
        slab0 = self.slab
        if slabs:
            assert slabs % NRAW == 0 and slabs % NSPLIT == 0
            self.slab_steps.append((loop, slabs))
        with self.nc.Fori(0, trips) as turn:
            loop.turn = turn
            body(turn)
        loop.turn = None
        for c in counters:
            assert c.n - starts[c] == per[c] * c.step, (c.sem, c.n - starts[c], per[c] * c.step)
            c.steps.pop()
            c.n = starts[c] + per[c] * c.step * trips
        for c, n in others.items():
            assert c.n == n, ("not declared", c.sem)
        assert self.slab - slab0 == slabs
        if slabs:
            self.slab_steps.pop()
            self.slab = slab0 + slabs * trips

    def all_counters(self):
        return [self.pe, self.act, self.dve, self.dve_turns, self.split_hi, self.split_lo, self.slab_used]

    def raw_landed(self, ahead):
        n = self.slab + ahead
        return Count(self.raw_sems[n % NRAW], 16 * (n // NRAW + 1),
                     [(l, 16 * k // NRAW) for l, k in self.slab_steps])

    def split(self, ahead):
        n = self.slab + ahead
        raw, hi, lo = self.raw[:, n % NRAW, :], self.w_hi[:, n % NSPLIT, :], self.w_lo[:, n % NSPLIT, :]
        wait(self.ACT, self.raw_landed(ahead),
             self.slab_used.ahead(ahead - NSPLIT + 1))
        hi_ready = self.split_hi(self.ACT.activation(hi, raw, ACT.Copy))
        wait(self.DVE, hi_ready)
        self.split_lo(self.DVE.tensor_tensor(lo, raw, hi.bitcast(F32), ALU.subtract))

    def slab_step(self, source, products, split_later=False):
        n = self.slab
        if n >= NRAW or self.slab_steps:
            wait(self.SP, self.split_lo.ahead(1 - self.split_ahead - NRAW))
        k = source.shape[1]
        self.SP.dma_start(self.raw[:, n % NRAW, :].rearrange("p (k n) -> p k n", k=k), source)\
            .then_inc(self.raw_sems[n % NRAW], 16)
        if split_later:
            self.split_ahead -= 1
        else:
            self.split(LEAD)
        wait(self.PE, self.split_lo.ahead(-self.split_ahead))
        hi = self.w_hi[:, n % NSPLIT, :].rearrange("p (k n) -> p k n", k=k)
        lo = self.w_lo[:, n % NSPLIT, :].rearrange("p (k n) -> p k n", k=k)
        self.slab_used(products(hi, lo))
        self.slab += 1

    def split_left(self):
        if self.split_ahead == LEAD - 1:
            self.split(LEAD - 1)
            self.split_ahead = LEAD

    def open_stream(self):
        for ahead in range(LEAD):
            self.split(ahead)
        self.split_ahead = LEAD

    def close_stream(self, source):
        for ahead in range(LEAD):
            wait(self.SP, self.split_lo.ahead(1 - LEAD - NRAW + ahead))
            slot = (self.slab + ahead) % NRAW
            self.SP.dma_start(self.raw[:, slot:slot + 1, 0:P], source[:, 0:1, 0:P]).then_inc(self.raw_sems[slot], 16)
        wait(self.PE, self.split_lo.ahead(0))
        self.PE.drain().then_inc(self.slab_used.sem, LEAD)
        self.slab_used.n += LEAD
        self.slab += LEAD
        self.split_ahead = 0

    def allocate(self):
        nc, ctx, place = self.nc, self.ctx, self.place
        self.raw = place("raw", [P, NRAW, SLAB])
        self.w_hi = place("w_hi", [P, NSPLIT, SLAB], F32R)
        self.w_lo = place("w_lo", [P, NSPLIT, SLAB], F32R)
        self.xt = place("xt", [P, KD, S])
        self.ht_hi = place("ht_hi", [P, KD, S], F32R)
        self.ht_lo = place("ht_lo", [P, KD, S], F32R)
        self.params = place("params", [P, NPARAM])
        self.consts = place("consts", [P, NCONST])
        self.stage = place("stage", [P, NSTAGE])
        self.small = place("small", [P, 96])
        self.zero = place("zero", [P, P], BF16)
        self.eps = place("eps", [P, 1])
        self.junk = place("junk", [P, 1])
        self.root = place("root", [P, TT])
        self.ra = self.region(24 * 2 * S * 4)
        self.rb = self.region(2 * KD * S * 4)
        self.rc = self.region(8256)
        self.rd = self.region(4160)
        self.sq = place("sq", [P, KD, S], at=self.rc)
        self.h32 = place("h32", [P, KD, S], at=self.rc)
        self.spread = place("spread", [P, TT, P], at=self.rd)
        self.ps = ctx.enter_context(nc.psum_tensor("ps", [P, 8, 512], F32))
        self.rstd = self.ps[:, 7, S:2 * S]
        self.split_hi = Done(nc, ctx, "split_hi_done", self.ACT)
        self.split_lo = Done(nc, ctx, "split_lo_done", self.DVE)
        self.slab_used = Done(nc, ctx, "slab_used", self.PE)
        self.raw_sems = [ctx.enter_context(nc.semaphore(f"raw_landed{i}")) for i in range(NRAW)]
        self.slab, self.slab_steps, self.split_ahead = 0, [], 0
        self.squares = {}
        self.fresh_counters("")
        self.load_sem = ctx.enter_context(nc.semaphore("small_loads"))
        self.loads = 0

    def load(self, out, source):
        self.POOL.dma_start(out, source).then_inc(self.load_sem, 16)
        self.loads += 16
        c = Count(self.load_sem, self.loads)
        wait(self.POOL, c)
        return c

    def param(self, name, i=0, n=1):
        at, _ = PARAMS[name]
        return self.params[:, at + i:at + i + n]

    def const(self, name, n=None):
        at, width = CONSTS[name]
        return self.consts[:, at:at + (n or width)]

    def ready_table(self, func):
        self.ACT.activation(self.junk[:, :], self.eps[:, :], func)

    def square(self, b, x_ready):
        c = slice(2 * b, 2 * b + 2)
        wait(self.ACT, x_ready)
        self.squares[b] = self.act(self.ACT.activation(self.sq[:, c, :], self.xt[:, c, :], ACT.Square))

    def add_square(self, b):
        wait(self.DVE, self.squares[b], self.squares[0] if b == 1 else self.dve.ahead(0))
        added = self.dve(self.DVE.tensor_tensor(self.sq[:, 0:2, :], self.sq[:, 0:2, :], self.sq[:, 2 * b:2 * b + 2, :], ALU.add))
        if b == KD // 2 - 1:
            wait(self.DVE, added)
            self.squares["sum"] = self.dve(self.DVE.tensor_tensor(self.sq[:, 0, :], self.sq[:, 0, :], self.sq[:, 1, :], ALU.add))

    def norm_factor(self, x_ready, meanwhile=None):
        ps = self.ps[:, 7, :]
        if "sum" not in self.squares:
            for b in range(KD // 2):
                self.square(b, x_ready[(b + 1) * len(x_ready) // 4 - 1] if x_ready else self.dve.ahead(0))
            for b in range(1, KD // 2):
                self.add_square(b)
        if meanwhile:
            meanwhile()
        wait(self.PE, self.squares["sum"])
        if len(x_ready) == KD:
            wait(self.PE, x_ready[-1])
        self.squares = {}
        for t in range(TT):
            mm = self.PE.matmul(ps[:, t:t + 1], self.sq[:, 0, t * P:(t + 1) * P], self.const("ones", 1), start=True, stop=True)
        summed = self.pe(mm)
        wait(self.ACT, summed)
        root = self.act(self.ACT.activation(self.root[:, :], ps[:, 0:TT], ACT.Sqrt, scale=1.0 / D, bias=self.eps[:, :]))
        wait(self.DVE, root)
        inverse = self.dve(self.DVE.reciprocal(self.root[:, :], self.root[:, :]))
        wait(self.DVE, inverse)
        for t in range(TT):
            spread = self.dve(self.DVE.tensor_scalar(self.spread[:, t, :], self.const("ones"), self.root[:, t:t + 1], None, ALU.mult))
        wait(self.PE, spread)
        for t in range(TT):
            mm = self.PE.matmul(ps[:, S + t * P:S + (t + 1) * P], self.spread[:, t, :], self.const("ident"), start=True, stop=True)
        return self.pe(mm)

    def norm(self, gain, x_ready, ht_free, meanwhile=None, whole_only=False):
        wait(self.DVE, self.norm_factor(x_ready, meanwhile))
        highs, ready, self.h32_ready = [], [], []

        def low_part(k):
            wait(self.DVE, highs[k // 2])
            ready.append(self.dve(self.DVE.tensor_tensor(
                self.ht_lo[:, k:k + 2, :], self.h32[:, k:k + 2, :], self.ht_hi[:, k:k + 2, :].bitcast(F32), ALU.subtract)))
        for k in range(0, KD, 2):
            for c in (k, k + 1):
                whole = self.dve(self.DVE.scalar_tensor_tensor(
                    self.h32[:, c, :], self.xt[:, c, :], self.param(gain, c), self.rstd, ALU.mult, ALU.mult))
                self.h32_ready.append(whole)
            if whole_only:
                continue
            wait(self.ACT, whole, *ht_free)
            highs.append(self.act(self.ACT.activation(self.ht_hi[:, k:k + 2, :], self.h32[:, k:k + 2, :], ACT.Copy)))
            if k:
                low_part(k - 2)
        if whole_only:
            self.split_left()
            return self.h32_ready
        low_part(KD - 2)
        self.split_left()
        self.ht_highs = highs
        return ready

    def split_from(self, hi, lo, source, source_ready, free=(), done=None):
        wait(self.ACT, source_ready, *free)
        high = self.act(self.ACT.activation(hi, source, ACT.Copy))
        wait(self.DVE, high)
        return (done or self.dve)(self.DVE.tensor_tensor(lo, source, hi.bitcast(F32), ALU.subtract))

    def columns(self, weight, start, n=2 * P):
        return weight.rearrange("(k p) n -> p k n", p=P)[:, :, bass.ds(start, n)]

    def rows(self, weight, start):
        return weight.rearrange("(k p) n -> p k n", p=P)[:, bass.ds(start, 2), :]

    def feature_major(self, bank, ht_ready=()):
        out = lambda c: self.ps[:, bank, c * S:(c + 1) * S]
        def products(hi, lo):
            for c in range(2):
                for k in range(KD):
                    mm = stationary_pair(self.PE, out(c), hi[:, k, c * P:(c + 1) * P], lo[:, k, c * P:(c + 1) * P],
                                         self.ht_hi[:, k, :], self.ht_lo[:, k, :], k == 0, k == KD - 1)
            return mm
        highs = self.ht_highs
        def products_as_ht_comes(hi, lo):
            self.clear_banks([bank])
            for k in range(0, KD, 2):
                for x, w_parts, ready in ((self.ht_hi, (hi, lo), highs), (self.ht_lo, (hi,), ht_ready)):
                    wait(self.PE, ready[k // 2])
                    for c in range(2):
                        for kk in (k, k + 1):
                            for w in w_parts:
                                mm = self.PE.matmul(out(c), w[:, kk, c * P:(c + 1) * P], x[:, kk, :],
                                                    start=False, stop=False, skip_group_check=True)
            return mm
        if ht_ready:
            return products_as_ht_comes
        return products

    def clear_banks(self, banks):
        for b in banks:
            self.PE.matmul(self.ps[:, b, :].rearrange("p (a n) -> p a n", n=P), self.zero[:, :],
                           self.zero[:, :].unsqueeze(1).to_broadcast([P, 4, P]), start=True, stop=True)

    def residual_open(self, bank, banks_free):
        wait(self.PE, *banks_free)
        self.clear_banks(range(bank, bank + 4))
        self.sum_bank, self.banks_done = bank, []

    def residual_step(self, weight, y_hi, y_lo, start, y_ready, last=False):
        wait(self.PE, *y_ready)
        def products(hi, lo):
            pairs = [(k, f) for k in range(2) for f in range(KD)] if not last else \
                [(k, 2 * b + f) for b in range(4) for k in range(2) for f in range(2)]
            for k, f in pairs:
                mm = stationary_pair(
                    self.PE, self.ps[:, self.sum_bank + f // 2, f % 2 * S:(f % 2 + 1) * S],
                    hi[:, k, f * P:(f + 1) * P], lo[:, k, f * P:(f + 1) * P],
                    y_hi(start + k), y_lo(start + k), False, False, skip_group_check=True)
                if last and k == 1 and f % 2 and f < KD - 1:
                    self.banks_done.append(self.pe(mm))
            return mm
        self.slab_step(self.rows(weight, start), products, split_later=last)

    def residual_close(self):
        self.banks_done.append(self.slab_used.ahead(0))
        ready = []
        self.ready_table(ACT.Sqrt)
        for b in range(4):
            wait(self.DVE, self.banks_done[b])
            ready.append(self.dve(self.DVE.tensor_tensor(
                self.xt[:, 2 * b:2 * b + 2, :], self.ps[:, self.sum_bank + b, :].rearrange("p (c s) -> p c s", c=2),
                self.xt[:, 2 * b:2 * b + 2, :], ALU.add)))
            self.square(b, ready[b])
            if b >= 2:
                self.add_square(b - 1)
        self.add_square(3)
        return ready

    def into_residual(self, weight, y_hi, y_lo, chunks, bank, banks_free, y_ready):
        self.residual_open(bank, banks_free)
        for i in range(chunks // 2):
            self.residual_step(weight, y_hi, y_lo, 2 * i, y_ready[i:i + 1], i == chunks // 2 - 1)
        return self.residual_close()

    def load_input(self, x):
        rows = self.place("x_rows", [P, TT, D], at=self.ra)
        for half, sem in enumerate(self.x_sems):
            c = slice(half * D // 2, (half + 1) * D // 2)
            self.SP.dma_start(rows[:, :, c], x.rearrange("a (t p) d -> p (a t) d", p=P)[:, :, c]).then_inc(sem, 16)
        ready = []
        for k in range(0, KD, 2):
            wait(self.PE, Count(self.x_sems[k // (KD // 2)], 16))
            for c in (k, k + 1):
                for t in range(TT):
                    mm = self.PE.transpose(self.ps[:, k // 2, (c - k) * S + t * P:(c - k) * S + (t + 1) * P],
                                           rows[:, t, c * P:(c + 1) * P], self.const("ident"))
            turned = self.pe(mm)
            wait(self.DVE, turned)
            ready.append(self.dve(self.DVE.tensor_copy(
                self.xt[:, k:k + 2, :], self.ps[:, k // 2, :].rearrange("p (c s) -> p c s", c=2))))
        return ready

    def project_inputs(self, w_in, ht_ready):
        self.u = u = self.place("u", [P, 24, S], at=self.ra)
        def body(turn):
            for j in range(NRAW):
                start = turn * (NRAW * BW + (COL_D - COL_DT if j >= 3 else 0)) + j * BW
                engine, done = (self.ACT, self.act) if j % 2 == 0 else (self.DVE, self.dve)
                wait(self.PE, done.ahead(1 - NRAW // 2))
                self.slab_step(self.columns(w_in, start), self.feature_major(j, ht_ready if j == 0 else ()))
                out = u[:, bass.ds(turn * 12 + 2 * j, 2), :]
                whole = self.ps[:, j, :].rearrange("p (c s) -> p c s", c=2)
                wait(engine, self.slab_used.ahead(0))
                done(engine.activation(out, whole, ACT.Copy) if j % 2 == 0 else engine.tensor_copy(out, whole))
        self.loop(2, {self.act: NRAW // 2, self.dve: NRAW // 2}, body, slabs=NRAW)
        return [self.act.ahead(0), self.dve.ahead(0)]

    def token_major(self, bank, chunks, out, ready, free=()):
        wait(self.PE, *ready, *free)
        for t in range(TT):
            for c in range(2):
                mm = self.PE.transpose(self.ps[:, bank, t * S + c * P:t * S + (c + 1) * P],
                                       self.u[:, chunks + c, t * P:(t + 1) * P], self.const("ident"))
        turned = self.pe(mm)
        wait(self.ACT, turned)
        return self.act(self.ACT.activation(out, self.ps[:, bank, :].rearrange("p (t f) -> p t f", t=TT), ACT.Copy))

    def softplus(self, out, x, x_ready, scratch):
        wait(self.ACT, x_ready)
        a = self.act(self.ACT.activation(scratch, x, ACT.Abs))
        wait(self.ACT, a)
        b = self.act(self.ACT.activation(scratch, scratch, ACT.Exp, scale=-1.0))
        wait(self.ACT, b)
        c = self.act(self.ACT.activation(scratch, scratch, ACT.Ln, bias=1.0))
        wait(self.DVE, c)
        return self.dve(self.DVE.scalar_tensor_tensor(out, x, 0.0, scratch, ALU.max, ALU.add))

    def wide(self, a, h, n=1):
        out = a[:, h * S:(h + n) * S]
        return out.rearrange("p (h s) -> p h s", h=n) if n > 1 else out

    def tail(self, a, h, n=1):
        out = a[:, NH * S + h * P:NH * S + (h + n) * P]
        return out.rearrange("p (h s) -> p h s", h=n) if n > 1 else out

    def banks(self, first, n=3):
        return self.ps[:, first:first + n, :].rearrange("p b n -> p (b n)")

    def time_step_logits(self, h32_ready):
        PE, DVE = self.PE, self.DVE
        for t in range(TT):
            for k in range(KD):
                wait(PE, h32_ready[k])
                mm = PE.matmul(self.ps[:, 6, t * NH:(t + 1) * NH], self.h32[:, k, t * P:(t + 1) * P],
                               self.param("w_dt", k * NH, NH), start=k == 0, stop=k == KD - 1)
        dts = self.pe(mm)
        x = self.small[:, 16:32]
        self.dve(DVE.tensor_copy(x[:, 8:16], self.param("decay", 0, 8)))
        wait(DVE, dts)
        return self.dve(DVE.tensor_tensor(x[:, 0:8], self.ps[:, 6, 0:8], self.param("dt_bias", 0, 8), ALU.add))

    def time_steps(self, logits_ready):
        ACT_, DVE, small = self.ACT, self.DVE, self.small
        x, scratch, rate = small[:, 16:32], small[:, 72:88], small[:, 40:48]
        dt, step, ln_gamma = small[:, 16:24], small[:, 32:40], small[:, 64:72]
        wait(ACT_, logits_ready)
        a = self.act(ACT_.activation(scratch, x, ACT.Abs))
        wait(ACT_, a)
        a = self.act(ACT_.activation(scratch, scratch, ACT.Exp, scale=-1.0))
        exp_a = self.act(ACT_.activation(rate, self.param("a_log", 0, 8), ACT.Exp))
        wait(ACT_, a)
        a = self.act(ACT_.activation(scratch, scratch, ACT.Ln, bias=1.0))
        wait(DVE, a)
        rates_ready = self.dve(DVE.scalar_tensor_tensor(ln_gamma, x[:, 8:16], 0.0, scratch[:, 8:16], ALU.min, ALU.subtract))
        dt_ready = self.dve(DVE.scalar_tensor_tensor(dt, dt, 0.0, scratch[:, 0:8], ALU.max, ALU.add))
        wait(DVE, exp_a, dt_ready)
        return self.dve(DVE.scalar_tensor_tensor(step, dt, -1.0, rate, ALU.mult, ALU.mult)), rates_ready

    def weighted_values(self, bank, weights, values, ready):
        wait(self.PE, *ready)
        for h in range(NH):
            low = h % 2 * HD
            out = self.ps[low:low + HD, bank + h // 2, :]
            v = lambda t: values[:, t, h * HD:(h + 1) * HD]
            self.PE.matmul(out[:, 0:S], v(0), self.wide(weights, h), start=True, stop=False)
            mm = self.PE.matmul(out[:, P:S], v(1), self.tail(weights, h), start=False, stop=True)
        return self.pe(mm)

    def mixers_and_merge(self, w_in, w_branch, u_ready, steps_ready, masks_ready):
        PE, ACT_, DVE, pe, act, dve, u, ps = self.PE, self.ACT, self.DVE, self.pe, self.act, self.dve, self.u, self.ps
        wide, tail, banks = self.wide, self.tail, self.banks
        y_hi = self.place("y_hi", [P, KD, S], F32R, at=self.rb)
        y_lo = self.place("y_lo", [P, KD, S], F32R, at=self.rb + KD * S * 4)
        zb = self.place("sb_scores", [P, NSTAGE], at=self.ra + 24576)
        sb = self.place("sb_softplus", [P, NSTAGE], at=self.ra + 24576 + 6144)
        zd = self.place("moba_scores", [P, NSTAGE], at=self.ra + 24576 + 12288)
        pd = self.place("moba_turned", [P, NSTAGE], at=self.ra + 24576 + 18432)
        vb = self.place("sb_values", [P, TT, BW], at=self.rc)
        vd = self.place("moba_values", [P, TT, BW], at=self.rc + 2048)
        xd = self.place("ssm_values", [P, TT, BW], at=self.rc)
        ap = self.place("a_padded", [P, 2, S + 2], at=self.rc + 6144)
        cp = self.place("xbc_padded", [P, 4, S + 3], at=self.rd)
        tri = self.place("ssm_steps", [P, NSTAGE], at=self.ra + 18 * 1024)
        dm = self.place("ssm_decay", [P, NSTAGE], at=self.ra + 6 * 1024)
        small, dt, step, before = self.small, self.small[:, 16:24], self.small[:, 32:40], self.small[:, 48:56]
        top, total = small[:, 0:8], small[:, 8:16]
        W3 = S + P
        strict_wide, strict_tail = self.stage[:, 0:S], self.stage[:, S:W3]
        causal_tail, causal_wide = self.stage[:, W3:W3 + P], self.stage[:, W3 + P:2 * W3]
        ssm_wide, ssm_tail = self.stage[:, 2 * W3:2 * W3 + S], self.stage[:, 2 * W3 + S:3 * W3]
        over_heads = lambda a: a.unsqueeze(1).to_broadcast([P, NH, a.shape[-1]])
        pair = lambda a: a.rearrange("p (c s) -> p c s", c=2)

        first_gate = self.place("gate_0", [P, 2, S], at=self.rc + 4096)
        later = self.place("gate_store", [P, 12, 2, S], at=self.ra + 24576)
        order = (3, 0, 1, 2)
        slots = [first_gate[:, :, :]] + [u[:, 2 * j:2 * j + 2, :] for j in range(3)] + \
            [later[:, j, :, :] for j in range(12)]
        bank_read, gates = {6: None, 7: None}, []
        slabs_done = []

        def gate_slab():
            n = len(slabs_done)
            bank = 6 + n % 2
            wait(PE, bank_read[bank])
            self.slab_step(self.columns(w_in, COL_G + order[n // 4] * D + n % 4 * 2 * P), self.feature_major(bank))
            slabs_done.append(self.slab_used.ahead(0))

        def gate_out(slot_free, raw=True):
            n = len(gates)
            wait(ACT_, slabs_done[n], *slot_free)
            bank_read[6 + n % 2] = act(ACT_.activation(slots[n], pair(ps[:, 6 + n % 2, :]), ACT.Copy if raw else ACT.Sigmoid))
            gates.append(bank_read[6 + n % 2])

        y_parts = {}
        branch_rows = w_branch.rearrange("a b (k p) n -> p (a b k) n", p=P)

        term_bank = lambda n: (n + 2) % 6
        used = []

        def branch_slab(place, banks_read=()):
            i = order[place]
            def products(hi, lo):
                for f in range(KD):
                    n = 4 * place + f // 2
                    if f % 2 == 0 and n >= 6:
                        wait(PE, used[n - 6])
                    for k in range(2):
                        mm = stationary_pair(PE, ps[:, term_bank(n), f % 2 * S:(f % 2 + 1) * S],
                                             hi[:, k, f * P:(f + 1) * P], lo[:, k, f * P:(f + 1) * P],
                                             y_hi[:, 2 * i + k, :], y_lo[:, 2 * i + k, :], k == 0, k == 1)
                return mm
            wait(PE, y_parts[i], *banks_read)
            self.slab_step(branch_rows[:, 2 * i:2 * i + 2, :], products)
            return self.slab_used.ahead(0)

        wait(PE, steps_ready, *u_ready)
        PE.matmul(ps[:, 5, 0:4], self.const("prefix"), step[:, 0:4], start=True, stop=True)
        PE.matmul(ps[:, 5, 4:8], self.const("ones"), step[:, 0:4], start=True, stop=False)
        summed = pe(PE.matmul(ps[:, 5, 4:8], self.const("prefix"), step[:, 4:8], start=False, stop=True))
        wait(DVE, summed)
        before_ready = dve(DVE.tensor_scalar(before, ps[:, 5, 0:8], -1.0, None, ALU.mult))

        for h in (0, 2, 1, 3):
            if h == 1:
                wait(PE, pe(mm))
            r = slice(h % 2 * HD, h % 2 * HD + HD)
            q, k = u[r, 6 + h // 2, :], u[r, 8 + h // 2, :]
            PE.matmul(wide(banks(0), h), k[:, 0:P], q, start=True, stop=True)
            mm = PE.matmul(tail(banks(0), h), k[:, P:S], q[:, P:S], start=True, stop=True)
        scores_b = pe(mm)
        bank_read[6] = vb_ready = self.token_major(6, 10, vb[:, :, :], [])
        bank_read[7] = vd_ready = self.token_major(7, 22, vd[:, :, :], [])
        wait(PE, before_ready)
        for h in (0, 2, 1, 3):
            if h == 1:
                wait(PE, pe(mm))
            r = slice(h % 2 * HD, h % 2 * HD + HD)
            q, k = u[r, 18 + h // 2, :], u[r, 20 + h // 2, :]
            PE.matmul(tail(banks(3), h), q[:, 0:P], k[:, 0:P], start=True, stop=True)
            mm = PE.matmul(wide(banks(3), h), q[:, P:S], k, start=True, stop=True)
        scores_d = pe(mm)
        wait(DVE, scores_b, masks_ready)
        dve(DVE.scalar_tensor_tensor(wide(zb, 0, NH), wide(banks(0), 0, NH), HD ** -0.5, over_heads(strict_wide), ALU.mult, ALU.add))
        zb_ready = dve(DVE.scalar_tensor_tensor(tail(zb, 0, NH), tail(banks(0), 0, NH), HD ** -0.5, over_heads(strict_tail), ALU.mult, ALU.add))
        wait(DVE, scores_d)
        dve(DVE.scalar_tensor_tensor(tail(zd, 0, NH), tail(banks(3), 0, NH), HD ** -0.5, over_heads(causal_tail), ALU.mult, ALU.add))
        zd_ready = dve(DVE.scalar_tensor_tensor(wide(zd, 0, NH), wide(banks(3), 0, NH), HD ** -0.5, over_heads(causal_wide), ALU.mult, ALU.add))
        gate_slab()
        self.ready_table(ACT.Exp)

        wait(DVE, zd_ready)
        dve(DVE.tensor_reduce(top[:, 0:4], tail(zd, 0, NH), AX.X, ALU.max))
        tops = dve(DVE.tensor_reduce(top[:, 4:8], wide(zd, 0, NH), AX.X, ALU.max))
        wait(DVE, tops)
        negated = dve(DVE.tensor_scalar(top, top, -1.0, None, ALU.mult))

        wait(DVE, *u_ready)
        dve(DVE.memset(ap[:, :, 0:2], 0.0))
        last = dve(DVE.tensor_tensor(ap[:, :, 2:S + 2], u[:, 4:6, :], u[:, 0:2, :], ALU.mult))
        wait(DVE, last)
        tap = lambda c, j: self.param("a_taps", 3 * c + j)
        for j in range(3):
            for c in range(2):
                if j == 0:
                    last = dve(DVE.tensor_scalar(u[:, c, :], ap[:, c, 0:S], tap(c, 0), None, ALU.mult))
                else:
                    last = dve(DVE.scalar_tensor_tensor(u[:, c, :], ap[:, c, j:j + S], tap(c, j), u[:, c, :], ALU.mult, ALU.add))
            wait(DVE, last)
        ya = dve(DVE.tensor_tensor(u[:, 0:2, :], u[:, 0:2, :], u[:, 2:4, :], ALU.mult))

        sp_ready = self.softplus(sb[:, :], zb[:, :], zb_ready, sb[:, :])
        gate_slab()
        gate_out([])
        y_parts[0] = y_a = self.split_from(y_hi[:, 0:2, :], y_lo[:, 0:2, :], u[:, 0:2, :], ya)
        gate_out([y_a])
        wait(PE, sp_ready)
        for h in range(NH):
            PE.matmul(wide(banks(0), h), self.const("suffix"), wide(sb, h), start=True, stop=False)
            PE.matmul(wide(banks(0), h)[:, P:S], self.const("ones"), tail(sb, h), start=False, stop=True)
            mm = PE.matmul(tail(banks(0), h), self.const("suffix"), tail(sb, h), start=True, stop=True)
        sums = pe(mm)

        wait(DVE, steps_ready, scores_d)
        prefix_ones = self.consts[:, CONSTS["prefix"][0]:CONSTS["prefix"][0] + S]
        for h in range(NH):
            dve(DVE.tensor_scalar(wide(tri, h), prefix_ones, step[:, h:h + 1], None, ALU.mult))
            tri_ready = dve(DVE.tensor_scalar(tail(tri, h), self.const("prefix"), step[:, 4 + h:5 + h], None, ALU.mult))
        zeroed = dve(DVE.memset(cp[:, :, 0:3], 0.0))

        wait(ACT_, negated)
        for t, part in ((0, tail), (1, wide)):
            for h in range(NH):
                e = act(ACT_.activation(part(zd, h), part(zd, h), ACT.Exp, bias=top[:, 4 * t + h:4 * t + h + 1],
                                        accum_out=total[:, 4 * t + h:4 * t + h + 1]))
        wait(DVE, sums)
        exponent = dve(DVE.tensor_tensor(zb[:, :], zb[:, :], banks(0), ALU.subtract))
        wait(ACT_, exponent)
        wb_ready = act(ACT_.activation(zb[:, :], zb[:, :], ACT.Exp))
        wait(DVE, e)
        inverse = dve(DVE.reciprocal(total, total))
        wait(DVE, inverse)
        for t, part in ((0, tail), (1, wide)):
            for h in range(NH):
                weights_d = dve(DVE.tensor_scalar(part(zd, h), part(zd, h), total[:, 4 * t + h:4 * t + h + 1], None, ALU.mult))
        gate_slab()
        copied = act(ACT_.activation(cp[:, :, 3:S + 3], u[:, 14:18, :], ACT.Copy))
        gate_slab()
        gate_out([y_a])
        wait(PE, weights_d)
        for h in range(NH):
            for source, target in ((tail(zd, h), wide(banks(3), h)[:, 0:P]), (wide(zd, h)[:, 0:P], wide(banks(3), h)[:, P:S]),
                                   (wide(zd, h)[:, P:S], tail(banks(3), h))):
                mm = PE.transpose(target, source, self.const("ident"))
        turned = pe(mm)
        out_b = self.weighted_values(0, zb, vb, [wb_ready, vb_ready])
        wait(ACT_, turned)
        pd_ready = act(ACT_.activation(pd[:, :], banks(3), ACT.Copy))

        wait(DVE, zeroed, copied)
        tap = lambda c, j: self.param("ssm_taps", 4 * c + j)
        for j in range(4):
            for c in range(4):
                if j == 0:
                    last = dve(DVE.tensor_scalar(u[:, 14 + c, :], cp[:, c, 0:S], tap(c, 0), self.param("ssm_bias", c), ALU.mult, ALU.add))
                else:
                    last = dve(DVE.scalar_tensor_tensor(u[:, 14 + c, :], cp[:, c, j:j + S], tap(c, j), u[:, 14 + c, :], ALU.mult, ALU.add))
            wait(DVE, last)
        gate_slab()
        gate_out([y_a])
        out_d = self.weighted_values(3, pd, vd, [pd_ready, vd_ready])
        wait(ACT_, last)
        act(ACT_.activation(u[:, 12:14, :], u[:, 12:14, :], ACT.Silu))
        xbc = act(ACT_.activation(u[:, 14:18, :], u[:, 14:18, :], ACT.Silu))
        two = lambda bank: ps[:, bank:bank + 2, 0:S]
        y_parts[1] = y_b = self.split_from(y_hi[:, 2:4, :], y_lo[:, 2:4, :], two(0), out_b)
        y_parts[3] = y_d = self.split_from(y_hi[:, 6:8, :], y_lo[:, 6:8, :], two(3), out_d)
        gate_out([out_b])

        wait(PE, tri_ready, y_b)
        for h in range(NH):
            PE.matmul(wide(banks(0), h), self.const("ones"), wide(tri, h), start=True, stop=False)
            mm = PE.matmul(wide(banks(0), h)[:, P:S], self.const("ones"), tail(tri, h), start=False, stop=True)
        running = pe(mm)
        wait(PE, xbc, y_d)
        for g in range(2):
            r = slice(g * HD, g * HD + HD)
            b, c = u[r, 16, :], u[r, 17, :]
            PE.matmul(ps[:, 3 + g, 0:S], b[:, 0:P], c, start=True, stop=True)
            mm = PE.matmul(ps[:, 3 + g, S:W3], b[:, P:S], c[:, P:S], start=True, stop=True)
        products = pe(mm)
        for t in range(TT):
            for c in range(2):
                mm = PE.transpose(ps[:, 5, t * S + c * P:t * S + (c + 1) * P], u[:, 14 + c, t * P:(t + 1) * P], self.const("ident"))
        turned = pe(mm)
        gate_slab()
        gate_out([out_b])
        wait(DVE, running, before_ready)
        for h in range(NH):
            dve(DVE.scalar_tensor_tensor(wide(dm, h), wide(banks(0), h), before[:, h:h + 1], ssm_wide, ALU.add, ALU.add))
            seg = dve(DVE.scalar_tensor_tensor(tail(dm, h), wide(banks(0), h)[:, P:S], before[:, 4 + h:5 + h], ssm_tail, ALU.add, ALU.add))
        wait(ACT_, seg)
        decay = act(ACT_.activation(dm[:, :], dm[:, :], ACT.Exp))
        wait(DVE, turned, out_b)
        for t in range(TT):
            for h in range(NH):
                xd_ready = dve(DVE.tensor_scalar(xd[:, t, h * HD:(h + 1) * HD], ps[:, 5, t * S + h * HD:t * S + (h + 1) * HD],
                                                 dt[:, 4 * t + h:4 * t + h + 1], None, ALU.mult))
        wait(DVE, decay, products)
        for g in range(2):
            group = lambda n: ps[:, 3 + g, n].unsqueeze(1).to_broadcast([P, 2, n.stop - n.start])
            dve(DVE.tensor_tensor(wide(dm, 2 * g, 2), wide(dm, 2 * g, 2), group(slice(0, S)), ALU.mult))
            mixed = dve(DVE.tensor_tensor(tail(dm, 2 * g, 2), tail(dm, 2 * g, 2), group(slice(S, W3)), ALU.mult))
        gate_slab()
        gate_out([out_b])
        out_c = self.weighted_values(0, dm, xd, [mixed, xd_ready])
        gate_slab()
        gate_out([out_d])
        wait(DVE, out_c)
        for c in range(2):
            skipped = dve(DVE.scalar_tensor_tensor(u[:, 14 + c, :], u[:, 14 + c, :], self.param("skip", c), ps[:, c, 0:S], ALU.mult, ALU.add))
        wait(DVE, skipped)
        gated = dve(DVE.tensor_tensor(u[:, 14:16, :], u[:, 14:16, :], u[:, 12:14, :], ALU.mult))
        wait(ACT_, gated)
        squares = act(ACT_.activation(u[:, 12:14, :], u[:, 14:16, :], ACT.Square))
        wait(PE, squares)
        for c in range(2):
            mm = PE.matmul(ps[:, 0, c * S:(c + 1) * S], self.const("ones"), u[:, 12 + c, :], start=True, stop=True)
        summed = pe(mm)
        branch_done = [branch_slab(0, [mixed, xd_ready])]
        gate_slab()
        gate_out([out_d])
        factor = u[:, 16:18, :]
        wait(ACT_, summed)
        m = root = act(ACT_.activation(factor, pair(ps[:, 0, :]), ACT.Sqrt, scale=1.0 / P, bias=self.eps[:, :]))
        wait(DVE, m)
        m = dve(DVE.reciprocal(factor, factor))
        wait(DVE, m)
        for c in range(2):
            normed = dve(DVE.scalar_tensor_tensor(u[:, 14 + c, :], u[:, 14 + c, :], self.param("ssm_norm", c), u[:, 16 + c, :], ALU.mult, ALU.mult))
        y_parts[2] = y_c = self.split_from(y_hi[:, 4:6, :], y_lo[:, 4:6, :], u[:, 14:16, :], normed)

        for _ in range(2):
            gate_slab()
            gate_out([out_d])

        held = len(gates)
        merged = self.place("merged", [P, KD, S], at=self.ra + 6144)
        m_hi = self.place("m_hi", [P, KD, S], F32R, at=self.ra + 24576)
        m_lo = self.place("m_lo", [P, KD, S], F32R, at=self.ra + 24576 + 8192)
        ready = []

        def add_term(n, branch_done):
            q = n % 4
            if n < held:
                wait(ACT_, gates[n])
                gates[n] = act(ACT_.activation(slots[n], slots[n], ACT.Sigmoid))
            chunk = merged[:, 2 * q:2 * q + 2, :]
            wait(DVE, gates[n], branch_done, *(used[-1:] or [y_c]))
            if n < 4:
                used.append(dve(DVE.tensor_tensor(chunk, slots[n], pair(ps[:, term_bank(n), :]), ALU.mult)))
                return
            term = dve(DVE.tensor_tensor(slots[n], slots[n], pair(ps[:, term_bank(n), :]), ALU.mult))
            wait(DVE, term)
            used.append(dve(DVE.tensor_tensor(chunk, chunk, slots[n], ALU.add)))

        def split_merged(q):
            c = slice(2 * q, 2 * q + 2)
            ready.append(self.split_from(m_hi[:, c, :], m_lo[:, c, :], merged[:, c, :], used[-1]))

        self.ready_table(ACT.Sigmoid)
        for place in range(4):
            if place:
                branch_done.append(branch_slab(place, [root, skipped]))
            for q in range(4):
                if place and q >= (3 if place == 1 else 2):
                    gate_slab()
                    gate_out([out_b, out_d], raw=False)
                add_term(4 * place + q, branch_done[place])
                if place == 3:
                    split_merged(q)
        self.y_banks_free = used[12:14]
        return m_hi, m_lo, ready

    def feed_forward(self, tag, gate, up, down, ht_ready, banks_free):
        ps, PE, ACT_, DVE, act, dve = self.ps, self.PE, self.ACT, self.DVE, self.act, self.dve_turns
        chunks = FF // P
        a_hi = self.place(f"ff_hi{tag}", [P, chunks, S], F32R, at=self.ra)
        a_lo = self.place(f"ff_lo{tag}", [P, chunks, S], F32R, at=self.ra + chunks * S * 4)
        silu = self.place(f"ff_silu{tag}", [P, 3, 2 * S], at=self.rb)
        whole = self.place(f"ff_act{tag}", [P, 3, 2 * S], at=self.rb + 6144)
        wait(PE, *banks_free)
        def step(turn, j, ht_ready=()):
            b = j % 3
            pair = turn * 3 + j
            earlier = dve.ahead(-5)
            wait(PE, earlier)
            self.slab_step(gate(pair), self.feature_major(2 * b, ht_ready))
            wait(ACT_, self.slab_used.ahead(0), earlier)
            s = act(ACT_.activation(silu[:, b, :], ps[:, 2 * b, :], ACT.Silu))
            self.slab_step(up(pair), self.feature_major(2 * b + 1))
            wait(DVE, self.slab_used.ahead(0), s, act.ahead(-5), dve.ahead(0))
            m = dve(DVE.tensor_tensor(whole[:, b, :], silu[:, b, :], ps[:, 2 * b + 1, :], ALU.mult))
            chunk = bass.ds(pair * 2, 2)
            flat = whole[:, b, :].rearrange("p (c s) -> p c s", c=2)
            self.split_from(a_hi[:, chunk, :], a_lo[:, chunk, :], flat, m, done=dve)
        def body(turn):
            for j in range(3):
                step(turn, j, ht_ready if j == 0 else ())
        pairs = chunks // 2
        self.loop(pairs // 3, {act: 6, dve: 6}, body, slabs=NRAW)
        for j in range(pairs % 3):
            step(pairs // 3, j)
        a_ready = [dve.ahead(-2 * (pairs - 1 - j)) for j in range(pairs)]
        return self.into_residual(down, lambda c: a_hi[:, bass.ds(c, 1), :].rearrange("p a s -> p (a s)"),
                                  lambda c: a_lo[:, bass.ds(c, 1), :].rearrange("p a s -> p (a s)"), chunks,
                                  4, [a_ready[pairs // 3 * 3 - 1]], a_ready)

    def norm_in_place(self, gain, x_ready, more=False):
        wait(self.DVE, self.norm_factor(x_ready))
        ready = []
        for c in range(KD):
            ready.append(self.dve(self.DVE.scalar_tensor_tensor(
                self.xt[:, c, :], self.xt[:, c, :], self.param(gain, c), self.rstd, ALU.mult, ALU.mult)))
            if c % 2 and more:
                self.square(c // 2, ready[c])
                if c >= 5:
                    self.add_square(c // 2 - 1)
        if more:
            self.add_square(3)
        return ready

    def retention(self, w_in, w_out, ht_ready, banks_free, stage_ready, rates_ready):
        ps, PE, ACT_, DVE, pe, act, dve = self.ps, self.PE, self.ACT, self.DVE, self.pe, self.act, self.dve
        small = self.small
        q_t = self.place("ret_q", [P, KD, S], at=self.ra)
        k_t = self.place("ret_k", [P, KD, S], at=self.ra + 8192)
        v = self.place("ret_v", [P, TT, 2 * D], at=self.ra + 16384)
        g_t = self.place("ret_g", [P, 2 * KD, S], at=self.ra + 32768)
        cos_part = self.place("ret_cos", [P, 2, S], at=self.rd)
        sin_part = self.place("ret_sin", [P, 2, S], at=self.rd + 2048)
        table = lambda i: self.stage[:, i * S:(i + 1) * S].unsqueeze(1).to_broadcast([P, 2, S])
        wait(PE, *banks_free)
        wait(DVE, stage_ready)

        turns = self.dve_turns

        def head(turn):
            for b, out in ((0, q_t), (1, k_t)):
                wait(PE, turns.ahead(2 - 8))
                self.slab_step(self.columns(w_in, turn * BW + b * D), self.feature_major(b, ht_ready if b == 0 else ()))
                pair = ps[:, b, :].rearrange("p (c s) -> p c s", c=2)
                wait(DVE, self.slab_used.ahead(0), turns.ahead(0))
                turns(DVE.tensor_tensor(cos_part[:, :, :], pair, table(0), ALU.mult))
                parts = turns(DVE.tensor_tensor(sin_part[:, :, :], pair, table(1), ALU.mult))
                wait(DVE, parts)
                first, second = out[:, bass.ds(turn * 2, 1), :], out[:, bass.ds(turn * 2 + 1, 1), :]
                turns(DVE.tensor_tensor(first, cos_part[:, 0:1, :], sin_part[:, 1:2, :], ALU.subtract))
                turns(DVE.tensor_tensor(second, sin_part[:, 0:1, :], cos_part[:, 1:2, :], ALU.add))
            for c in range(2):
                wait(PE, act.ahead(1 - 4))
                def products(hi, lo, bank=2 + c):
                    for t in range(TT):
                        tok = slice(t * P, (t + 1) * P)
                        for k in range(KD):
                            out = ps[:, bank, t * S:(t + 1) * S]
                            PE.matmul(out, self.ht_hi[:, k, tok], hi[:, k, :], start=k == 0, stop=False)
                            PE.matmul(out, self.ht_hi[:, k, tok], lo[:, k, :], start=False, stop=False)
                            mm = PE.matmul(out, self.ht_lo[:, k, tok], hi[:, k, :], start=False, stop=k == KD - 1)
                    return mm
                self.slab_step(self.columns(w_in, turn * (2 * BW) + 2 * D + c * BW), products)
                wait(ACT_, self.slab_used.ahead(0))
                act(ACT_.activation(v[:, :, bass.ds(turn * (2 * BW) + c * BW, BW)],
                                    ps[:, 2 + c, :].rearrange("p (t f) -> p t f", t=TT), ACT.Copy))
            for c in range(2):
                wait(PE, act.ahead(1 - 4))
                self.slab_step(self.columns(w_in, turn * (2 * BW) + 4 * D + c * BW), self.feature_major(4 + c))
                wait(ACT_, self.slab_used.ahead(0))
                act(ACT_.activation(g_t[:, bass.ds(turn * 4 + 2 * c, 2), :],
                                    ps[:, 4 + c, :].rearrange("p (c s) -> p c s", c=2), ACT.Silu))
        self.loop(NH, {act: 4, turns: 8}, head, slabs=NRAW)
        loop_act, loop_dve = act.ahead(0), turns.ahead(0)

        decay = self.place("ret_decay", [P, NH, 2, S], at=self.rc)
        rate, decay_ready = small[:, 64:72], []
        distances = lambda i: self.stage[:, 2 * i * S:2 * (i + 1) * S].rearrange("p (m s) -> p m s", m=TT)
        wait(DVE, rates_ready, *ht_ready)
        for h in range(NH):
            a = dve(DVE.tensor_scalar(decay[:, h, :, :], distances(1), rate[:, h:h + 1], None, ALU.mult))
            wait(DVE, a)
            a = dve(DVE.scalar_tensor_tensor(decay[:, h, :, :], distances(2), rate[:, 4 + h:5 + h], decay[:, h, :, :], ALU.mult, ALU.add))
            wait(ACT_, a)
            decay_ready.append(act(ACT_.activation(decay[:, h, :, :], decay[:, h, :, :], ACT.Exp)))

        wait(PE, loop_dve, loop_act)
        weights = []
        for h in range(NH):
            for m in range(TT):
                for c in range(2):
                    mm = PE.matmul(ps[:, h, m * S:(m + 1) * S], k_t[:, 2 * h + c, m * P:(m + 1) * P], q_t[:, 2 * h + c, :],
                                   start=c == 0, stop=c == 1)
            scored = pe(mm)
            wait(DVE, scored, decay_ready[h])
            pair = ps[:, h, :].rearrange("p (m s) -> p m s", m=2)
            weights.append(dve(DVE.scalar_tensor_tensor(decay[:, h, :, :], pair, 1.0 / 16, decay[:, h, :, :], ALU.mult, ALU.mult)))
        y_hi = self.place("ret_y_hi", [P, 2 * KD, S], F32R, at=self.ra)
        y_lo = self.place("ret_y_lo", [P, 2 * KD, S], F32R, at=self.rb)
        yn = self.place("ret_normed", [P, TT, 2 * BW], at=self.rd)
        stats, moments = small[:, 80:92], small[:, 92:96]
        summed, normed, turned, ready = [], [], [], []

        def values(h):
            wait(PE, weights[h])
            for t in range(TT):
                bank = 4 + t
                wait(PE, *normed[h - 1][t:t + 1] if h else ())
                for m in range(TT):
                    mm = PE.matmul(ps[:, bank, :], decay[:, h, m, t * P:(t + 1) * P],
                                   v[:, m, h * 2 * BW:(h + 1) * 2 * BW], start=m == 0, stop=m == TT - 1)
                summed.append(pe(mm))

        def norm_values(h):
            normed.append([])
            for t in range(TT):
                bank = 4 + t
                wait(DVE, summed[2 * h + t], loop_dve)
                a = dve(DVE.bn_stats(stats[:, 6 * t:6 * t + 6], ps[:, bank, :]))
                wait(DVE, a)
                a = dve(DVE.bn_aggr(moments[:, 2 * t:2 * t + 2], stats[:, 6 * t:6 * t + 6]))
                wait(ACT_, a)
                a = act(ACT_.activation(stats[:, 6 * t:6 * t + 1], moments[:, 2 * t + 1:2 * t + 2], ACT.Sqrt, bias=self.eps[:, :]))
                wait(DVE, a)
                a = dve(DVE.reciprocal(stats[:, 6 * t:6 * t + 1], stats[:, 6 * t:6 * t + 1]))
                wait(DVE, a, *turned[-1:])
                normed[h].append(dve(DVE.tensor_scalar(yn[:, t, :], ps[:, bank, :], moments[:, 2 * t:2 * t + 1],
                                                       stats[:, 6 * t:6 * t + 1], ALU.subtract, ALU.mult)))

        def turn_values(h):
            wait(PE, *normed[h], *ready[-1:])
            for c in range(4):
                for t in range(TT):
                    mm = PE.transpose(ps[:, 6 + c // 2, c % 2 * S + t * P:c % 2 * S + (t + 1) * P],
                                      yn[:, t, c * P:(c + 1) * P], self.const("ident"))
            turned.append(pe(mm))
            wait(DVE, turned[-1])
            for c in range(4):
                z = dve(DVE.scalar_tensor_tensor(g_t[:, 4 * h + c, :], ps[:, 6 + c // 2, c % 2 * S:(c % 2 + 1) * S],
                                                 self.param("gn_gain", 4 * h + c), g_t[:, 4 * h + c, :], ALU.mult, ALU.mult))
            c = slice(4 * h, 4 * h + 4)
            ready.append(self.split_from(y_hi[:, c, :], y_lo[:, c, :], g_t[:, c, :], z))
        one = lambda a: (lambda c: a[:, bass.ds(c, 1), :].rearrange("p a s -> p (a s)"))
        values(0)
        norm_values(0)
        self.residual_open(0, weights)
        turn_values(0)
        for h in range(NH):
            if h + 1 < NH:
                values(h + 1)
                norm_values(h + 1)
            for i in range(2):
                self.residual_step(w_out, one(y_hi), one(y_lo), 4 * h + 2 * i, [ready[h]], h == NH - 1 and i == 1)
                if i == 0 and h + 1 < NH:
                    turn_values(h + 1)
        return self.residual_close()

    def fourier(self, w_out, h32_ready, banks_free, stage_ready):
        ps, PE, ACT_, DVE, pe, act, dve = self.ps, self.PE, self.ACT, self.DVE, self.pe, self.act, self.dve
        mixed = self.place("fft_features", [P, KD, 2 * S], at=self.ra)
        y_hi = self.place("fft_hi", [P, KD, S], F32R, at=self.rb)
        y_lo = self.place("fft_lo", [P, KD, S], F32R, at=self.rb + KD * S * 4)
        cos_sin = self.stage[:, 0:4 * S].rearrange("p (c n) -> p c n", c=2)
        minus_sin = self.stage[:, 4 * S:6 * S].rearrange("p (c n) -> p c n", c=2)
        wait(PE, *banks_free, stage_ready)
        copied = []
        for g in range(4):
            for t in range(TT):
                b = 2 * g + t
                for c in range(2):
                    wait(PE, h32_ready[2 * g + c])
                    mm = PE.matmul(ps[:, b, :], self.h32[:, 2 * g + c, t * P:(t + 1) * P], cos_sin[:, c, :],
                                   start=c == 0, stop=c == 1)
                done = pe(mm)
                engine, count = (ACT_, act) if b % 2 else (DVE, dve)
                wait(engine, done)
                copied.append(count(engine.activation(mixed[:, b, :], ps[:, b, :], ACT.Copy) if b % 2
                                    else engine.tensor_copy(mixed[:, b, :], ps[:, b, :])))
        ready = []
        for g in range(4):
            wait(PE, copied[2 * g], copied[2 * g + 1])
            for c in range(2):
                for t in range(TT):
                    out = ps[:, g, c * S:(c + 1) * S]
                    PE.matmul(out, mixed[:, 2 * g + t, c * P:(c + 1) * P], cos_sin[:, t, 0:S], start=t == 0, stop=False)
                    mm = PE.matmul(out, mixed[:, 2 * g + t, S + c * P:S + (c + 1) * P], minus_sin[:, t, :],
                                   start=False, stop=t == TT - 1)
            done = pe(mm)
            ready.append(self.split_from(y_hi[:, 2 * g:2 * g + 2, :], y_lo[:, 2 * g:2 * g + 2, :],
                                         ps[:, g, :].rearrange("p (c s) -> p c s", c=2), done))
        one = lambda a: (lambda c: a[:, bass.ds(c, 1), :].rearrange("p a s -> p (a s)"))
        return self.into_residual(w_out, one(y_hi), one(y_lo), KD, 4, copied, ready)

    def route(self, h32_ready):
        ps, PE, ACT_, DVE, pe, act, dve = self.ps, self.PE, self.ACT, self.DVE, self.pe, self.act, self.dve
        self.rows_hi = rows_hi = self.place("rows_hi", [P, TT, D], F32R, at=self.rb)
        self.rows_lo = rows_lo = self.place("rows_lo", [P, TT, D], F32R, at=self.rb + TT * D * 4)
        names = ["logit", "score", "first", "rest", "second", "gate", "chosen"]
        at = self.ra + 32768
        tiles = {}
        for n in names:
            tiles[n] = self.place("route_" + n, [P, TT, NE], at=at)
            at += TT * NE * 4
        self.gates = self.place("gates_of", [P, TT, NE + 1], at=at)
        self.places = self.place("place_of", [P, TT, NE + 1], at=at + 96)
        self.total = self.place("chosen_total", [P, NE + 1], at=at + 192)
        self.most = self.place("most_chosen", [P, 1], I32, at=at + 256)
        col = self.place("route_columns", [P, 16], at=at + 288)
        logit, score, first, rest, second, gate, chosen = (tiles[n] for n in names)
        order = self.const("order")

        for t in range(TT):
            for k in range(KD):
                wait(PE, h32_ready[k])
                mm = PE.matmul(ps[:, 6, t * NE:(t + 1) * NE], self.h32[:, k, t * P:(t + 1) * P],
                               self.param("router", k * NE, NE), start=k == 0, stop=k == KD - 1)
        routed = pe(mm)
        turned = []
        for t in range(TT):
            for half in range(2):
                b = 2 * t + half
                for c in range(4):
                    mm = PE.transpose(ps[:, b, c * P:(c + 1) * P], self.h32[:, 4 * half + c, t * P:(t + 1) * P], self.const("ident"))
                turned.append(pe(mm))
        wait(DVE, routed)
        last = dve(DVE.tensor_copy(logit[:, :, :], ps[:, 6, 0:TT * NE].rearrange("p (t e) -> p t e", t=TT)))

        def pick(values, out, top, mark):
            nonlocal last
            along = lambda a: a.unsqueeze(2).to_broadcast([P, TT, NE])
            for step in (lambda: DVE.tensor_reduce(top, values[:, :, :], AX.X, ALU.max),
                         lambda: DVE.tensor_tensor(score[:, :, :], values[:, :, :], along(top), ALU.is_equal),
                         lambda: DVE.tensor_tensor(score[:, :, :], score[:, :, :], order.unsqueeze(1).to_broadcast([P, TT, NE]), ALU.mult),
                         lambda: DVE.tensor_reduce(mark, score[:, :, :], AX.X, ALU.max),
                         lambda: DVE.tensor_tensor(out[:, :, :], score[:, :, :], along(mark), ALU.is_equal)):
                wait(DVE, last)
                last = dve(step())
        pick(logit, first, col[:, 0:2], col[:, 4:6])
        wait(DVE, last)
        last = dve(DVE.scalar_tensor_tensor(rest[:, :, :], first[:, :, :], NEG, logit[:, :, :], ALU.mult, ALU.add))
        pick(rest, second, col[:, 2:4], col[:, 4:6])
        wait(DVE, last)
        picked = dve(DVE.tensor_tensor(chosen[:, :, :], first[:, :, :], second[:, :, :], ALU.add))
        difference = dve(DVE.tensor_tensor(col[:, 6:8], col[:, 2:4], col[:, 0:2], ALU.subtract))
        wait(ACT_, difference)
        e = act(ACT_.activation(col[:, 8:10], col[:, 6:8], ACT.Exp))
        highs, rows = [], None
        part = lambda i: (i // 2, slice(i % 2 * 4 * P, (i % 2 + 1) * 4 * P))
        for i in range(4):
            t, c = part(i)
            wait(ACT_, turned[i])
            highs.append(act(ACT_.activation(rows_hi[:, t, c], ps[:, i, :], ACT.Copy)))
        def low_rows(i):
            t, c = part(i)
            wait(DVE, highs[i])
            return dve(DVE.tensor_tensor(rows_lo[:, t, c], ps[:, i, :], rows_hi[:, t, c].bitcast(F32), ALU.subtract))
        low_rows(0)
        low_rows(1)
        wait(PE, picked)
        PE.matmul(ps[:, 6, 0:NE], self.const("before"), chosen[:, 0, :], start=True, stop=True)
        PE.matmul(ps[:, 6, NE:2 * NE], self.const("ones"), chosen[:, 0, :], start=True, stop=False)
        PE.matmul(ps[:, 6, NE:2 * NE], self.const("before"), chosen[:, 1, :], start=False, stop=True)
        PE.matmul(ps[:, 6, 2 * NE:3 * NE], self.const("ones"), chosen[:, 0, :], start=True, stop=False)
        counted = pe(PE.matmul(ps[:, 6, 2 * NE:3 * NE], self.const("ones"), chosen[:, 1, :], start=False, stop=True))
        cleared = dve(DVE.memset(self.places[:, :, NE:NE + 1], -1.0))
        wait(DVE, counted)
        a = dve(DVE.scalar_tensor_tensor(self.places[:, :, 0:NE], ps[:, 6, 0:2 * NE].rearrange("p (t e) -> p t e", t=TT),
                                         1.0, chosen[:, :, :], ALU.add, ALU.mult))
        counted_most = dve(DVE.tensor_reduce(self.total[:, 0:1], ps[:, 6, 2 * NE:3 * NE], AX.X, ALU.max))
        low_rows(2)
        wait(DVE, a)
        placed = dve(DVE.tensor_scalar(self.places[:, :, 0:NE], self.places[:, :, 0:NE], -1.0, None, ALU.add))
        rows = low_rows(3)

        def gates_of():
            wait(DVE, counted_most, e)
            most = dve(DVE.tensor_copy(self.most[:, :], self.total[:, 0:1]))
            last = dve(DVE.tensor_scalar(col[:, 10:12], col[:, 8:10], 1.0, None, ALU.add))
            wait(DVE, last)
            last = dve(DVE.reciprocal(col[:, 12:14], col[:, 10:12]))
            wait(DVE, last)
            last = dve(DVE.tensor_tensor(col[:, 14:16], col[:, 8:10], col[:, 12:14], ALU.mult))
            wait(DVE, last)
            for t in range(TT):
                last = dve(DVE.tensor_scalar(gate[:, t, :], first[:, t, :], col[:, 12 + t:13 + t], None, ALU.mult))
            dve(DVE.memset(self.gates[:, :, NE:NE + 1], 0.0))
            wait(DVE, last)
            for t in range(TT):
                last = dve(DVE.scalar_tensor_tensor(self.gates[:, t, 0:NE], second[:, t, :], col[:, 14 + t:15 + t], gate[:, t, :], ALU.mult, ALU.add))
            return [last, most]
        return [placed, rows, cleared], gates_of

    def experts(self, w_gate, w_up, w_down, slot0, routed, tag, gates_of=None):
        ps, PE, ACT_, DVE, pe, act, dve = self.ps, self.PE, self.ACT, self.DVE, self.pe, self.act, self.dve
        at = self.ra
        def buf(name, shape, dtype=F32):
            nonlocal at
            t = self.place(name + tag, shape, dtype, at=at)
            at += -(-int(np.prod(shape[1:])) * 4 // 32) * 32
            return t
        xg_hi, xg_lo = buf("xg_hi", [P, KD, P], F32R), buf("xg_lo", [P, KD, P], F32R)
        pick = buf("pick", [P, TT, P], F32R)
        pick_t = buf("pick_t", [P, S], F32R)
        y_hi, y_lo = buf("y_hi_", [P, D], F32R), buf("y_lo_", [P, D], F32R)
        silu, whole = buf("silu_", [P, 4 * P]), buf("act_", [P, 4 * P])
        a_parts = [(buf(f"a_hi{i}_", [P, 4, P], F32R), buf(f"a_lo{i}_", [P, 4, P], F32R))
                   for i in range(2)]
        columns = buf("expert_columns", [P, 8])
        slot_gate = buf("slot_gate", [P, 1])
        gate_w = w_gate.rearrange("a e (k p) n -> p (a e k) n", p=P)
        up_w = w_up.rearrange("a e (k p) n -> p (a e k) n", p=P)
        down_w = w_down.rearrange("a e (k p) n -> p (a e k) n", p=P)
        slots = self.consts[:, CONSTS["slot"][0] + slot0:CONSTS["slot"][0] + slot0 + P]
        tiles = FE // (4 * P)
        HC = FE // P

        def build_pick(e, free):
            wait(DVE, *free, dve.ahead(0))
            a = dve(DVE.tensor_copy(columns[:, 0:TT], self.places[:, :, bass.ds(e, 1)].rearrange("p t e -> p (t e)")))
            wait(DVE, a)
            for t in range(TT):
                p = dve(DVE.tensor_scalar(pick[:, t, :], slots, columns[:, t:t + 1], None, ALU.is_equal))
            return p

        def gather(pick_ready, banks_free):
            wait(PE, pick_ready, *banks_free)
            for f in range(KD):
                out = ps[:, 6 + f // 4, f % 4 * P:(f % 4 + 1) * P]
                n = 0
                for t in range(TT):
                    for part in (self.rows_hi, self.rows_lo):
                        mm = PE.matmul(out, part[:, t, f * P:(f + 1) * P], pick[:, t, :], start=n == 0, stop=n == 3)
                        n += 1
            return pe(mm)

        def split_gathered(done):
            flat = lambda a: a[:, :, :].rearrange("p k s -> p (k s)")
            return self.split_from(flat(xg_hi), flat(xg_lo), ps[:, 6:8, :].rearrange("p b n -> p (b n)"), done,
                                   free=[self.slab_used.ahead(0)])

        def hidden(weight, e, f, half, bank):
            def products(hi, lo):
                for k in range(4):
                    kk = 4 * half + k
                    PE.matmul(ps[:, bank, :], xg_hi[:, kk, :], hi[:, k, :], start=kk == 0, stop=False)
                    PE.matmul(ps[:, bank, :], xg_hi[:, kk, :], lo[:, k, :], start=False, stop=False)
                    mm = PE.matmul(ps[:, bank, :], xg_lo[:, kk, :], hi[:, k, :], start=False, stop=kk == KD - 1)
                return mm
            return weight[:, bass.ds(e * KD + 4 * half, 4), bass.ds(f * (4 * P), 4 * P)], products

        def gate_tile(e, f):
            wait(PE, act.ahead(0))
            for half in range(2):
                self.slab_step(*hidden(gate_w, e, f, half, 0))

        def silu_tile():
            wait(ACT_, self.slab_used.ahead(0), dve.ahead(0))
            return act(ACT_.activation(silu[:, :], ps[:, 0, :], ACT.Silu))

        def up_tile(e, f):
            for half in range(2):
                self.slab_step(*hidden(up_w, e, f, half, 1))

        def act_tile(s):
            wait(DVE, self.slab_used.ahead(0), s, pe.ahead(0))
            return dve(DVE.tensor_tensor(whole[:, :], silu[:, :], ps[:, 1, :], ALU.mult))

        def turn_tile(whole_ready, bank_free):
            wait(PE, whole_ready, *bank_free)
            for c in range(4):
                mm = PE.transpose(ps[:, 2, c * P:(c + 1) * P], whole[:, c * P:(c + 1) * P], self.const("ident"))
            return pe(mm)

        def split_tile(turned, which=0):
            flat = lambda a: a[:, :, :].rearrange("p k s -> p (k s)")
            return self.split_from(flat(a_parts[which][0]), flat(a_parts[which][1]), ps[:, 2, :], turned)

        def down_tile(e, f, a_ready, which=0, halves=range(2)):
            a_hi, a_lo = a_parts[which]
            wait(PE, a_ready)
            for j in halves:
                def products(hi, lo):
                    for k in range(2):
                        for n in range(2):
                            out = ps[:, 4 + n, :]
                            w = slice(n * 512, (n + 1) * 512)
                            PE.matmul(out, a_hi[:, 2 * j + k, :], hi[:, k, w], start=False, stop=False, skip_group_check=True)
                            PE.matmul(out, a_hi[:, 2 * j + k, :], lo[:, k, w], start=False, stop=False, skip_group_check=True)
                            mm = PE.matmul(out, a_lo[:, 2 * j + k, :], hi[:, k, w], start=False, stop=False, skip_group_check=True)
                    return mm
                self.slab_step(down_w[:, bass.ds(e * HC + f * 4 + 2 * j, 2), :], products)

        def give_back(free, final=False):
            wait(PE, *free)
            banks = (2, 3, 6, 7)
            adds = []
            for f in range(KD):
                out = ps[:, banks[f // 2], f % 2 * S:(f % 2 + 1) * S]
                PE.matmul(out, y_hi[:, f * P:(f + 1) * P], pick_t[:, :], start=True, stop=False)
                mm = PE.matmul(out, y_lo[:, f * P:(f + 1) * P], pick_t[:, :], start=False, stop=True)
                if f % 2:
                    done = pe(mm)
                    wait(DVE, done)
                    c = slice(f - 1, f + 1)
                    adds.append(dve(DVE.tensor_tensor(self.xt[:, c, :], ps[:, banks[f // 2], :].rearrange("p (c s) -> p c s", c=2),
                                                      self.xt[:, c, :], ALU.add)))
                    if final:
                        self.square(f // 2, adds[-1])
                        if f >= 5:
                            self.add_square(f // 2 - 1)
            if final:
                self.add_square(3)
                adds.append(self.squares["sum"])
            return adds

        wait(DVE, *routed)
        dve(DVE.memset(y_hi[:, :].bitcast(F32), 0.0))
        dve(DVE.memset(y_lo[:, :].bitcast(F32), 0.0))
        y_ready = dve(DVE.memset(pick_t[:, :].bitcast(F32), 0.0))
        gathered = gather(build_pick(0, []), routed)
        if gates_of:
            wait(DVE, *gates_of())
        xg_ready = split_gathered(gathered)
        wait(PE, xg_ready, y_ready)

        def expert(e):
            last_split = [dve.ahead(0), act.ahead(0)]
            gate_tile(e, 0)
            s = silu_tile()
            adds = give_back(last_split)
            up_tile(e, 0)
            g = dve(DVE.tensor_copy(columns[:, 4:4 + TT], self.gates[:, :, bass.ds(e, 1)].rearrange("p t e -> p (t e)")))
            wait(PE, g, adds[1])
            for t in range(TT):
                PE.transpose(ps[:, 3, t * P:(t + 1) * P], pick[:, t, :].bitcast(F32), self.const("ident"))
            for t in range(TT):
                mm = PE.matmul(ps[:, 3, S:S + 1], pick[:, t, :].bitcast(F32), columns[:, 4 + t:5 + t], start=t == 0, stop=t == TT - 1)
            picked = pe(mm)
            wait(ACT_, picked)
            act(ACT_.activation(pick_t[:, :], ps[:, 3, 0:S], ACT.Copy))
            slot_ready = act(ACT_.activation(slot_gate[:, :], ps[:, 3, S:S + 1], ACT.Copy))
            act_tile(s)
            next_pick = build_pick(e + 1, [picked])
            wait(PE, adds[0])
            self.clear_banks((4, 5))

            def tile(turn):
                f = turn + 1
                gate_tile(e, f)
                s = silu_tile()
                turned = turn_tile(dve.ahead(0), [])
                a_ready = split_tile(turned)
                up_tile(e, f)
                act_tile(s)
                down_tile(e, f - 1, a_ready)
            self.loop(tiles - 2, {act: 2, dve: 2, pe: 1}, tile, slabs=NRAW)

            gate_tile(e, tiles - 1)
            s = silu_tile()
            a_ready = split_tile(turn_tile(dve.ahead(0), []))
            gathered = gather(next_pick, adds)
            up_tile(e, tiles - 1)
            whole_ready = act_tile(s)
            xg_ready = split_gathered(gathered)
            down_tile(e, tiles - 2, a_ready, halves=[0])
            last_ready = split_tile(turn_tile(whole_ready, [a_ready]), 1)
            down_tile(e, tiles - 2, a_ready, halves=[1])
            down_tile(e, tiles - 1, last_ready, 1)
            wait(ACT_, self.slab_used.ahead(0), slot_ready)
            both = ps[:, 4:6, :].rearrange("p b n -> p (b n)")
            high = act(ACT_.activation(y_hi[:, :], both, ACT.Copy, scale=slot_gate[:, :]))
            wait(DVE, high)
            y_ready = dve(DVE.scalar_tensor_tensor(y_lo[:, :], both, slot_gate[:, :], y_hi[:, :].bitcast(F32), ALU.mult, ALU.subtract))
            wait(PE, xg_ready)
        self.loop(NE, {act: 18, dve: 24, pe: 13}, expert, slabs=6 * tiles)
        last_split = [dve.ahead(0), act.ahead(0)]
        self.close_stream(gate_w)
        return give_back(last_split, final=True)


def build(nc, x, packed, lasting, staged, w_in, w_branch, w_o, w_gate_up, w_down, ret_w_in, ret_w_out,
          dense_gate, dense_up, dense_down, fnet_w, moe_gate, moe_up, moe_down, out):
    with ExitStack() as ctx:
        k = Kernel(nc, ctx)
        k.allocate()
        k.x_sems = [ctx.enter_context(nc.semaphore(f"x_landed{i}")) for i in range(2)]
        stored = ctx.enter_context(nc.semaphore("stored"))
        first_loads = []

        for queue, tile, source in ((k.SP, k.consts, lasting), (k.ACT, k.params, packed)):
            landed = Count(ctx.enter_context(nc.semaphore(f"landed_{tile.name}")), 16)
            queue.dma_start(tile[:, :], source).then_inc(landed.sem, 16)
            first_loads.append(landed)
        consts_ready, params_ready = first_loads
        zeroed = k.dve(k.DVE.memset(k.zero[:, :], 0.0))
        wait(k.PE, zeroed)
        wait(k.ACT, k.dve(k.DVE.memset(k.eps[:, :], EPS)))

        wait(k.PE, consts_ready)
        wait(k.DVE, consts_ready)
        x_ready = k.load_input(x)
        wait(k.POOL, Count(k.x_sems[1], 16))
        stage_ready = k.load(k.stage[:, :], staged[0, :, :])
        def start_stream():
            k.split(0)
            for engine in (k.ACT, k.DVE, k.PE):
                wait(engine, params_ready)
        ht = k.norm("norm1", x_ready, [], start_stream)
        k.split(1)
        k.split_ahead = LEAD
        logits_ready = k.time_step_logits(k.h32_ready)
        u_ready = k.project_inputs(w_in, ht)
        steps_ready, rates_ready = k.time_steps(logits_ready)
        m_hi, m_lo, merged = k.mixers_and_merge(w_in, w_branch, u_ready, steps_ready, stage_ready)
        wait(k.POOL, *merged)
        stage_ready = k.load(k.stage[:, :], staged[1, :, :])
        x_ready = k.into_residual(w_o, lambda c: m_hi[:, c, :], lambda c: m_lo[:, c, :], KD, 0, k.y_banks_free, merged)
        ht = k.norm("norm2", x_ready, [])
        x_ready = k.feed_forward(
            "1", lambda j: k.columns(w_gate_up, j * (2 * P)), lambda j: k.columns(w_gate_up, j * (2 * P) + FF),
            w_down, ht, x_ready)
        x_ready = k.norm_in_place("final1", x_ready, more=True)

        ht = k.norm("mix0", x_ready, [])
        x_ready = k.retention(ret_w_in, ret_w_out, ht, x_ready, stage_ready, rates_ready)
        wait(k.POOL, *x_ready)
        stage_ready = k.load(k.stage[:, :], staged[2, :, :])
        ht = k.norm("ffn0", x_ready, [])
        x_ready = k.feed_forward(
            "2", lambda j: k.columns(dense_gate, j * (2 * P)), lambda j: k.columns(dense_up, j * (2 * P)),
            dense_down, ht, x_ready)

        h32_ready = k.norm("mix1", x_ready, [], whole_only=True)
        x_ready = k.fourier(fnet_w, h32_ready, x_ready, stage_ready)
        routed, gates_of = k.route(k.norm("ffn1", x_ready, [], whole_only=True))
        x_ready = k.experts(moe_gate, moe_up, moe_down, 0, routed, "", gates_of)
        for engine in (k.SP, k.POOL, k.ACT, k.DVE, k.PE):
            wait(engine, *x_ready)
        most = nc.values_load(k.most[0:1, 0:1], min_val=0, max_val=S)
        with nc.If(most > P):
            k.open_stream()
            extra = k.experts(moe_gate, moe_up, moe_down, P, routed, "_more")
            for engine in (k.SP, k.POOL, k.ACT, k.DVE, k.PE):
                wait(engine, *extra)
        k.fresh_counters("_final")
        k.squares = {"sum": k.dve.ahead(0)}
        finish(k, [], "final2", out, stored)


def finish(k, x_ready, gain, out, stored):
    if gain:
        x_ready = k.norm_in_place(gain, x_ready)
    rows = k.place("out_rows", [P, TT, D], at=k.ra)
    wait(k.PE, *x_ready)
    wait(k.ACT, *x_ready)
    for t in range(TT):
        copied = []
        for half in range(2):
            b = 2 * t + half
            for c in range(4):
                mm = k.PE.transpose(k.ps[:, b, c * P:(c + 1) * P], k.xt[:, 4 * half + c, t * P:(t + 1) * P], k.const("ident"))
            turned = k.pe(mm)
            wait(k.ACT, turned)
            copied.append(k.act(k.ACT.activation(rows[:, t, 4 * P * half:4 * P * (half + 1)], k.ps[:, b, :], ACT.Copy)))
        wait(k.SP, *copied)
        k.SP.dma_start(out[0, t * P:(t + 1) * P, :], rows[:, t, :]).then_inc(stored, 16)
    k.SP.wait_ge(stored, 16 * TT)


_WEIGHTS = ["w_in", "w_branch", "w_o", "w_gate_up", "w_down", "ret_w_in_2", "ret_w_out_2", "dense_w_gate_2",
            "dense_w_up_2", "dense_w_down_2", "fnet_w_out_2", "moe_w_gate_2", "moe_w_up_2", "moe_w_down_2"]


def pack_parameters(v):
    def chunks(a):
        return np.ascontiguousarray(a).reshape(-1, P).T

    def everywhere(a):
        return np.broadcast_to(np.ascontiguousarray(a).reshape(1, -1), (P, a.size))

    def per_head(a):
        return np.repeat(a, HD).reshape(2, P).T

    taps = lambda w: w.reshape(w.shape[-2], -1, P).transpose(2, 1, 0).reshape(P, -1)
    rows = lambda w: w.reshape(KD, P, -1).transpose(1, 0, 2).reshape(P, -1)
    twice = lambda a: np.concatenate([a.reshape(-1), a.reshape(-1)])
    parts = dict(
        norm1=chunks(v["norm1_g"]), norm2=chunks(v["norm2_g"]), mix0=chunks(v["mix_norm_2"][0]),
        mix1=chunks(v["mix_norm_2"][1]), ffn0=chunks(v["ffn_norm_2"][0]), ffn1=chunks(v["ffn_norm_2"][1]),
        final1=chunks(v["final_g"]), final2=chunks(v["final_norm_2"]),
        ssm_taps=taps(v["ssm_conv_w"]), a_taps=taps(v["conv_a_w"]), ssm_bias=chunks(v["ssm_conv_b"]),
        dt_bias=everywhere(twice(v["ssm_dt_bias"])), a_log=everywhere(twice(v["ssm_a_log"])),
        skip=per_head(v["ssm_d"].reshape(-1)), ssm_norm=chunks(v["ssm_norm_g"]), gn_gain=chunks(v["ret_gn_gain_2"]),
        decay=everywhere(v["ret_decay_logit_2"]), w_dt=rows(v["w_in"][0, :, COL_DT:COL_DT + NH]),
        router=rows(v["moe_router_2"][0]))
    return np.ascontiguousarray(np.concatenate([parts[name] for name in PARAMS], 1))


def kernel(**inputs):
    import concourse.bacc as _bacc
    from concourse.bass_utils import run_bass_kernel_spmd as _run

    v = {name: np.asarray(a) for name, a in inputs.items()}
    nc = _bacc.Bacc("TRN2", target_bir_lowering=False, num_devices=1)
    lasting, staged = host_constants()
    arrays = {"x": v["x"], "params": pack_parameters(v), "lasting": lasting, "staged": staged}
    arrays.update({name: v[name] for name in _WEIGHTS})
    arrays = {f"in_{name}": np.ascontiguousarray(a) for name, a in arrays.items()}
    args = []
    for name, a in arrays.items():
        t = nc.dram_tensor(name, a.shape, mybir.dt.from_np(a.dtype), kind="ExternalInput").ap()
        short = name[3:]
        if short in ("w_in", "w_o", "w_gate_up", "w_down", "ret_w_in_2", "ret_w_out_2", "dense_w_gate_2",
                     "dense_w_up_2", "dense_w_down_2", "fnet_w_out_2"):
            t = t.rearrange("a k n -> (a k) n")
        args.append(t)
    args.append(nc.dram_tensor("out", (1, S, D), F32, kind="ExternalOutput").ap())
    build(nc, *args)
    r = _run(nc, [arrays], core_ids=[0])
    return r.results[0]["out"]
```
